# Optimizing a Trainium2 kernel written in Bass

```python
import math
import jax, jax.numpy as jnp
from jax import lax
import numpy as np

D_MODEL = 1024
BATCH = 1
SEQ = 512
DEPTH = 1

MEM_LEN = 256
MIX_WIDTH = D_MODEL
GDN_HEADS = 4
GDN_HEAD_DIM = 128
GDN_WIDTH = GDN_HEADS * GDN_HEAD_DIM
CFM_WIDTH = MIX_WIDTH - GDN_WIDTH
GDN_SHORT_CONV = 4
CHUNK = 64
CFM_KERNEL = 31
XATTN_HEADS = 4
XATTN_HEAD_DIM = D_MODEL // XATTN_HEADS
D_FF = 2816
FFN_CONV = 3
EPS = 1e-6
IN_COLS = 4 * GDN_WIDTH + 2 * GDN_HEADS + 2 * CFM_WIDTH


def rmsnorm(x, g):
    xf = x.astype(jnp.float32)
    y = xf * lax.rsqrt(jnp.mean(xf * xf, axis=-1, keepdims=True) + EPS)
    return (y * g.astype(jnp.float32)).astype(x.dtype)

def layernorm(x, g, b):
    xf = x.astype(jnp.float32)
    mu = jnp.mean(xf, axis=-1, keepdims=True)
    xc = xf - mu
    var = jnp.mean(xc * xc, axis=-1, keepdims=True)
    return (xc * lax.rsqrt(var + EPS) * g.astype(jnp.float32) + b.astype(jnp.float32)).astype(x.dtype)

def l2norm(x):
    return x * lax.rsqrt(jnp.sum(x * x, axis=-1, keepdims=True) + EPS)

def causal_dwconv(x, w):
    K, C = w.shape
    return lax.conv_general_dilated(
        x, w[:, None, :].astype(x.dtype), window_strides=(1,), padding=[(K - 1, 0)],
        dimension_numbers=("NWC", "WIO", "NWC"), feature_group_count=C)

def gated_delta_rule_chunked(q, k, v, g, beta):
    B, T, H, Dk = q.shape
    Dv = v.shape[-1]
    N = T // CHUNK

    def to_chunks(a):
        a = a.reshape((B, N, CHUNK, H) + a.shape[3:])
        return jnp.moveaxis(a, (1, 3), (0, 2))

    qc = to_chunks(q * (Dk ** -0.5))
    kc = to_chunks(k)
    vc = to_chunks(v)
    bc = to_chunks(beta)
    gc = jnp.cumsum(to_chunks(g), axis=-1)

    idx = jnp.arange(CHUNK)
    causal = idx[:, None] >= idx[None, :]
    strict = idx[:, None] > idx[None, :]
    diff = gc[..., :, None] - gc[..., None, :]
    decay = jnp.where(causal, jnp.exp(jnp.where(causal, diff, 0.0)), 0.0)

    kb = kc * bc[..., None]
    L = jnp.where(strict, jnp.einsum('nbhid,nbhjd->nbhij', kb, kc) * decay, 0.0)
    eye = jnp.eye(CHUNK, dtype=jnp.float32)
    rhs = jnp.concatenate([vc * bc[..., None], kb * jnp.exp(gc)[..., None]], axis=-1)
    sol = lax.linalg.triangular_solve(eye + L, rhs, left_side=True, lower=True, unit_diagonal=True)
    u = sol[..., :Dv]
    w = sol[..., Dv:]
    attn_intra = jnp.einsum('nbhid,nbhjd->nbhij', qc, kc) * decay

    def step(S, inp):
        q_i, k_i, u_i, w_i, g_i, a_i = inp
        v_new = u_i - jnp.einsum('bhcd,bhde->bhce', w_i, S)
        o = (jnp.einsum('bhcd,bhde->bhce', q_i * jnp.exp(g_i)[..., None], S)
             + jnp.einsum('bhij,bhje->bhie', a_i, v_new))
        g_last = g_i[..., -1]
        k_dec = k_i * jnp.exp(g_last[..., None] - g_i)[..., None]
        S = S * jnp.exp(g_last)[..., None, None] + jnp.einsum('bhcd,bhce->bhde', k_dec, v_new)
        return S, o

    S0 = jnp.zeros((B, H, Dk, Dv), jnp.float32)
    _, o = lax.scan(step, S0, (qc, kc, u, w, gc, attn_intra))
    return jnp.moveaxis(o, (0, 2), (1, 3)).reshape(B, T, H, Dv)

def hybrid_mixer(h, w_in, gdn_conv_w, a_log, dt_bias, gdn_norm_g,
                 cfm_dw_w, cfm_dw_b, cfm_ln_g, cfm_ln_b, w_out):
    B, T, _ = h.shape
    z = h @ w_in
    s1 = 3 * GDN_WIDTH
    s2 = 4 * GDN_WIDTH
    s3 = s2 + GDN_HEADS
    s4 = s3 + GDN_HEADS
    qkv, gate, a_logit, b_logit, cfm_in = jnp.split(z, [s1, s2, s3, s4], axis=-1)

    qkv = jax.nn.silu(causal_dwconv(qkv, gdn_conv_w)).astype(jnp.float32)
    q, k, v = jnp.split(qkv, 3, axis=-1)
    shp = (B, T, GDN_HEADS, GDN_HEAD_DIM)
    q = l2norm(q.reshape(shp))
    k = l2norm(k.reshape(shp))
    v = v.reshape(shp)
    g = -jnp.exp(a_log.astype(jnp.float32)) * jax.nn.softplus(
        a_logit.astype(jnp.float32) + dt_bias.astype(jnp.float32))
    beta = jax.nn.sigmoid(b_logit.astype(jnp.float32))
    o = gated_delta_rule_chunked(q, k, v, g, beta)
    o = rmsnorm(o, gdn_norm_g) * jax.nn.silu(gate.astype(jnp.float32).reshape(shp))
    o_gdn = o.reshape(B, T, GDN_WIDTH).astype(h.dtype)

    c = jax.nn.glu(cfm_in, axis=-1)
    c = causal_dwconv(c, cfm_dw_w) + cfm_dw_b
    c = jax.nn.silu(layernorm(c, cfm_ln_g, cfm_ln_b))

    return jnp.concatenate([o_gdn, c], axis=-1) @ w_out

def memory_cross_attention(h, mem_n, w_q, w_kv, w_o):
    B, T, _ = h.shape
    M = mem_n.shape[1]
    q = (h @ w_q).reshape(B, T, XATTN_HEADS, XATTN_HEAD_DIM)
    k, v = jnp.split(mem_n @ w_kv, 2, axis=-1)
    k = k.reshape(B, M, XATTN_HEADS, XATTN_HEAD_DIM)
    v = v.reshape(B, M, XATTN_HEADS, XATTN_HEAD_DIM)
    s = jnp.einsum('bthd,bmhd->bhtm', q, k).astype(jnp.float32) * (XATTN_HEAD_DIM ** -0.5)
    p = jax.nn.softmax(s, axis=-1).astype(h.dtype)
    o = jnp.einsum('bhtm,bmhd->bthd', p, v).reshape(B, T, D_MODEL)
    return o @ w_o

def conv_glu_ffn(h, w_up, conv_w, conv_b, w_down):
    u = causal_dwconv(h @ w_up, conv_w) + conv_b
    a, b = jnp.split(u, 2, axis=-1)
    return (jax.nn.silu(a) * b) @ w_down

def first_inputs(seed: int = 0) -> dict:
    key = jax.random.key(seed)
    ks = jax.random.split(key, 24)
    f32 = jnp.float32

    def nrm(k, shape, scale):
        return jax.random.normal(k, shape, f32) * scale

    x = nrm(ks[0], (BATCH, SEQ, D_MODEL), 1.0)
    mem = nrm(ks[1], (BATCH, MEM_LEN, D_MODEL), 1.0)
    norm_g = 1.0 + nrm(ks[2], (DEPTH, 6, D_MODEL), 0.05)
    w_in = nrm(ks[3], (DEPTH, D_MODEL, IN_COLS), D_MODEL ** -0.5)
    gdn_conv_w = nrm(ks[4], (DEPTH, GDN_SHORT_CONV, 3 * GDN_WIDTH), GDN_SHORT_CONV ** -0.5)
    gdn_a_log = jnp.log(jax.random.uniform(ks[5], (DEPTH, GDN_HEADS), f32, 1.0, 16.0))
    dt = jnp.exp(jax.random.uniform(ks[6], (DEPTH, GDN_HEADS), f32,
                                    math.log(1e-3), math.log(1e-1)))
    gdn_dt_bias = dt + jnp.log(-jnp.expm1(-dt))
    gdn_norm_g = 1.0 + nrm(ks[7], (DEPTH, GDN_HEAD_DIM), 0.05)
    cfm_dw_w = nrm(ks[8], (DEPTH, CFM_KERNEL, CFM_WIDTH), CFM_KERNEL ** -0.5)
    cfm_dw_b = nrm(ks[9], (DEPTH, CFM_WIDTH), 0.02)
    cfm_ln_g = 1.0 + nrm(ks[10], (DEPTH, CFM_WIDTH), 0.05)
    cfm_ln_b = nrm(ks[11], (DEPTH, CFM_WIDTH), 0.02)
    w_out = nrm(ks[12], (DEPTH, MIX_WIDTH, D_MODEL), MIX_WIDTH ** -0.5)
    mem_norm_g = 1.0 + nrm(ks[13], (DEPTH, D_MODEL), 0.05)
    xa_w_q = nrm(ks[14], (DEPTH, D_MODEL, D_MODEL), D_MODEL ** -0.5)
    xa_w_kv = nrm(ks[15], (DEPTH, D_MODEL, 2 * D_MODEL), D_MODEL ** -0.5)
    xa_w_o = nrm(ks[16], (DEPTH, D_MODEL, D_MODEL), D_MODEL ** -0.5)
    ffn_w_up = nrm(ks[17], (DEPTH, D_MODEL, 2 * D_FF), D_MODEL ** -0.5)
    ffn_conv_w = nrm(ks[18], (DEPTH, FFN_CONV, 2 * D_FF), FFN_CONV ** -0.5)
    ffn_conv_b = nrm(ks[19], (DEPTH, 2 * D_FF), 0.02)
    ffn_w_down = nrm(ks[20], (DEPTH, D_FF, D_MODEL), D_FF ** -0.5)
    return {"x": x, "mem": mem, "norm_g": norm_g, "w_in": w_in, "gdn_conv_w": gdn_conv_w,
            "gdn_a_log": gdn_a_log, "gdn_dt_bias": gdn_dt_bias, "gdn_norm_g": gdn_norm_g,
            "cfm_dw_w": cfm_dw_w, "cfm_dw_b": cfm_dw_b, "cfm_ln_g": cfm_ln_g, "cfm_ln_b": cfm_ln_b,
            "w_out": w_out, "mem_norm_g": mem_norm_g, "xa_w_q": xa_w_q, "xa_w_kv": xa_w_kv,
            "xa_w_o": xa_w_o, "ffn_w_up": ffn_w_up, "ffn_conv_w": ffn_conv_w,
            "ffn_conv_b": ffn_conv_b, "ffn_w_down": ffn_w_down}

def first_block(x, mem, norm_g, w_in, gdn_conv_w, gdn_a_log, gdn_dt_bias, gdn_norm_g,
              cfm_dw_w, cfm_dw_b, cfm_ln_g, cfm_ln_b, w_out, mem_norm_g,
              xa_w_q, xa_w_kv, xa_w_o, ffn_w_up, ffn_conv_w, ffn_conv_b, ffn_w_down):
    h = x
    for l in range(DEPTH):
        g = norm_g[l]
        y = hybrid_mixer(rmsnorm(h, g[0]), w_in[l], gdn_conv_w[l], gdn_a_log[l], gdn_dt_bias[l],
                         gdn_norm_g[l], cfm_dw_w[l], cfm_dw_b[l], cfm_ln_g[l], cfm_ln_b[l], w_out[l])
        h = h + rmsnorm(y, g[1])
        y = memory_cross_attention(rmsnorm(h, g[2]), rmsnorm(mem, mem_norm_g[l]),
                                   xa_w_q[l], xa_w_kv[l], xa_w_o[l])
        h = h + rmsnorm(y, g[3])
        y = conv_glu_ffn(rmsnorm(h, g[4]), ffn_w_up[l], ffn_conv_w[l], ffn_conv_b[l], ffn_w_down[l])
        h = h + rmsnorm(y, g[5])
    return h


DEPTH_2 = 2

N_A_LAYERS = DEPTH_2 // 2
N_B_LAYERS = DEPTH_2 - N_A_LAYERS

RET_HEADS = 4
RET_QK_DIM = 256
RET_V_DIM = 512
RET_WIDTH = RET_HEADS * RET_V_DIM
RET_QK_WIDTH = RET_HEADS * RET_QK_DIM
RET_CHUNK = 128
ROPE_BASE = 10000.0

SB_HEADS = 8
SB_QK_DIM = 128
SB_V_DIM = 256
SB_QK_WIDTH = SB_HEADS * SB_QK_DIM
SB_WIDTH = SB_HEADS * SB_V_DIM
SB_BLOCK = 128


def rms_norm(x, g):
    xf = x.astype(jnp.float32)
    y = xf * lax.rsqrt(jnp.mean(xf * xf, axis=-1, keepdims=True) + EPS)
    return (y * g.astype(jnp.float32)).astype(x.dtype)

def split_heads(t, n_heads):
    b, s, w = t.shape
    return t.reshape(b, s, n_heads, w // n_heads).transpose(0, 2, 1, 3)

def merge_heads(t):
    b, h, s, d = t.shape
    return t.transpose(0, 2, 1, 3).reshape(b, s, h * d)

def rope(x, pos):
    half = x.shape[-1] // 2
    inv_freq = 1.0 / (ROPE_BASE ** (jnp.arange(half, dtype=jnp.float32) / half))
    ang = pos[:, None] * inv_freq[None, :]
    cos, sin = jnp.cos(ang), jnp.sin(ang)
    x1, x2 = x[..., :half], x[..., half:]
    return jnp.concatenate([x1 * cos - x2 * sin, x1 * sin + x2 * cos], axis=-1)

def retention_chunkwise(q, k, v):
    b, h, t, dk = q.shape
    dv = v.shape[-1]
    c = RET_CHUNK
    nc = t // c
    log_gamma = jnp.log1p(-jnp.exp2(-5.0 - jnp.arange(h, dtype=jnp.float32)))
    idx = jnp.arange(c, dtype=jnp.float32)
    diff = idx[:, None] - idx[None, :]
    intra_decay = jnp.where(diff >= 0, jnp.exp(log_gamma[:, None, None] * diff), 0.0)
    q_decay = jnp.exp(log_gamma[:, None] * (idx[None, :] + 1.0))
    k_decay = jnp.exp(log_gamma[:, None] * (c - 1.0 - idx[None, :]))
    chunk_decay = jnp.exp(log_gamma * c)

    def to_chunks(a):
        return a.reshape(b, h, nc, c, a.shape[-1]).transpose(2, 0, 1, 3, 4)

    def step(state, inp):
        qc, kc, vc = inp
        scores = jnp.einsum('bhid,bhjd->bhij', qc, kc) * intra_decay
        o = jnp.einsum('bhij,bhje->bhie', scores, vc)
        o = o + jnp.einsum('bhid,bhde->bhie', qc * q_decay[None, :, :, None], state)
        state = state * chunk_decay[None, :, None, None] + jnp.einsum(
            'bhjd,bhje->bhde', kc * k_decay[None, :, :, None], vc)
        return state, o

    state0 = jnp.zeros((b, h, dk, dv), jnp.float32)
    _, out = lax.scan(step, state0, (to_chunks(q), to_chunks(k), to_chunks(v)))
    return out.transpose(1, 2, 0, 3, 4).reshape(b, h, t, dv)

def stick_breaking_attention(q, k, v):
    b, h, t, dk = q.shape
    nb = t // SB_BLOCK
    scale = 1.0 / math.sqrt(dk)
    key_idx = jnp.arange(t)
    q_blocks = q.reshape(b, h, nb, SB_BLOCK, dk).transpose(2, 0, 1, 3, 4)

    def block(args):
        qb, blk = args
        t_idx = blk * SB_BLOCK + jnp.arange(SB_BLOCK)
        z = jnp.einsum('bhqd,bhkd->bhqk', qb, k) * scale
        causal = key_idx[None, :] < t_idx[:, None]
        log_not = jnp.where(causal, jax.nn.log_sigmoid(-z), 0.0)
        suffix = lax.cumsum(log_not, axis=3, reverse=True) - log_not
        weights = jnp.where(causal, jnp.exp(jax.nn.log_sigmoid(z) + suffix), 0.0)
        return jnp.einsum('bhqk,bhke->bhqe', weights, v)

    out = lax.map(block, (q_blocks, jnp.arange(nb)))
    return out.transpose(1, 2, 0, 3, 4).reshape(b, h, t, v.shape[-1])

def second_inputs(seed: int = 0) -> dict:
    key = jax.random.key(seed)
    ks = jax.random.split(key, 12)
    d = D_MODEL
    ret_in_cols = 2 * RET_QK_WIDTH + 2 * RET_WIDTH
    sb_in_cols = SB_QK_WIDTH + SB_WIDTH
    kv_cols = SB_QK_WIDTH + SB_WIDTH

    def gain(k, shape):
        return 1.0 + 0.02 * jax.random.normal(k, shape, jnp.float32)

    def dense(k, shape, fan_in):
        return jax.random.normal(k, shape, jnp.float32) * (fan_in ** -0.5)

    return {
        "x": jax.random.normal(ks[0], (BATCH, SEQ, d), jnp.float32),
        "ret_norm_pre": gain(ks[1], (N_A_LAYERS, d)),
        "ret_w_in": dense(ks[2], (N_A_LAYERS, d, ret_in_cols), d),
        "ret_w_out": dense(ks[3], (N_A_LAYERS, RET_WIDTH, d), RET_WIDTH),
        "ret_norm_post": gain(ks[4], (N_A_LAYERS, d)),
        "kv_norm": gain(ks[5], (d,)),
        "w_kv": dense(ks[6], (d, kv_cols), d),
        "sb_norm_pre": gain(ks[7], (N_B_LAYERS, d)),
        "sb_w_in": dense(ks[8], (N_B_LAYERS, d, sb_in_cols), d),
        "sb_w_out": dense(ks[9], (N_B_LAYERS, SB_WIDTH, d), SB_WIDTH),
        "sb_norm_post": gain(ks[10], (N_B_LAYERS, d)),
    }

def second_block(x, ret_norm_pre, ret_w_in, ret_w_out, ret_norm_post, kv_norm, w_kv,
              sb_norm_pre, sb_w_in, sb_w_out, sb_norm_post):
    b, t, _ = x.shape
    pos = jnp.arange(t, dtype=jnp.float32)
    h = x
    k_shared = None
    v_shared = None
    for i in range(DEPTH_2):
        if i < N_A_LAYERS:
            u = rms_norm(h, ret_norm_pre[i])
            proj = u @ ret_w_in[i]
            q, k, v, g = jnp.split(
                proj, [RET_QK_WIDTH, 2 * RET_QK_WIDTH, 2 * RET_QK_WIDTH + RET_WIDTH], axis=-1)
            q = rope(split_heads(q, RET_HEADS).astype(jnp.float32), pos)
            k = rope(split_heads(k, RET_HEADS).astype(jnp.float32), pos) * (RET_QK_DIM ** -0.5)
            v = split_heads(v, RET_HEADS).astype(jnp.float32)
            o = retention_chunkwise(q, k, v)
            mu = jnp.mean(o, axis=-1, keepdims=True)
            var = jnp.mean(jnp.square(o - mu), axis=-1, keepdims=True)
            o = (o - mu) * lax.rsqrt(var + EPS)
            o = merge_heads(o).astype(h.dtype) * jax.nn.silu(g)
            y = o @ ret_w_out[i]
            h = h + rms_norm(y, ret_norm_post[i])
            if i == N_A_LAYERS - 1:
                kv = rms_norm(h, kv_norm) @ w_kv
                k_sh, v_sh = jnp.split(kv, [SB_QK_WIDTH], axis=-1)
                k_shared = split_heads(k_sh, SB_HEADS).astype(jnp.float32)
                v_shared = split_heads(v_sh, SB_HEADS).astype(jnp.float32)
        else:
            j = i - N_A_LAYERS
            u = rms_norm(h, sb_norm_pre[j])
            proj = u @ sb_w_in[j]
            q, g = jnp.split(proj, [SB_QK_WIDTH], axis=-1)
            q = split_heads(q, SB_HEADS).astype(jnp.float32)
            o = stick_breaking_attention(q, k_shared, v_shared)
            o = merge_heads(o).astype(h.dtype) * jax.nn.silu(g)
            y = o @ sb_w_out[j]
            h = h + rms_norm(y, sb_norm_post[j])
    return h


def setup_inputs(seed=0):
    out = dict(first_inputs(seed))
    for name, value in second_inputs(seed + 1).items():
        if name != "x":
            out[name + "_2"] = value
    return out


def reference(
    x, mem, norm_g, w_in, gdn_conv_w, gdn_a_log, gdn_dt_bias, gdn_norm_g, cfm_dw_w, cfm_dw_b,
    cfm_ln_g, cfm_ln_b, w_out, mem_norm_g, xa_w_q, xa_w_kv, xa_w_o, ffn_w_up, ffn_conv_w,
    ffn_conv_b, ffn_w_down, ret_norm_pre_2, ret_w_in_2, ret_w_out_2, ret_norm_post_2, kv_norm_2,
    w_kv_2, sb_norm_pre_2, sb_w_in_2, sb_w_out_2, sb_norm_post_2,
):
    x = first_block(
        x, mem, norm_g, w_in, gdn_conv_w, gdn_a_log, gdn_dt_bias, gdn_norm_g, cfm_dw_w,
        cfm_dw_b, cfm_ln_g, cfm_ln_b, w_out, mem_norm_g, xa_w_q, xa_w_kv, xa_w_o, ffn_w_up,
        ffn_conv_w, ffn_conv_b, ffn_w_down,
    )
    return second_block(
        x, ret_norm_pre_2, ret_w_in_2, ret_w_out_2, ret_norm_post_2, kv_norm_2, w_kv_2,
        sb_norm_pre_2, sb_w_in_2, sb_w_out_2, sb_norm_post_2,
    )


_drawn_inputs = setup_inputs


def setup_inputs(seed=0):
    import zlib

    import numpy as np

    out = dict(_drawn_inputs(seed))
    spreads = {}
    factors = {'cfm_ln_b': 3.114,
     'ffn_conv_b': 2.749,
     'ret_norm_post_2': 5.823,
     'kv_norm_2': 6.609,
     'sb_norm_pre_2': 6.175,
     'sb_norm_post_2': 6.991}
    for name, (base, spread) in spreads.items():
        noise = np.random.default_rng([zlib.crc32(name.encode()), seed]).standard_normal(out[name].shape)
        drawn = base * np.exp(spread * noise) if base else spread * noise
        out[name] = __import__('jax').numpy.asarray(drawn.astype(out[name].dtype))
    for name, factor in factors.items():
        out[name] = (out[name] * factor).astype(out[name].dtype)
    return out
```

```python
from contextlib import ExitStack

import numpy as np

import concourse.bass as bass
from concourse import mybir

F32 = mybir.dt.float32
F32R = mybir.dt.float32r
ALU = mybir.AluOpType
ACT = mybir.ActivationFunctionType
AXX = mybir.AxisListType.X

T = 512
NB = 4
EPS = 1e-6
NRAW = 3
NSPL = 3
SLAB = 1024

PCOL = {}
_at = 0
for _n, _w in (("norm_g", 48), ("mem_g", 8), ("gconv", 48), ("gn", 1), ("cw", 124), ("cb", 4), ("lg", 4), ("lb", 4),
               ("fw", 132), ("fb", 44), ("rpre", 8), ("rpost", 8), ("kvn", 8), ("spre", 8), ("spost", 8),
               ("alog", 4), ("dtb", 4)):
    PCOL[_n] = _at
    _at += _w
NPRM = _at

CST = ["ident", "ones", "tri", "blk", "m1t", "mc", "ms", "m2", "m4", "m8", "m16", "m32"]


class Engine:

    def __init__(self, sems):
        self.sems = sems
        self.phase = 0
        self.n = 0
        self.q = []
        self.seen = {}

    def wait(self, *toks):
        for t in toks:
            if t is None:
                continue
            if isinstance(t, list):
                self.wait(*t)
                continue
            s, v = t
            if self.seen.get(s.name, 0) < v:
                self.seen[s.name] = v
                self.q.append(("w", s, v))

    def do(self, fn, *toks, inc=True):
        self.wait(*toks)
        if not inc:
            self.q.append(("i", fn, None))
            return None
        self.n += 1
        s = self.sems[self.phase]
        self.q.append(("i", fn, s))
        return (s, self.n)

    def last(self):
        return (self.sems[self.phase], self.n) if self.n else None

    def next_phase(self):
        self.phase += 1
        self.n = 0

    def emit(self, e):
        for kind, a, b in self.q:
            if kind == "w":
                e.wait_ge(a, b)
            else:
                ins = a(e)
                if b is not None:
                    ins.then_inc(b, 1)


class Banks(list):

    def __init__(self, x):
        super().__init__(x)
        self.held = [False] * len(x)

    def __setitem__(self, i, toks):
        self.held[i] = False
        super().__setitem__(i, toks)


def bc(ap, n):
    return ap.unsqueeze(2).broadcast_to([ap.shape[0], ap.shape[1], n])


def bm(ap, n):
    return ap.unsqueeze(1).broadcast_to([ap.shape[0], n, ap.shape[1]])


def weight_order():
    o = []
    for c in range(4):
        o += [("wcfm", 4 + c), ("wcfm", c)]
    for p in range(2):
        for j in range(3):
            for h in range(2):
                o.append(("wqkv", j * 4 + 2 * p + h))
    o += [("wgate", i) for i in range(4)]
    o += [("wmk", i) for i in range(8)]
    o += [("wmv", i) for i in range(8)]
    o += [("wout", i) for i in range(8)]
    o += [("wxq", i) for i in range(8)]
    o += [("wxo", i) for i in range(8)]
    for a, b in ((0, 8), (8, 16), (16, 22)):
        for j in range(a, b):
            o += [("wup", j), ("wup", 22 + j)]
        o += [("wdn", (a // 8) * 8 + i) for i in range(8)]
    for h in range(4):
        o += [("rqk", 4 * h + i) for i in range(4)]
        o += [("rv", 4 * h + i) for i in range(4)]
        o += [("rg", 4 * h + i) for i in range(4)]
        if h % 2:
            o += [("rout", (h // 2) * 8 + i) for i in range(8)]
    for p in range(4):
        o += [("sk", 2 * p), ("sk", 2 * p + 1), ("sq", 2 * p), ("sq", 2 * p + 1)]
        o += [("sv", 4 * p + i) for i in range(4)]
        o += [("sg", 4 * p + i) for i in range(4)]
        if p:
            o += [("sout", 4 * (p - 1) + i) for i in range(4)]
    o += [("sout", 12 + i) for i in range(4)]
    return o


def program(nc, A, out):
    root = ExitStack()
    with root:
        def sem(n):
            return root.enter_context(nc.semaphore(n))

        NPH = 6
        PE, AC, DV, GP = (Engine([sem(f"s_{n}{i}") for i in range(NPH)]) for n in ("pe", "act", "dve", "pool"))
        SY = Engine([sem("s_sy")])
        engines = (PE, AC, DV, GP)

        def alloc(stack, name, shape, dt=F32):
            return stack.enter_context(nc.sbuf_tensor(name, shape, dt))

        banks = [root.enter_context(nc.psum_tensor(f"ps{i}", [128, 512], F32)) for i in range(8)]
        bank_free = Banks([[] for _ in range(8)])
        bank_at = {}

        def bank(pool=(0, 1, 2, 3)):
            bank_at[pool] = bank_at.get(pool, -1) + 1
            i = pool[bank_at[pool] % len(pool)]
            assert not bank_free.held[i], i
            bank_free.held[i] = True
            return i, banks[i], bank_free[i]

        dma_sems = {}

        def load(name, dst, src, *after, eng=SY):
            s = dma_sems.get(name)
            if s is None:
                s = dma_sems[name] = [sem("d_" + name), 0]
            s[1] += 16
            sm, v = s[0], s[1]
            eng.wait(*after)
            eng.q.append(("d", (dst, src), sm))
            return (sm, v)

        RAW = [alloc(root, f"raw{i}", [128, SLAB]) for i in range(NRAW)]
        SH = [alloc(root, f"sh{i}", [128, SLAB], F32R) for i in range(NSPL)]
        SL = [alloc(root, f"sl{i}", [128, SLAB], F32R) for i in range(NSPL)]
        XH = alloc(root, "xh", [128, 8, T], F32R)
        XL = alloc(root, "xl", [128, 8, T], F32R)
        X2H = alloc(root, "x2h", [128, 8, T], F32R)
        X2L = alloc(root, "x2l", [128, 8, T], F32R)
        PRM = alloc(root, "prm", [128, NPRM])
        IDN = alloc(root, "idn", [128, 128])
        ONE = alloc(root, "one", [128, 128])
        RB = alloc(root, "rb", [128, T])
        RC = alloc(root, "rc", [128, 16])
        MSQ = alloc(root, "msq", [128, 16])
        NH = alloc(root, "nh", [128, 16])
        SQ = [alloc(root, f"sq{i}", [128, T]) for i in range(2)]
        DG = alloc(root, "dg", [128, T])

        def prm(n, i=0):
            return PRM[:, PCOL[n] + i:PCOL[n] + i + 1]

        t_prm = load("prm", PRM[:], A["prm"])
        t_cst = load("cst", IDN[:], A["cst"][0])
        t_cst = load("cst", ONE[:], A["cst"][1])
        t_nh = GP.do(lambda e: e.memset(NH[:], -0.5))

        order = weight_order()
        raw_free = [[] for _ in range(NRAW)]
        spl_free = [None] * NSPL
        raw_tok = {}
        spl_tok = {}
        st = {"dma": 0, "spl": 0, "use": 0}

        def send(j):
            n, i = order[j]
            raw_tok[j] = load(f"w{j % NRAW}", RAW[j % NRAW][:], A[n][i], raw_free[j % NRAW])

        def split(j):
            r, s = j % NRAW, j % NSPL
            a = AC.do(lambda e: e.activation(SH[s][:], RAW[r][:], ACT.Copy), raw_tok[j], spl_free[s])
            d = DV.do(lambda e: e.tensor_tensor(SL[s][:], RAW[r][:], SH[s][:].bitcast(F32), ALU.subtract),
                      a, raw_tok[j])
            raw_free[r] = [a, d]
            spl_tok[j] = [a, d]

        def pump():
            while True:
                if st["dma"] < len(order) and st["dma"] < st["spl"] + NRAW:
                    send(st["dma"])
                    st["dma"] += 1
                elif st["spl"] < min(len(order), st["use"] + NSPL):
                    split(st["spl"])
                    st["spl"] += 1
                else:
                    return

        def take(name, cols):
            j = st["use"]
            assert order[j][0] == name, (order[j], name)
            pump()
            s = j % NSPL
            v = [x[s][:].rearrange("p (k c) -> p k c", c=cols) for x in (SH, SL)]
            return v[0], v[1], spl_tok[j], s

        def done(s, tok):
            spl_free[s] = tok
            st["use"] += 1
            pump()

        fills = []

        def tick():
            while fills:
                try:
                    next(fills[0])
                    return
                except StopIteration:
                    fills.pop(0)

        def drain():
            while fills:
                tick()

        small = []

        def trickle(n=1):
            for _ in range(n):
                if small:
                    small.pop(0)()

        def mm3(dst, ah, al, bh, bl, start, stop, *w, inc=False):
            PE.do(lambda e: e.matmul(dst, ah, bh, start=start, stop=False, skip_group_check=True), *w, inc=False)
            PE.do(lambda e: e.matmul(dst, ah, bl, start=False, stop=False, skip_group_check=True), inc=False)
            return PE.do(lambda e: e.matmul(dst, al, bh, start=False, stop=stop, skip_group_check=True), inc=stop or inc)

        def mm(dst, a, b, start, stop, *w, inc=None):
            return PE.do(lambda e: e.matmul(dst, a, b, start=start, stop=stop, skip_group_check=True), *w,
                         inc=stop if inc is None else inc)

        def proj_fm(name, dst, X, xt, nk, bw, N=T, groups=1, mt=1):
            for g in range(groups):
                wh, wl, wt, s = take(name, 128 * mt)
                for m in range(mt):
                    for k in range(nk):
                        kk = g * 8 + k
                        c = slice(m * 128, m * 128 + 128)
                        t = mm3(dst[m][:, 0:N], wh[:, k, c], wl[:, k, c], X[0][:, kk, 0:N], X[1][:, kk, 0:N],
                                kk == 0, g == groups - 1 and k == nk - 1, wt, xt[kk], bw)
                        if m == 0 and k == nk // 2 - 1:
                            tick()
                            trickle()
                done(s, t)
                trickle()
            tick()
            return t

        def proj_tm(name, dst, X, xt, bw, nb=NB):
            for g in range(4):
                wh, wl, wt, s = take(name, 512)
                for tb in range(nb):
                    for k in range(2):
                        kk = 2 * g + k
                        c = slice(tb * 128, tb * 128 + 128)
                        st_, sp_ = kk == 0, kk == 7
                        t = mm3(dst[tb][:], X[0][:, kk, c], X[1][:, kk, c], wh[:, k, :], wl[:, k, :],
                                st_, sp_, wt, xt[kk], bw, inc=(tb == nb - 1 and k == 1))
                    if tb == nb // 2 - 1:
                        tick()
                        trickle()
                done(s, t)
                tick()
                trickle()
            return t

        PE.wait(t_cst)
        for e_ in (AC, DV, GP):
            e_.wait(t_prm, t_cst)
        GP.wait(t_nh)
        DV.wait(t_nh)

        sq_free = [None, None]
        sq_at = [0]

        def colsum(src, col0, dst, first, last, N, srct, bw=None):
            i = sq_at[0] % 2
            sq_at[0] += 1
            a = AC.do(lambda e: e.activation(SQ[i][:, 0:N], src, ACT.Square), srct, sq_free[i])

            def sums():
                for tb in range(N // 128):
                    t = mm(dst[:, col0 + tb:col0 + tb + 1], SQ[i][:, tb * 128:tb * 128 + 128], ONE[:, 0:1],
                           first and tb == 0, last, a, bw, inc=(tb == N // 128 - 1))
                sq_free[i] = t
                return t
            return sums

        rc_free = {}

        def rstd(src, n, t, scale, col=0):
            m, r = MSQ[:, col:col + n], RC[:, col:col + n]
            d = DV.do(lambda e: e.tensor_scalar(m, src, scale, EPS, ALU.mult, ALU.add), t, rc_free.get(col))
            g = GP.do(lambda e: e.tensor_tensor(r, m, NH[:, 0:n], ALU.pow), d)
            rc_free[col] = g
            return d, g

        dg_free = [None]

        def rows(col, nb, ct, bw, dst):
            d = DV.do(lambda e: e.tensor_tensor(DG[:, 0:nb * 128].rearrange("p (a b) -> p a b", b=128),
                                                bm(IDN[:], nb), bc(col, 128), ALU.mult), ct, dg_free[0])
            t = mm(dst, ONE[:], DG[:, 0:nb * 128], True, True, d, bw)
            dg_free[0] = t
            return t

        ctx = {"PE": PE, "AC": AC, "DV": DV, "GP": GP}

        rb_free = [[]]

        def stats(k_src, N, post=()):
            bi, bk, bw = bank((7,))
            pend = None
            for k in range(8):
                ap, tk = k_src(k)
                f = colsum(ap, 0, bk, k == 0, k == 7, N, tk, bw)
                if pend:
                    pend()
                pend = f
            return bi, bk, pend()

        def finish_stats(bi, bk, t, nb, rb=None, keep=True):
            d, g = rstd(bk[:, 0:nb], nb, t, 1.0 / 1024)
            bank_free[bi] = [d]
            i2, b2, w2 = bank((6,))
            t2 = rows(RC[:, 0:nb], nb, g, w2, b2[:, 0:nb * 128])
            if not keep:
                return i2, b2, t2
            c = DV.do(lambda e: e.tensor_copy(rb[:, 0:nb * 128], b2[:, 0:nb * 128]), t2, rb_free[0])
            bank_free[i2] = [c]
            return g, c

        def scaled(src, g, k, XXH, XXL, tk, N=T, free=None):
            a = AC.do(lambda e: e.activation(XXH[:, k, 0:N], src, ACT.Copy, scale=g), tk, free)
            d = DV.do(lambda e: e.scalar_tensor_tensor(XXL[:, k, 0:N], src, g, XXH[:, k, 0:N].bitcast(F32),
                                                       ALU.mult, ALU.subtract), a, tk, free)
            return [a, d]

        def parts(src, k, XXH, XXL, tk, free=None):
            a = AC.do(lambda e: e.activation(XXH[:, k, :], src, ACT.Copy), tk, free)
            d = DV.do(lambda e: e.tensor_tensor(XXL[:, k, :], src, XXH[:, k, :].bitcast(F32), ALU.subtract),
                      a, tk, free)
            return [a, d]

        keepA = ExitStack()
        QK0 = alloc(keepA, "qk0", [128, 4, T])
        ACC = alloc(keepA, "acc", [128, 4, T])
        ph = ExitStack()
        XF = alloc(ph, "cp", [128, 4, T + 32])
        CP = XF
        QK1 = alloc(ph, "qk1", [128, 4, T])
        CM = alloc(ph, "cm", [128, len(CST) - 2, 128])
        t_cm = load("cm", CM[:], A["cst"][2:].rearrange("n p c -> p n c"))
        cst = {n: CM[:, i, :] for i, n in enumerate(CST[2:])}
        DV.wait(t_cm)
        PE.wait(t_cm)
        GP.wait(t_cm)
        UNIT = {n: alloc(ph, n, [128, 2 * T]) for n in ("u_bv", "u_kbe", "u_kd", "u_at", "u_lt", "u_t", "u_tt", "u_x")}
        GT = alloc(ph, "gt", [128, 4, T])
        PADB = [alloc(ph, f"pad{i}", [128, T + 4]) for i in range(2)]
        CA = alloc(ph, "ca", [128, T])
        VF = alloc(ph, "vf", [128, T])
        SG = alloc(ph, "sg_", [128, T])
        SS = alloc(ph, "ss", [128, 2, 128])
        SMV = alloc(ph, "smv", [128, 160])
        WAB = alloc(ph, "wab", [128, 64])
        WABH = alloc(ph, "wabh", [128, 64], F32R)
        WABL = alloc(ph, "wabl", [128, 64], F32R)

        xsrc = A["xT"].rearrange("(k p) t -> p k t", p=128)
        t_x = [load(f"x{i}", (QK0, ACC)[i // 2][:, 2 * (i % 2):2 * (i % 2) + 2, :], xsrc[:, 2 * i:2 * i + 2, :])
               for i in range(4)]
        t_wab = load("wab", WAB[:], A["wab"])
        pump()

        def xk(k):
            return (QK0, ACC)[k // 4][:, k % 4, :]

        xt = [scaled(xk(k), prm("norm_g", k), k, XH, XL, t_x[k // 2]) for k in range(8)]
        bi, bk, tt_ = stats(lambda k: (xk(k), t_x[k // 2]), T)
        t_rc, t_rb = finish_stats(bi, bk, tt_, 4, RB)
        x_read = [AC.last(), DV.last()]
        tabh = AC.do(lambda e: e.activation(WABH[:], WAB[:], ACT.Copy), t_wab)
        tabl = DV.do(lambda e: e.tensor_tensor(WABL[:], WAB[:], WABH[:].bitcast(F32), ALU.subtract), tabh, t_wab)
        X = (XH, XL)

        zp = [GP.do(lambda e, p=p: e.memset(p[:, 0:4], 0.0)) for p in PADB]
        zp.append(GP.do(lambda e: e.memset(CP[:, :, 0:32], 0.0)))
        zp.append(GP.do(lambda e: e.memset(SS[:], 0.0)))
        t_ss0 = zp[-1]

        acc_t = [None] * 4

        def cfm_conv(c, tk):
            stt = {"t": tk}

            def one(j):
                w = prm("cw", c * 31 + j)
                src = CP[:, c, 2 + j:2 + j + T]
                if j == 0:
                    stt["t"] = DV.do(lambda e: e.tensor_scalar(ACC[:, c, :], src, w, prm("cb", c), ALU.mult,
                                                               ALU.add), stt["t"], x_read)
                else:
                    stt["t"] = DV.do(lambda e: e.scalar_tensor_tensor(ACC[:, c, :], src, w, ACC[:, c, :],
                                                                      ALU.mult, ALU.add), stt["t"])
                acc_t[c] = stt["t"]
            return [lambda j=j: one(j) for j in range(31)]

        sg_free = [None]
        for c in range(4):
            i, b, w = bank()
            t = proj_fm("wcfm", [b], X, xt, 8, w)
            d = DV.do(lambda e, b=b: e.tensor_tensor(SG[:], b[:], RB[:], ALU.mult), t, t_rb, sg_free[0])
            bank_free[i] = [d]
            a = AC.do(lambda e: e.activation(SG[:], SG[:], ACT.Sigmoid), d)
            i, b, w = bank()
            t = proj_fm("wcfm", [b], X, xt, 8, w)
            cpv = CP[:, c, 32:32 + T]
            d = DV.do(lambda e, b=b, v=cpv: e.tensor_tensor(v, b[:], RB[:], ALU.mult), t, t_rb)
            bank_free[i] = [d]
            d = DV.do(lambda e, v=cpv: e.tensor_tensor(v, v, SG[:], ALU.mult), d, a, zp)
            sg_free[0] = d
            small.extend(cfm_conv(c, d))

        i, b, w = bank()
        PE.wait(tabh, tabl)
        for tb in range(NB):
            for k in range(8):
                c = slice(tb * 128, tb * 128 + 128)
                t = mm3(b[:, tb * 8:tb * 8 + 8], XH[:, k, c], XL[:, k, c], WABH[:, 8 * k:8 * k + 8],
                        WABL[:, 8 * k:8 * k + 8], k == 0, k == 7, w, xt[k])
        ab = SMV[:, 0:32].rearrange("p (b c) -> p b c", c=8)
        d = DV.do(lambda e, b=b: e.tensor_tensor(ab, b[:, 0:32].rearrange("p (b c) -> p b c", c=8), bc(RC[:, 0:4], 8),
                                            ALU.mult), t, t_rc)
        bank_free[i] = [d]
        av = ab[:, :, 0:4]
        d = DV.do(lambda e: e.tensor_tensor(av, av, bm(PRM[:, PCOL["dtb"]:PCOL["dtb"] + 4], 4), ALU.add), d)

        def sv(i, n=16):
            return SMV[:, 32 + i * 16:32 + i * 16 + n]

        def sv3(i):
            return sv(i).rearrange("p (b h) -> p b h", h=4)

        AC.q.append(("i", lambda e: e.preload_act_table_set("natural_log_exp_and_others"), None))
        ea = AC.do(lambda e: e.activation(MSQ[:, 8:12], PRM[:, PCOL["alog"]:PCOL["alog"] + 4], ACT.Exp))
        a1 = AC.do(lambda e: e.activation(sv3(0), av, ACT.Abs), d)
        a2 = AC.do(lambda e: e.activation(sv(0), sv(0), ACT.Exp, scale=-1.0), a1)
        a3 = AC.do(lambda e: e.activation(sv(0), sv(0), ACT.Ln, bias=1.0), a2)
        d1 = DV.do(lambda e: e.scalar_tensor_tensor(sv3(1), av, 0.0, sv3(0), ALU.max, ALU.add), a3, d)
        d2 = DV.do(lambda e: e.scalar_tensor_tensor(sv3(1), sv3(1), -1.0, bm(MSQ[:, 8:12], 4), ALU.mult, ALU.mult),
                   d1, ea)
        a4 = AC.do(lambda e: e.activation(sv3(2), ab[:, :, 4:8], ACT.Sigmoid), d)
        AC.q.append(("i", lambda e: e.preload_act_table_set("natural_log_exp_and_others"), None))
        i, b, w = bank()
        mm(b[:, 0:16], cst["tri"], sv(1), True, True, d2, w, inc=False)
        t = mm(b[:, 16:32], cst["blk"], sv(1), False, True)
        d3 = DV.do(lambda e, b=b: e.tensor_copy(SMV[:, 80:112], b[:, 0:32]), t)
        bank_free[i] = [d3]
        a5 = AC.do(lambda e: e.activation(sv(5), sv(3), ACT.Exp), d3)
        d4 = DV.do(lambda e: e.tensor_tensor(sv(6), sv(5), sv(2), ALU.mult), a5, a4)
        d5 = DV.do(lambda e: e.tensor_tensor(sv(7), sv(4), sv(3), ALU.subtract), d3)
        a6 = AC.do(lambda e: e.activation(sv(7), sv(7), ACT.Exp), d5)
        sm_t = [d4, a6, a4, d3]
        DV.wait(*sm_t)
        AC.wait(*sm_t)
        t_beta, t_gc = a4, d3

        pad_free = [[], []]
        pad_at = [0]
        ca_free = [None]
        vf_free = [[]]
        unit_free = {}

        def evac_conv(tile, dst, extra):
            i, b, w = bank()
            t = proj_fm("wqkv", [b], X, xt, 8, w)
            pi = pad_at[0] % 2
            pad_at[0] += 1
            P = PADB[pi]
            d = DV.do(lambda e: e.tensor_tensor(P[:, 4:4 + T], b[:], RB[:], ALU.mult), t, pad_free[pi], zp)
            bank_free[i] = [d]
            d = DV.do(lambda e: e.tensor_scalar(CA[:], P[:, 1:1 + T], prm("gconv", tile * 4), None, ALU.mult),
                      d, ca_free[0])
            for j in range(1, 4):
                d = DV.do(lambda e, j=j: e.scalar_tensor_tensor(CA[:], P[:, 1 + j:1 + j + T],
                                                                prm("gconv", tile * 4 + j), CA[:], ALU.mult,
                                                                ALU.add), d)
            pad_free[pi] = [d]
            a = AC.do(lambda e: e.activation(dst, CA[:], ACT.Silu), d, extra)
            ca_free[0] = a
            return a

        def v4(x):
            return x.rearrange("p (h b c) -> p h b c", h=2, b=NB)

        u_done = []

        def gdn(p, QK, qk_t, out_t):
            UB, UKB, UKD, UA, UL, UT, UTT, UX = (UNIT[n][:] for n in
                                                 ("u_bv", "u_kbe", "u_kd", "u_at", "u_lt", "u_t", "u_tt", "u_x"))
            h3 = lambda x, h: x[:, h * T:h * T + T].rearrange("p (b c) -> p b c", c=128)
            hd = lambda x, h: x[:, h * T:h * T + T]
            gch = lambda i, h: sv3(i)[:, :, 2 * p + h]
            bi, bk, bw = bank((4, 5))
            pend = []
            for n in range(4):
                f = colsum(QK[:, n, :], 4 * n, bk, n == 0, True, T, qk_t[n], bw)
                pend.append(f)
                if len(pend) > 1:
                    pend.pop(0)()
            t = pend[0]()
            yield
            d, g = rstd(bk[:, 0:16], 16, t, 1.0)
            bank_free[bi] = [d]
            nt = [None] * 4
            for n in range(4):
                i2, b2, w2 = bank((4, 5))
                t = rows(RC[:, 4 * n:4 * n + 4], 4, g, w2, b2[:])
                if n < 2:
                    nt[n] = DV.do(lambda e, n=n, b2=b2: e.scalar_tensor_tensor(
                        QK[:, n, :], QK[:, n, :], 128.0 ** -0.5, b2[:], ALU.mult, ALU.mult), t, qk_t[n])
                else:
                    nt[n] = DV.do(lambda e, n=n, b2=b2: e.tensor_tensor(QK[:, n, :], QK[:, n, :], b2[:], ALU.mult),
                                  t, qk_t[n])
                bank_free[i2] = [nt[n]]
                yield
            dt_ = [None, None]
            kb = [None, None]
            qe = [None, None]
            at = [None, None]
            lt = [None, None]
            for h in range(2):
                i2, b2, w2 = bank((4, 5))
                t = rows(gch(3, h), 4, t_gc, w2, b2[:])
                ar = []
                for tb in range(NB):
                    ar.append(AC.do(lambda e, h=h, tb=tb, b2=b2: e.activation(
                        h3(UA, h)[:, tb], b2[:, tb * 128:tb * 128 + 128], ACT.Relu, scale=-1.0,
                        bias=sv(3)[:, tb * 4 + 2 * p + h:tb * 4 + 2 * p + h + 1]), t, unit_free.get("u_at")))
                a = AC.do(lambda e, h=h: e.activation(hd(UA, h), hd(UA, h), ACT.Exp, scale=-1.0), ar)
                a2 = AC.do(lambda e, h=h, b2=b2: e.activation(hd(UT, h), b2[:], ACT.Exp), t, unit_free.get("u_t"))
                bank_free[i2] = [a2]
                dt_[h] = GP.do(lambda e, h=h: e.tensor_tensor(h3(UA, h), h3(UA, h), bm(cst["mc"], 4), ALU.mult), a)
                i2, b2, w2 = bank((4, 5))
                t = rows(gch(2, h), 4, t_beta, w2, b2[:])
                kb[h] = DV.do(lambda e, h=h, b2=b2: e.tensor_tensor(hd(UX, h), QK[:, 2 + h, :], b2[:], ALU.mult),
                              t, nt[2 + h], unit_free.get("u_x"))
                bank_free[i2] = [kb[h]]
                yield
                i3, b3, w3 = bank((4, 5))
                for tb in range(NB):
                    c = slice(tb * 128, tb * 128 + 128)
                    t = mm(b3[:, c], QK[:, 2 + h, c], hd(UX, h)[:, c], True, True, kb[h], w3, nt[2 + h])
                lm = GP.do(lambda e, h=h: e.tensor_tensor(h3(UL, h), h3(UA, h), bm(cst["ms"], 4), ALU.mult),
                           dt_[h], unit_free.get("u_lt"))
                lt[h] = DV.do(lambda e, h=h, b3=b3: e.tensor_tensor(hd(UL, h), hd(UL, h), b3[:], ALU.mult), t, lm)
                bank_free[i3] = [lt[h]]
                yield
                i3, b3, w3 = bank((4, 5))
                for tb in range(NB):
                    c = slice(tb * 128, tb * 128 + 128)
                    t = mm(b3[:, c], QK[:, 2 + h, c], QK[:, h, c], True, True, w3, nt[h])
                at[h] = DV.do(lambda e, h=h, b3=b3: e.tensor_tensor(hd(UA, h), hd(UA, h), b3[:], ALU.mult), t,
                              dt_[h], lm)
                bank_free[i3] = [at[h]]
                qe[h] = DV.do(lambda e, h=h: e.tensor_tensor(QK[:, h, :], QK[:, h, :], hd(UT, h), ALU.mult), a2, t)
                eg = DV.do(lambda e, h=h: e.tensor_copy(EG[:, h, :], hd(UT, h)[:, 63:T:64]), a2,
                                        unit_free.get("eg"))
                yield
                i3, b3, w3 = bank((4, 5))
                for tb in range(NB):
                    c = slice(tb * 128, tb * 128 + 128)
                    t = PE.do(lambda e, c=c, h=h, b3=b3: e.transpose(b3[:, c], QK[:, 2 + h, c], IDN[:]), w3,
                              nt[2 + h])
                b33 = b3[:].rearrange("p (b c) -> p b c", c=128)
                k1 = DV.do(lambda e, h=h, b33=b33: e.tensor_tensor(h3(UKB, h), b33, bc(gch(6, h), 128), ALU.mult),
                           t, unit_free.get("u_kbe"))
                k2 = DV.do(lambda e, h=h, b33=b33: e.tensor_tensor(h3(UKD, h), b33, bc(gch(7, h), 128), ALU.mult),
                           t, unit_free.get("u_kd"))
                bank_free[i3] = [k2]
                yield
            tt = [None, None]
            tl = [None, None]
            for h in range(2):
                d = DV.do(lambda e, h=h: e.scalar_tensor_tensor(h3(UTT, h), h3(UL, h), -1.0, bm(cst["m1t"], 4),
                                                                ALU.mult, ALU.mult), lt[h], unit_free.get("u_tt"))
                tt[h] = DV.do(lambda e, h=h: e.tensor_tensor(h3(UTT, h), h3(UTT, h), bm(IDN[:], 4), ALU.add), d)
            for h in range(2):
                i3, b3, w3 = bank((4, 5))
                for tb in range(NB):
                    c = slice(tb * 128, tb * 128 + 128)
                    t = PE.do(lambda e, c=c, h=h, b3=b3: e.transpose(b3[:, c], hd(UTT, h)[:, c], IDN[:]), w3,
                              tt[h])
                tl[h] = AC.do(lambda e, h=h, b3=b3: e.activation(hd(UT, h), b3[:], ACT.Copy), t, qe[h], eg)
                bank_free[i3] = [tl[h]]
            yield
            xfree = [kb[0], kb[1], PE.last()]
            for s in (2, 4, 8, 16, 32):
                lastl = s == 32
                xx = [None, None]
                for h in range(2):
                    i3, b3, w3 = bank((4, 5))
                    for tb in range(NB):
                        c = slice(tb * 128, tb * 128 + 128)
                        t = mm(b3[:, c], hd(UL, h)[:, c], hd(UT, h)[:, c], True, True, w3, tl[h], lt[h])
                    b33 = b3[:].rearrange("p (b c) -> p b c", c=128)
                    xx[h] = DV.do(lambda e, h=h, b33=b33, s=s: e.tensor_tensor(h3(UX, h), b33, bm(cst[f"m{s}"], 4),
                                                                              ALU.mult), t, xfree)
                    bank_free[i3] = [xx[h]]
                yield
                xfree = []
                for h in range(2):
                    if not lastl:
                        i3, b3, w3 = bank((4, 5))
                        for tb in range(NB):
                            c = slice(tb * 128, tb * 128 + 128)
                            t = mm(b3[:, c], hd(UTT, h)[:, c], hd(UX, h)[:, c], True, True, w3, xx[h], tt[h])
                    i4, b4, w4 = bank((4, 5))
                    for tb in range(NB):
                        c = slice(tb * 128, tb * 128 + 128)
                        t2 = mm(b4[:, c], hd(UX, h)[:, c], hd(UTT, h)[:, c], True, True, w4, xx[h], tt[h])
                    xfree.append(t2)
                    if not lastl:
                        tl[h] = DV.do(lambda e, h=h, b3=b3: e.tensor_tensor(hd(UT, h), hd(UT, h), b3[:],
                                                                            ALU.subtract), t, t2)
                        bank_free[i3] = [tl[h]]
                    tt[h] = DV.do(lambda e, h=h, b4=b4: e.tensor_tensor(hd(UTT, h), hd(UTT, h), b4[:],
                                                                        ALU.subtract), t2)
                    bank_free[i4] = [tt[h]]
                yield
            ut = [None, None]
            wt = [None, None]
            for h in range(2):
                i3, b3, w3 = bank((4, 5))
                for tb in range(NB):
                    c = slice(tb * 128, tb * 128 + 128)
                    t = mm(b3[:, c], hd(UTT, h)[:, c], hd(UB, h)[:, c], True, True, w3, tt[h], bv_t[p][h])
                ut[h] = AC.do(lambda e, h=h, b3=b3: e.activation(hd(UT, h), b3[:], ACT.Copy), t)
                bank_free[i3] = [ut[h]]
                i3, b3, w3 = bank((4, 5))
                for tb in range(NB):
                    c = slice(tb * 128, tb * 128 + 128)
                    t = mm(b3[:, c], hd(UKB, h)[:, c], hd(UTT, h)[:, c], True, True, w3)
                wt[h] = AC.do(lambda e, h=h, b3=b3: e.activation(hd(UX, h), b3[:], ACT.Copy), t, xx[h])
                bank_free[i3] = [wt[h]]
                yield
            VN = QK[:, 2:4, :].rearrange("p h (b c) -> p h b c", c=128)
            i4, po, w4 = bank((6,))
            i5, po1, w5 = bank((7,))
            P2 = [po, po1]
            s_t = [t_ss0 if p == 0 else None] * 2
            if p:
                z = GP.do(lambda e: e.memset(SS[:], 0.0), u_done)
                s_t = [z, z]
            for n in range(8):
                tb, o = n // 2, (n % 2) * 64
                R = slice(o, o + 64)
                cc = slice(n * 64, n * 64 + 64)
                i3, b3, w3 = bank((4, 5))
                for h in range(2):
                    t = mm(b3[R, h * 128:h * 128 + 128], hd(UX, h)[:, cc], SS[:, h, :], True, True, w3, wt[h],
                           s_t[h])
                U4 = UT.rearrange("p (h b c) -> p h b c", h=2, b=NB)
                vn = DV.do(lambda e, R=R, tb=tb, b3=b3, U4=U4: e.tensor_tensor(
                    VN[R, :, tb, :], U4[R, :, tb, :], b3[R, 0:256].rearrange("p (h c) -> p h c", h=2),
                    ALU.subtract), t, ut[0], ut[1], nt[2], nt[3])
                bank_free[i3] = [vn]
                for h in range(2):
                    mm(P2[h][:, cc], SS[:, h, :], QK[:, h, cc], True, False, s_t[h], qe[h], w4, w5)
                yield
                i3, b3, w3 = bank((4, 5))
                for h in range(2):
                    tk = mm(b3[:, h * 128:h * 128 + 128], hd(UKD, h)[R, tb * 128:tb * 128 + 128], VN[R, h, tb, :],
                            True, True, vn, w3)
                for h in range(2):
                    to = mm(P2[h][:, cc], VN[R, h, tb, :], hd(UA, h)[R, tb * 128 + o:tb * 128 + o + 64], False, True,
                            at[h])
                for h in range(2):
                    s_t[h] = DV.do(lambda e, h=h, n=n, b3=b3: e.scalar_tensor_tensor(
                        SS[:, h, :], SS[:, h, :], EG[:, h, n:n + 1], b3[:, h * 128:h * 128 + 128], ALU.mult,
                        ALU.add), tk, to, eg)
                bank_free[i3] = [s_t[1]]
                yield
            ot = []
            for h in range(2):
                ot.append(AC.do(lambda e, h=h: e.activation(QK[:, h, :], P2[h][:], ACT.Copy), to))
            bank_free[i4] = [ot[0]]
            bank_free[i5] = [ot[1]]
            u_done.extend([PE.last(), DV.last(), AC.last()])
            for n in list(UNIT) + ["eg"]:
                unit_free[n] = [PE.last(), DV.last(), AC.last()]
            out_t.extend(ot)

        EG = alloc(ph, "eg", [128, 2, 8])
        bv_t = [[None, None], [None, None]]
        o_t = [[], []]
        qk_t = [[None] * 4, [None] * 4]
        QKS = (QK0, QK1)

        def v_tm(p, h, a):
            i, b, w = bank((4, 5))
            for tb in range(NB):
                c = slice(tb * 128, tb * 128 + 128)
                t = PE.do(lambda e, c=c: e.transpose(b[:, c], VF[:, c], IDN[:]), w, a)
            vf_free[0] = [t]
            dst = UNIT["u_bv"][:, h * T:h * T + T].rearrange("p (b c) -> p b c", c=128)
            bv_t[p][h] = DV.do(lambda e: e.tensor_tensor(dst, b[:].rearrange("p (b c) -> p b c", c=128),
                                                         bc(sv3(2)[:, :, 2 * p + h], 128), ALU.mult), t,
                               unit_free.get("u_bv"))
            bank_free[i] = [bv_t[p][h]]

        for p in range(2):
            for j in range(2):
                for h in range(2):
                    qk_t[p][2 * j + h] = evac_conv(j * 4 + 2 * p + h, QKS[p][:, 2 * j + h, :], x_read)
            if p:
                drain()
            for h in range(2):
                a = evac_conv(8 + 2 * p + h, VF[:], vf_free[0])
                v_tm(p, h, a)
            fills.append(gdn(p, QKS[p], qk_t[p], o_t[p]))

        gt_t = []
        for c in range(4):
            i, b, w = bank()
            t = proj_fm("wgate", [b], X, xt, 8, w)
            d = DV.do(lambda e, b=b, c=c: e.tensor_tensor(GT[:, c, :], b[:], RB[:], ALU.mult), t)
            bank_free[i] = [d]
            gt_t.append(AC.do(lambda e, c=c: e.activation(GT[:, c, :], GT[:, c, :], ACT.Silu), d))

        while small:
            trickle()

        def cfm_norm():
            bi, bk, bw = bank((3,))
            for c in range(4):
                for tb in range(NB):
                    t = mm(bk[:, tb:tb + 1], ACC[:, c, tb * 128:tb * 128 + 128], ONE[:, 0:1], c == 0 and tb == 0,
                           c == 3, acc_t[c], bw)
            d = DV.do(lambda e: e.tensor_scalar(LNC[:, 0:4], bk[:, 0:4], 1.0 / 512, None, ALU.mult), t)
            bank_free[bi] = [d]
            i2, b2, w2 = bank((3,))
            t = rows(LNC[:, 0:4], 4, d, w2, b2[:])
            xs = []
            for c in range(4):
                xs.append(DV.do(lambda e, c=c: e.tensor_tensor(ACC[:, c, :], ACC[:, c, :], b2[:], ALU.subtract), t,
                                acc_t[c]))
            bank_free[i2] = [xs[-1]]
            yield
            bi, bk, bw = bank((3,))
            pend = None
            for c in range(4):
                f = colsum(ACC[:, c, :], 0, bk, c == 0, c == 3, T, xs[c], bw)
                if pend:
                    pend()
                pend = f
            t = pend()
            d = DV.do(lambda e: e.tensor_scalar(LNC[:, 4:8], bk[:, 0:4], 1.0 / 512, EPS, ALU.mult, ALU.add), t)
            g = GP.do(lambda e: e.tensor_tensor(LNC[:, 8:12], LNC[:, 4:8], NH[:, 0:4], ALU.pow), d)
            bank_free[bi] = [d]
            yield
            i2, b2, w2 = bank((3,))
            t = rows(LNC[:, 8:12], 4, g, w2, b2[:])
            for c in range(4):
                d = DV.do(lambda e, c=c: e.scalar_tensor_tensor(ACC[:, c, :], ACC[:, c, :], prm("lg", c), b2[:],
                                                                ALU.mult, ALU.mult), t)
                a = AC.do(lambda e, c=c: e.activation(ACC[:, c, :], ACC[:, c, :], ACT.Silu, bias=prm("lb", c)), d)
                mix_t[4 + c] = parts(ACC[:, c, :], 4 + c, X2H, X2L, a)
                acc_read.extend(mix_t[4 + c])
            bank_free[i2] = [d]

        LNC = alloc(ph, "lnc", [128, 12])
        mix_t = [None] * 8
        acc_read = []
        for _ in cfm_norm():
            tick()

        t_m = [load(f"x{i}", CP[:, i, 0:512].rearrange("p (k t) -> p k t", k=2),
                    A["memT"].rearrange("(k p) t -> p k t", p=128)[:, 2 * i:2 * i + 2, :], acc_t[3])
               for i in range(4)]

        def mk(k):
            return CP[:, k // 2, (k % 2) * 256:(k % 2) * 256 + 256]

        MXH = X2H[:, 0:4, :].rearrange("p k (a t) -> p (k a) t", a=2)
        MXL = X2L[:, 0:4, :].rearrange("p k (a t) -> p (k a) t", a=2)
        mt_ = [scaled(mk(k), prm("mem_g", k), k, MXH, MXL, t_m[k // 2], N=256) for k in range(8)]
        bi, bk, bw = bank((3,))
        pend = None
        for k in range(8):
            f = colsum(mk(k), 0, bk, k == 0, k == 7, 256, t_m[k // 2], bw)
            if pend:
                pend()
            pend = f
        t = pend()
        d = DV.do(lambda e: e.tensor_scalar(LNC[:, 0:2], bk[:, 0:2], 1.0 / 1024, EPS, ALU.mult, ALU.add), t)
        mrc = GP.do(lambda e: e.tensor_tensor(LNC[:, 2:4], LNC[:, 0:2], NH[:, 0:2], ALU.pow), d)
        bank_free[bi] = [d]
        i2, b2, w2 = bank((3,))
        t = rows(LNC[:, 2:4], 2, mrc, w2, b2[:, 0:256])
        MRB = SG[:, 0:256]
        mrb = DV.do(lambda e: e.tensor_copy(MRB, b2[:, 0:256]), t, sg_free[0])
        bank_free[i2] = [mrb]
        KM = ACC[:].rearrange("p a (b t) -> p (a b) t", t=256)
        VM = QK0[:].rearrange("p a t -> p (a t)").rearrange("p (b c) -> p b c", b=2)
        km_t = []
        for m in range(8):
            i, b, w = bank((0, 1, 2))
            t = proj_fm("wmk", [b], (MXH, MXL), mt_, 8, w, N=256)
            km_t.append(DV.do(lambda e, b=b, m=m: e.tensor_tensor(KM[:, m, :], b[:, 0:256], MRB, ALU.mult), t, mrb,
                              acc_read))
            bank_free[i] = [km_t[-1]]
        fin_t = []

        def gdn_out(p):
            QK = QKS[p]
            for h in range(2):
                hh = 2 * p + h
                bi, bk, bw = bank((3,))
                t = colsum(QK[:, h, :], 0, bk, True, True, T, o_t[p][h], bw)()
                d = DV.do(lambda e: e.tensor_scalar(LNC[:, 4:8], bk[:, 0:4], 1.0 / 128, EPS, ALU.mult, ALU.add), t)
                g = GP.do(lambda e: e.tensor_tensor(LNC[:, 8:12], LNC[:, 4:8], NH[:, 0:4], ALU.pow), d)
                bank_free[bi] = [d]
                i2, b2, w2 = bank((3,))
                t = rows(LNC[:, 8:12], 4, g, w2, b2[:])
                d = DV.do(lambda e, h=h, b2=b2: e.scalar_tensor_tensor(QK[:, h, :], QK[:, h, :], prm("gn"), b2[:],
                                                                       ALU.mult, ALU.mult), t, o_t[p][h])
                bank_free[i2] = [d]
                d = DV.do(lambda e, h=h, hh=hh: e.tensor_tensor(GT[:, hh, :], QK[:, h, :], GT[:, hh, :], ALU.mult),
                          d, gt_t[hh])
                fin_t.append(d)

        gdn_out(0)
        v_free = [AC.last(), DV.last(), PE.last()]
        vm_t = []
        for cg in range(2):
            bb = [bank((0, 1, 2)) for _ in range(2)]
            t = proj_tm("wmv", [x[1] for x in bb], (MXH, MXL), mt_, [x[2] for x in bb], nb=2)
            for tb in range(2):
                i, b, w = bb[tb]
                vm_t.append(AC.do(lambda e, b=b, tb=tb, cg=cg: e.activation(
                    VM[:, tb, cg * 512:cg * 512 + 512], b[:], ACT.Copy, scale=LNC[:, 2 + tb:3 + tb]), t, v_free,
                    mrc))
                bank_free[i] = [vm_t[-1]]
        mem_read = [PE.last()]
        drain()
        gdn_out(1)
        for hh in range(4):
            mix_t[hh] = parts(GT[:, hh, :], hh, X2H, X2L, fin_t[hh], mem_read)

        end_m = [e_.last() for e_ in engines]
        ph.close()

        def phase(names):
            for e_ in engines:
                e_.wait(end_m)

        ph = ExitStack()
        phase(0)
        for e_ in engines:
            e_.next_phase()

        def y_evac(k, b, i, t, first, last, ystate):
            if first:
                yt = AC.do(lambda e: e.activation(Y[:, k, :], b[:], ACT.Copy), t, y_free[0])
            else:
                yt = DV.do(lambda e: e.tensor_tensor(Y[:, k, :], Y[:, k, :], b[:], ALU.add), t, ystate["t"][k])
            ystate["t"][k] = yt
            bank_free[i] = [yt]
            if last:
                if k == 0:
                    ystate["bank"] = bank((7,))
                bi, bk, bw = ystate["bank"]
                f = colsum(Y[:, k, :], 0, bk, k == 0, k == 7, T, yt, bw)
                if ystate.get("pend"):
                    ystate["pend"]()
                ystate["pend"] = f

        y_free = [[]]

        def boundary(ystate, gpost, hts, pres):
            bi, bk, bw = ystate["bank"]
            t = ystate["pend"]()
            i2, b2, t2 = finish_stats(bi, bk, t, 4, keep=False)
            ht = []
            xts = [[] for _ in pres]
            pend = None
            sb_ = bank((7,))
            t_last = None
            for k in range(8):
                d = DV.do(lambda e, k=k: e.scalar_tensor_tensor(Y[:, k, :], Y[:, k, :], prm(gpost[0], gpost[1] + k),
                                                                b2[:], ALU.mult, ALU.mult), t2, ystate["t"][k])
                d = DV.do(lambda e, k=k: e.tensor_tensor(H[:, k, :], H[:, k, :], Y[:, k, :], ALU.add), d, hts[k])
                ht.append(d)
                if pres:
                    for n, (g, XXH, XXL, free) in enumerate(pres):
                        xts[n].append(scaled(H[:, k, :], prm(g[0], g[1] + k), k, XXH, XXL, d, free=free))
                    f = colsum(H[:, k, :], 0, sb_[1], k == 0, k == 7, T, d, sb_[2])
                    if pend:
                        pend()
                    pend = f
            bank_free[i2] = [ht[-1]]
            y_free[0] = [ht[-1]]
            if not pres:
                return ht, None, None, None
            t = pend()
            rb_free[0] = [DV.last(), AC.last()]
            g_, r_ = finish_stats(sb_[0], sb_[1], t, 4, RB)
            return ht, xts, g_, r_

        H = alloc(ph, "h", [128, 8, T])
        Y = alloc(ph, "y", [128, 8, T])
        hts = [load(f"h{i}", H[:, 2 * i:2 * i + 2, :], xsrc[:, 2 * i:2 * i + 2, :], end_m) for i in range(4)]
        hts = [hts[k // 2] for k in range(8)]
        X2 = (X2H, X2L)

        ys = {"t": [None] * 8}
        for m in range(8):
            i, b, w = bank()
            t = proj_fm("wout", [b], X2, mix_t, 8, w)
            y_evac(m, b, i, t, True, True, ys)
        xt_free = [PE.last()]
        hts, xts, t_rc, t_rb = boundary(ys, ("norm_g", 8), hts, [(("norm_g", 16), XH, XL, xt_free)])
        xt = xts[0]

        pa = ExitStack()
        QX = [alloc(pa, f"qx{i}", [128, 2, T]) for i in range(2)]
        PM = [alloc(pa, f"pm{i}", [128, NB, 256]) for i in range(2)]
        PT = alloc(pa, "pt", [128, 2, T])
        SX = alloc(pa, "sx", [128, 16])
        o_x = [None] * 8
        ax = {"q": [[], []], "pt": [], "sx": [], "pm": [[], []]}

        def attend(h, qt):
            Q = QX[h % 2]
            Pm = PM[h % 2]
            pe_ = []
            for u in range(2):
                i, b, w = bank((4, 5))
                for v in range(2):
                    c = slice((2 * u + v) * 128, (2 * u + v) * 128 + 128)
                    for d_ in range(2):
                        t = mm(b[:, v * 256:v * 256 + 256], Q[:, d_, c], KM[:, 2 * h + d_, :], d_ == 0, d_ == 1, w,
                               qt[d_], km_t[2 * h + d_])
                d = DV.do(lambda e, u=u, b=b: e.tensor_reduce(SX[:, 2 * u:2 * u + 2],
                                                              b[:].rearrange("p (v m) -> p v m", v=2), AXX,
                                                              ALU.max), t, ax["sx"])
                d = DV.do(lambda e, u=u: e.tensor_scalar(SX[:, 4 + 2 * u:6 + 2 * u], SX[:, 2 * u:2 * u + 2], -1.0 / 16,
                                                         None, ALU.mult), d)
                for v in range(2):
                    tb = 2 * u + v
                    a = AC.do(lambda e, tb=tb, v=v, b=b: e.activation(
                        Pm[:, tb, :], b[:, v * 256:v * 256 + 256], ACT.Exp, scale=1.0 / 16,
                        bias=SX[:, 4 + tb:5 + tb], accum_out=SX[:, 8 + tb:9 + tb]), d, ax["pm"][h % 2])
                    pe_.append(a)
                bank_free[i] = [a]
                yield
            ax["q"][h % 2] = [t]
            r = DV.do(lambda e: e.reciprocal(SX[:, 12:16], SX[:, 8:12]), pe_)
            n_ = DV.do(lambda e: e.tensor_tensor(Pm[:], Pm[:], bc(SX[:, 12:16], 256), ALU.mult), r)
            ax["sx"] = [n_]
            yield
            pt = []
            for mb in range(2):
                i, b, w = bank((4, 5))
                for tb in range(NB):
                    t = PE.do(lambda e, tb=tb, mb=mb, b=b: e.transpose(
                        b[:, tb * 128:tb * 128 + 128], Pm[:, tb, mb * 128:mb * 128 + 128], IDN[:]), w, n_)
                pt.append(AC.do(lambda e, mb=mb, b=b: e.activation(PT[:, mb, :], b[:], ACT.Copy), t, ax["pt"]))
                bank_free[i] = [pt[-1]]
            ax["pm"][h % 2] = [t]
            yield
            for et in range(2):
                i, b, w = bank((4, 5))
                for mb in range(2):
                    c = slice(h * 256 + et * 128, h * 256 + et * 128 + 128)
                    t = mm(b[:], VM[:, mb, c], PT[:, mb, :], mb == 0, mb == 1, w, pt[mb], vm_t)
                o_x[2 * h + et] = parts(b[:], 2 * h + et, X2H, X2L, t, xo_free)
                bank_free[i] = list(o_x[2 * h + et])
            ax["pt"] = [t]
            yield

        xo_free = [xt_free]
        for h in range(4):
            qt = []
            for d_ in range(2):
                i, b, w = bank()
                t = proj_fm("wxq", [b], (XH, XL), xt, 8, w)
                if d_ == 0 and len(fills) > 1:
                    while len(fills) > 1:
                        tick()
                qt.append(DV.do(lambda e, b=b, d_=d_, h=h: e.tensor_tensor(QX[h % 2][:, d_, :], b[:], RB[:],
                                                                          ALU.mult), t, t_rb, ax["q"][h % 2]))
                bank_free[i] = [qt[-1]]
            fills.append(attend(h, qt))
        drain()
        ys = {"t": [None] * 8}
        for m in range(8):
            i, b, w = bank()
            t = proj_fm("wxo", [b], X2, o_x, 8, w)
            y_evac(m, b, i, t, True, True, ys)
        xt_free = [PE.last()]
        hts, xts, t_rc, t_rb = boundary(ys, ("norm_g", 24), hts, [(("norm_g", 32), XH, XL, xt_free)])
        xt = xts[0]
        end_m = [e_.last() for e_ in engines]
        pa.close()
        phase(0)
        for e_ in engines:
            e_.next_phase()

        pf = ExitStack()
        UP = [alloc(pf, f"up{i}", [128, T + 4]) for i in range(4)]
        UC = [alloc(pf, f"uc{i}", [128, T]) for i in range(4)]
        zu = [GP.do(lambda e, u=u: e.memset(u[:, 0:4], 0.0)) for u in UP]
        up_free = [[] for _ in range(4)]
        uc_free = [[] for _ in range(4)]
        ys = {"t": [None] * 8}
        m_free = [PE.last()]
        mid = [None] * 8
        for part, (a0, b0) in enumerate(((0, 8), (8, 16), (16, 22))):
            for j in range(a0, b0):
                ab_ = []
                for half in range(2):
                    i, b, w = bank()
                    t = proj_fm("wup", [b], (XH, XL), xt, 8, w)
                    n = (2 * j + half) % 4
                    ch = j + 22 * half
                    U, C = UP[n], UC[n]
                    d = DV.do(lambda e, U=U, b=b: e.tensor_tensor(U[:, 4:4 + T], b[:], RB[:], ALU.mult), t, t_rb,
                              up_free[n], zu)
                    bank_free[i] = [d]
                    d = DV.do(lambda e, U=U, C=C, ch=ch: e.tensor_scalar(C[:], U[:, 2:2 + T], prm("fw", ch * 3),
                                                                         prm("fb", ch), ALU.mult, ALU.add), d,
                              uc_free[n])
                    for q in (1, 2):
                        d = DV.do(lambda e, U=U, C=C, ch=ch, q=q: e.scalar_tensor_tensor(
                            C[:], U[:, 2 + q:2 + q + T], prm("fw", ch * 3 + q), C[:], ALU.mult, ALU.add), d)
                    up_free[n] = [d]
                    if half == 0:
                        d = AC.do(lambda e, C=C: e.activation(C[:], C[:], ACT.Silu), d)
                    ab_.append((d, C, n))
                (ta, Ca, na), (tb_, Cb, nb_) = ab_
                d = DV.do(lambda e, Ca=Ca, Cb=Cb: e.tensor_tensor(Ca[:], Ca[:], Cb[:], ALU.mult), ta, tb_)
                mid[j - a0] = parts(Ca[:], j - a0, X2H, X2L, d, m_free)
                uc_free[na] = list(mid[j - a0])
                uc_free[nb_] = [d]
            nk = b0 - a0
            for m in range(8):
                i, b, w = bank()
                t = proj_fm("wdn", [b], X2, mid, nk, w)
                y_evac(m, b, i, t, part == 0, part == 2, ys)
            m_free = [PE.last()]
        xt_free = [PE.last()]
        hts, xts, t_rc, t_rb = boundary(ys, ("norm_g", 40), hts, [(("rpre", 0), XH, XL, xt_free)])
        xt = xts[0]
        end_m = [e_.last() for e_ in engines]
        pf.close()
        phase(0)
        for e_ in engines:
            e_.next_phase()

        pr = ExitStack()
        CS = alloc(pr, "cs", [128, 2, T])
        DD = alloc(pr, "dd", [128, T])
        QR = alloc(pr, "qr", [128, 2, T])
        KR = alloc(pr, "kr", [128, 2, T])
        TM = [alloc(pr, f"tm{i}", [128, T]) for i in range(3)]
        SC = alloc(pr, "sc", [128, 1280])
        VR = alloc(pr, "vr", [128, NB, T])
        GR = alloc(pr, "gr", [128, NB, T])
        BN = alloc(pr, "bn", [128, NB, 10])
        SOFF = [0, 512, 896, 1152]
        t_cs = load("cs", CS[:], A["rope"], end_m)
        tm_free = [[], [], []]
        free = {"qk": [], "v": [], "sc": [], "g": [], "dd": [], "bn": []}
        o_r = [None] * 8
        x2_free = [[PE.last()]]

        def rot(dst, ops):
            (i1, b1, t1), (i2, b2, t2) = ops
            a = DV.do(lambda e: e.tensor_tensor(TM[0][:], b1[:], RB[:], ALU.mult), t1, t_rb, tm_free[0])
            bank_free[i1] = [a]
            c = DV.do(lambda e: e.tensor_tensor(TM[1][:], b2[:], RB[:], ALU.mult), t2, tm_free[1])
            bank_free[i2] = [c]
            cos, sin = CS[:, 0, :], CS[:, 1, :]
            d1 = DV.do(lambda e: e.tensor_tensor(dst[:, 0, :], TM[0][:], cos, ALU.mult), a, t_cs, free["qk"])
            d2 = DV.do(lambda e: e.tensor_tensor(TM[2][:], TM[1][:], sin, ALU.mult), c, tm_free[2])
            d3 = DV.do(lambda e: e.tensor_tensor(dst[:, 0, :], dst[:, 0, :], TM[2][:], ALU.subtract), d1, d2)
            d4 = DV.do(lambda e: e.tensor_tensor(dst[:, 1, :], TM[0][:], sin, ALU.mult), a)
            d5 = DV.do(lambda e: e.tensor_tensor(TM[2][:], TM[1][:], cos, ALU.mult), d3)
            d6 = DV.do(lambda e: e.tensor_tensor(dst[:, 1, :], dst[:, 1, :], TM[2][:], ALU.add), d4, d5)
            tm_free[0] = [d4]
            tm_free[1] = [d5]
            tm_free[2] = [d6]
            return [d3, d6]

        def retain(h, qt, kt, vt, gt, t_dd):
            sc = []
            for s in range(NB):
                n = (4 - s) * 128
                i, b, w = bank((4, 5))
                for d_ in range(2):
                    t = mm(b[:, 0:n], KR[:, d_, s * 128:s * 128 + 128], QR[:, d_, s * 128:T], d_ == 0, d_ == 1, w, qt,
                           kt)
                sc.append(DV.do(lambda e, s=s, n=n, b=b: e.tensor_tensor(SC[:, SOFF[s]:SOFF[s] + n], b[:, 0:n],
                                                                         DD[:, 0:n], ALU.mult), t, t_dd,
                                free["sc"]))
                bank_free[i] = [sc[-1]]
                yield
            free["qk"] = [t]
            free["dd"] = [sc[-1]]
            while gt[0] is None:
                yield
            gg = []
            for tb in range(NB):
                i, b, w = bank((6, 7))
                for s in range(tb + 1):
                    t = mm(b[:], SC[:, SOFF[s] + (tb - s) * 128:SOFF[s] + (tb - s) * 128 + 128], VR[:, s, :], s == 0,
                           s == tb, w, sc, vt[s])
                s6, ag, rs = BN[:, tb, 0:6], BN[:, tb, 6:8], BN[:, tb, 8:9]
                d = DV.do(lambda e, b=b, s6=s6: e.bn_stats(s6, b[:]), t, free["bn"])
                d = DV.do(lambda e, s6=s6, ag=ag: e.bn_aggr(ag, s6), d)
                d = DV.do(lambda e, tb=tb: e.tensor_scalar(BN[:, tb, 9:10], BN[:, tb, 7:8], EPS, None, ALU.add), d)
                g = GP.do(lambda e, tb=tb, rs=rs: e.tensor_tensor(rs, BN[:, tb, 9:10], NH[:, 0:1], ALU.pow), d)
                yield
                c = DV.do(lambda e, tb=tb, b=b, rs=rs: e.tensor_scalar(
                    SQB[tb % 2][:], b[:], BN[:, tb, 6:7], rs, ALU.subtract, ALU.mult), g, d, sqb_free[tb % 2])
                bank_free[i] = [c]
                c = DV.do(lambda e, tb=tb: e.tensor_tensor(GR[:, tb, :], GR[:, tb, :], SQB[tb % 2][:], ALU.mult), c,
                          gt[tb])
                sqb_free[tb % 2] = [c]
                gg.append(c)
            free["v"] = [t]
            free["sc"] = [t]
            free["bn"] = [gg[-1]]
            yield
            for et in range(4):
                i, b, w = bank((4, 5))
                for tb in range(NB):
                    t = PE.do(lambda e, tb=tb, et=et, b=b: e.transpose(
                        b[:, tb * 128:tb * 128 + 128], GR[:, tb, et * 128:et * 128 + 128], IDN[:]), w, gg[tb])
                kk = (h % 2) * 4 + et
                o_r[kk] = parts(b[:], kk, X2H, X2L, t, x2_free[0])
                bank_free[i] = list(o_r[kk])
                if et % 2:
                    yield
            free["g"] = [t]

        SQB = [alloc(pr, f"sqb{i}", [128, T]) for i in range(2)]
        sqb_free = [[], []]
        ys = {"t": [None] * 8}
        for h in range(4):
            ops = []
            for j in range(2):
                two = []
                for d_ in range(2):
                    i, b, w = bank()
                    two.append((i, b, proj_fm("rqk", [b], (XH, XL), xt, 8, w)))
                if j == 0:
                    qt = rot(QR, two)
                else:
                    kt = rot(KR, two)
            drain()
            t_dd = load("dd", DD[:], A["rdec"][h], free["dd"], end_m)
            res = []
            for j, nm in enumerate(("rv", "rg")):
                bb = [bank() for _ in range(4)]
                t = proj_tm(nm, [x[1] for x in bb], (XH, XL), xt, [x[2] for x in bb])
                r_ = []
                for tb in range(NB):
                    i, b, w = bb[tb]
                    if j == 0:
                        a = AC.do(lambda e, tb=tb, b=b: e.activation(VR[:, tb, :], b[:], ACT.Copy,
                                                                     scale=RC[:, tb:tb + 1]), t, t_rc, free["v"])
                    else:
                        a = AC.do(lambda e, tb=tb, b=b: e.activation(GR[:, tb, :], b[:], ACT.Silu,
                                                                     scale=RC[:, tb:tb + 1]), t, t_rc, free["g"])
                    bank_free[i] = [a]
                    r_.append(a)
                res.append(r_)
                if j == 0:
                    gt = [None] * 4
                    fills.append(retain(h, qt, kt, r_, gt, t_dd))
                else:
                    for tb in range(NB):
                        gt[tb] = r_[tb]
            if h % 2:
                drain()
                for m in range(8):
                    i, b, w = bank()
                    t = proj_fm("rout", [b], X2, o_r, 8, w)
                    y_evac(m, b, i, t, h == 1, h == 3, ys)
                x2_free[0] = [PE.last()]
        xt_free = [PE.last()]
        hts, xts, t_rc, t_rb = boundary(ys, ("rpost", 0), hts, [(("kvn", 0), XH, XL, xt_free),
                                                               (("spre", 0), X2H, X2L, xt_free)])
        xk_t, xs_t = xts
        end_m = [e_.last() for e_ in engines]
        pr.close()
        phase(0)
        for e_ in engines:
            e_.next_phase()

        sbs = ExitStack()
        MH = alloc(sbs, "mh", [128, 4, T], F32R)
        ML = alloc(sbs, "ml", [128, 4, T], F32R)
        KS = alloc(sbs, "ks", [128, 2, T])
        QS = alloc(sbs, "qs", [128, 2, T])
        VS, GS = QK0, ACC
        ZZ = alloc(sbs, "zz", [128, 1280])
        SP = alloc(sbs, "sp", [128, 1280])
        BIG = alloc(sbs, "big", [128, 128])
        LOW = alloc(sbs, "low", [128, 128])
        t_big = load("big", BIG[:], A["sbc"][0], end_m)
        t_low = load("big", LOW[:], A["sbc"][1])
        free = {"k": [], "q": [], "v": [], "g": [[], [], [], []], "z": [], "sp": []}
        m_free = [[]]
        o_s = [None] * 4
        AC.q.append(("i", lambda e: e.preload_act_table_set("natural_log_exp_and_others"), None))

        sb = {"z": 0, "busy": False}

        def stick(h, kt, qt, vt, gt):
            zt = []
            for s in range(NB):
                n = (4 - s) * 128
                i, b, w = bank((4, 5))
                t = mm(b[:, 0:n], KS[:, h, s * 128:s * 128 + 128], QS[:, h, s * 128:T], True, True, w, kt, qt)
                o = SOFF[s]
                d = DV.do(lambda e, o=o, b=b: e.tensor_tensor(ZZ[:, o:o + 128], b[:, 0:128], BIG[:], ALU.min), t,
                          t_big, free["z"])
                zt.append(d)
                if n > 128:
                    a = AC.do(lambda e, o=o, n=n, b=b: e.activation(ZZ[:, o + 128:o + n], b[:, 128:n], ACT.Copy), t,
                              free["z"], d)
                    zt.append(a)
                    bank_free[i] = [d, a]
                else:
                    bank_free[i] = [d]
                if s % 2:
                    yield
            if h:
                free["k"] = [t]
            sb["z"] += 1
            a = AC.do(lambda e: e.activation(SP[:], ZZ[:], ACT.Abs), zt, free["sp"])
            a = AC.do(lambda e: e.activation(SP[:], SP[:], ACT.Exp, scale=-1.0), a)
            a = AC.do(lambda e: e.activation(SP[:], SP[:], ACT.Ln, bias=1.0), a)
            sp = DV.do(lambda e: e.scalar_tensor_tensor(SP[:], ZZ[:], 0.0, SP[:], ALU.max, ALU.add), a, zt)
            yield
            wt = []
            for s in range(NB):
                n = (4 - s) * 128
                i, b, w = bank((4, 5))
                for j in range(s, NB):
                    m = (4 - j) * 128
                    t = mm(b[:, n - m:n], LOW[:] if j == s else ONE[:], SP[:, SOFF[j]:SOFF[j] + m], j == s, j == 3, w,
                           sp, t_low)
                o = SOFF[s]
                d = DV.do(lambda e, o=o, n=n, b=b: e.tensor_tensor(ZZ[:, o:o + n], ZZ[:, o:o + n], b[:, 0:n],
                                                                   ALU.subtract), t, sp)
                bank_free[i] = [d]
                wt.append(AC.do(lambda e, o=o, n=n: e.activation(ZZ[:, o:o + n], ZZ[:, o:o + n], ACT.Exp), d))
                if s % 2:
                    yield
            free["sp"] = [t]
            while sb["busy"]:
                yield
            for et in range(2):
                i, b, w = bank((6, 7))
                for s in range(NB):
                    n = (4 - s) * 128
                    t = mm(b[:, T - n:T], VS[:, s, h * 256 + et * 128:h * 256 + et * 128 + 128],
                           ZZ[:, SOFF[s]:SOFF[s] + n], s == 0, s == 3, w, wt[s], vt[s])
                kk = 2 * h + et
                d = DV.do(lambda e, kk=kk, b=b: e.tensor_tensor(GS[:, kk, :], GS[:, kk, :], b[:], ALU.mult), t,
                          gt[kk])
                bank_free[i] = [d]
                o_s[kk] = parts(GS[:, kk, :], kk, MH, ML, d, m_free[0])
                free["g"][kk] = list(o_s[kk])
                yield
            free["z"] = [t]
            if h:
                free["v"] = [t]

        ys = {"t": [None] * 8}

        def sout(part):
            for mp in range(4):
                bb = [bank() for _ in range(2)]
                t = proj_fm("sout", [x[1] for x in bb], (MH, ML), o_s, 4, [x[2] for x in bb], mt=2)
                for m in range(2):
                    i, b, w = bb[m]
                    y_evac(2 * mp + m, b, i, t, part == 0, part == 3, ys)
            m_free[0] = [PE.last()]

        XS, XK = (X2H, X2L), (XH, XL)
        for p in range(4):
            bb = []
            for nm, XX, tx in (("sk", XK, xk_t), ("sq", XS, xs_t)):
                for h in range(2):
                    i, b, w = bank()
                    bb.append((i, b, proj_fm(nm, [b], XX, tx, 8, w)))
            while p and sb["z"] < 2 * p:
                tick()
            kt, qt, gt = [], [], [None] * 4
            for n, (i, b, t) in enumerate(bb):
                h = n % 2
                if n < 2:
                    kt.append(DV.do(lambda e, b=b, h=h: e.tensor_tensor(KS[:, h, :], b[:], RB[:], ALU.mult), t, t_rb,
                                    free["k"]))
                    bank_free[i] = kt[-1:]
                else:
                    qt.append(DV.do(lambda e, b=b, h=h: e.scalar_tensor_tensor(
                        QS[:, h, :], b[:], 128.0 ** -0.5, RB[:], ALU.mult, ALU.mult), t))
                    bank_free[i] = qt[-1:]
            bb = [bank() for _ in range(4)]
            t = proj_tm("sv", [x[1] for x in bb], XK, xk_t, [x[2] for x in bb])
            drain()
            vt = []
            for tb in range(NB):
                i, b, w = bb[tb]
                vt.append(AC.do(lambda e, tb=tb, b=b: e.activation(VS[:, tb, :], b[:], ACT.Copy,
                                                                   scale=RC[:, tb:tb + 1]), t, t_rc, free["v"]))
                bank_free[i] = [vt[-1]]
            for kk in range(4):
                i, b, w = bank()
                t = proj_fm("sg", [b], XS, xs_t, 8, w)
                d = DV.do(lambda e, kk=kk, b=b: e.tensor_tensor(GS[:, kk, :], b[:], RB[:], ALU.mult), t,
                          free["g"][kk])
                bank_free[i] = [d]
                gt[kk] = AC.do(lambda e, kk=kk: e.activation(GS[:, kk, :], GS[:, kk, :], ACT.Silu), d)
            fills.append(stick(0, kt, qt, vt, gt))
            fills.append(stick(1, kt, qt, vt, gt))
            if p:
                sb["busy"] = True
                sout(p - 1)
                sb["busy"] = False
        drain()
        sout(3)
        hts, _, _, _ = boundary(ys, ("spost", 0), hts, [])
        osrc = out.rearrange("(k p) t -> p k t", p=128)
        ot = [load(f"h{i}", osrc[:, 2 * i:2 * i + 2, :], H[:, 2 * i:2 * i + 2, :], hts[2 * i], hts[2 * i + 1])
              for i in range(4)]
        SY.wait(*ot)
        sbs.close()
        ph.close()
        keepA.close()

        block = root.enter_context(nc.Block())

        @block.sync
        def _(e):
            for kind, a, b in SY.q:
                if kind == "w":
                    e.wait_ge(a, b)
                else:
                    e.dma_start(a[0], a[1]).then_inc(b, 16)

        @block.tensor
        def _(e):
            PE.emit(e)

        @block.scalar
        def _(e):
            AC.emit(e)

        @block.vector
        def _(e):
            DV.emit(e)

        @block.gpsimd
        def _(e):
            GP.emit(e)


def constants():
    i = np.arange(128)
    p, c = i[:, None], i[None, :]
    same = (p // 64) == (c // 64)
    m = {"ident": p == c, "ones": np.ones((128, 128), bool), "tri": same & (p <= c), "blk": same,
         "mc": same & (p <= c), "ms": same & (p < c), "m1t": (p // 2 == c // 2) & (p < c)}
    for s in (2, 4, 8, 16, 32):
        m[f"m{s}"] = (p // (2 * s) == c // (2 * s)) & ((p // s) % 2 == 1) & ((c // s) % 2 == 0)
    cst = np.stack([m[n].astype(np.float32) for n in CST])
    half = 128
    inv = (1.0 / (np.float32(10000.0) ** (np.arange(half, dtype=np.float32) / np.float32(half)))).astype(np.float32)
    ang = (np.arange(T, dtype=np.float32)[None, :] * inv[:, None]).astype(np.float32)
    rope = np.stack([np.cos(ang.astype(np.float64)), np.sin(ang.astype(np.float64))], 1).astype(np.float32)
    rd = []
    for h in range(4):
        lg = np.log1p(-np.exp2(-5.0 - h))
        diff = np.arange(T)[None, :] - p
        rd.append(np.where(diff >= 0, np.exp(lg * np.maximum(diff, 0)), 0.0) / 16.0)
    rdec = np.stack(rd).astype(np.float32)
    sbc = np.stack([np.where(p < c, np.float32(3e38), np.float32(-30000.0)), (p >= c).astype(np.float32)])
    return {"cst": cst, "rope": np.ascontiguousarray(rope), "rdec": rdec, "sbc": sbc.astype(np.float32)}


def cols(v):
    v = np.asarray(v)
    return v.reshape(-1, 128).T


def fm(w, nk=8):
    K, N = w.shape
    return w.reshape(K // 128 // nk, nk, 128, N // 128, 128).transpose(0, 3, 2, 1, 4).reshape(-1, 128, nk * 128)


def tm(w):
    K, N = w.shape
    return w.reshape(K // 256, 2, 128, N // 512, 512).transpose(3, 0, 2, 1, 4).reshape(-1, 128, 1024)


def kernel(**inputs):
    import concourse.bacc as _bacc
    from concourse.bass_utils import run_bass_kernel_spmd as _run

    I = {k: np.asarray(v) for k, v in inputs.items()}
    w_in = I["w_in"][0]
    gw = I["gdn_conv_w"][0]
    P = np.concatenate([
        cols(I["norm_g"][0]), cols(I["mem_norm_g"][0]),
        gw.reshape(4, 12, 128).transpose(2, 1, 0).reshape(128, 48), cols(I["gdn_norm_g"][0]),
        I["cfm_dw_w"][0].reshape(31, 4, 128).transpose(2, 1, 0).reshape(128, 124),
        cols(I["cfm_dw_b"][0]), cols(I["cfm_ln_g"][0]), cols(I["cfm_ln_b"][0]),
        I["ffn_conv_w"][0].reshape(3, 44, 128).transpose(2, 1, 0).reshape(128, 132), cols(I["ffn_conv_b"][0]),
        cols(I["ret_norm_pre_2"][0]), cols(I["ret_norm_post_2"][0]), cols(I["kv_norm_2"]),
        cols(I["sb_norm_pre_2"][0]), cols(I["sb_norm_post_2"][0]),
        np.broadcast_to(I["gdn_a_log"][0][None, :], (128, 4)), np.broadcast_to(I["gdn_dt_bias"][0][None, :], (128, 4)),
    ], axis=1)
    dn = I["ffn_w_down"][0]
    dn2 = fm(dn[2048:], 6)
    wdn = np.concatenate([fm(dn[:2048]), np.pad(dn2, ((0, 0), (0, 0), (0, 256)))])
    rin = I["ret_w_in_2"][0]
    rqk = np.concatenate([rin[:, j * 1024 + h * 256:j * 1024 + h * 256 + 256] for h in range(4) for j in range(2)],
                         axis=1)
    kv = I["w_kv_2"]
    sin_ = I["sb_w_in_2"][0]
    so = I["sb_w_out_2"][0]
    sout = so.reshape(4, 4, 128, 4, 256).transpose(0, 3, 2, 1, 4).reshape(16, 128, 1024)
    arrays = {
        "xT": I["x"][0].T, "memT": I["mem"][0].T, "prm": P,
        "wab": w_in[:, 2048:2056].reshape(8, 128, 8).transpose(1, 0, 2).reshape(128, 64),
        "wcfm": fm(w_in[:, 2056:3080]), "wqkv": fm(w_in[:, 0:1536]), "wgate": fm(w_in[:, 1536:2048]),
        "wmk": fm(I["xa_w_kv"][0][:, :1024]), "wmv": tm(I["xa_w_kv"][0][:, 1024:]),
        "wout": fm(I["w_out"][0]), "wxq": fm(I["xa_w_q"][0]), "wxo": fm(I["xa_w_o"][0]),
        "wup": fm(I["ffn_w_up"][0]), "wdn": wdn, "rqk": fm(rqk), "rv": tm(rin[:, 2048:4096]),
        "rg": tm(rin[:, 4096:]), "rout": fm(I["ret_w_out_2"][0]), "sk": fm(kv[:, :1024]), "sv": tm(kv[:, 1024:]),
        "sq": fm(sin_[:, :1024]), "sg": fm(sin_[:, 1024:]), "sout": sout,
    }
    arrays.update(constants())
    nc = _bacc.Bacc("TRN2", target_bir_lowering=False, num_devices=1)
    arrs, A = {}, {}
    for n, a in arrays.items():
        a = np.ascontiguousarray(a)
        arrs["in_" + n] = a
        A[n] = nc.dram_tensor("in_" + n, a.shape, mybir.dt.from_np(a.dtype), kind="ExternalInput").ap()
    out = nc.dram_tensor("out_0", (1024, T), F32, kind="ExternalOutput").ap()
    program(nc, A, out)
    r = _run(nc, [arrs], core_ids=[0])
    return np.ascontiguousarray(r.results[0]["out_0"].T)[None]
```

```python
from contextlib import ExitStack

import numpy as np

import concourse.bass as bass
from concourse import mybir

F32 = mybir.dt.float32
F32R = mybir.dt.float32r
ALU = mybir.AluOpType
ACT = mybir.ActivationFunctionType
AXX = mybir.AxisListType.X

T = 512
NB = 4
EPS = 1e-6
NRAW = 3
NSPL = 4
SLAB = 1024

PCOL = {}
_at = 0
for _n, _w in (("norm_g", 48), ("mem_g", 8), ("gconv", 48), ("gn", 1), ("cw", 124), ("cb", 4), ("lg", 4), ("lb", 4),
               ("fw", 132), ("fb", 44), ("rpre", 8), ("rpost", 8), ("kvn", 8), ("spre", 8), ("spost", 8),
               ("alog", 4), ("dtb", 4)):
    PCOL[_n] = _at
    _at += _w
NPRM = _at

CST = ["ident", "ones", "tri", "blk"]
CSH = ["id64", "mc", "ms", "m1t", "m2t", "m4t", "m8t", "m16t", "m32t"]


class Engine:

    def __init__(self, sems):
        self.sems = sems
        self.phase = 0
        self.n = 0
        self.q = []
        self.seen = {}

    def wait(self, *toks):
        for t in toks:
            if t is None:
                continue
            if isinstance(t, list):
                self.wait(*t)
                continue
            s, v = t
            if self.seen.get(s.name, 0) < v:
                self.seen[s.name] = v
                self.q.append(("w", s, v))

    def do(self, fn, *toks, inc=True):
        self.wait(*toks)
        if not inc:
            self.q.append(("i", fn, None))
            return None
        self.n += 1
        s = self.sems[self.phase]
        self.q.append(("i", fn, s))
        return (s, self.n)

    def last(self):
        return (self.sems[self.phase], self.n) if self.n else None

    def next_phase(self):
        self.phase += 1
        self.n = 0

    def emit(self, e):
        for kind, a, b in self.q:
            if kind == "w":
                e.wait_ge(a, b)
            else:
                ins = a(e)
                if b is not None:
                    ins.then_inc(b, 1)


class Banks(list):

    def __init__(self, x):
        super().__init__(x)
        self.held = [False] * len(x)

    def __setitem__(self, i, toks):
        self.held[i] = False
        super().__setitem__(i, toks)


def bc(ap, n):
    return ap.unsqueeze(2).broadcast_to([ap.shape[0], ap.shape[1], n])


def bm(ap, n):
    return ap.unsqueeze(1).broadcast_to([ap.shape[0], n, ap.shape[1]])


def weight_order():
    o = []
    for p in range(2):
        for j in range(3):
            for h in range(2):
                if (p, j, h) == (1, 2, 0):
                    for c in range(4):
                        o += [("wcfm", 4 + c), ("wcfm", c)]
                o.append(("wqkv", j * 4 + 2 * p + h))
    o += [("wmk", i) for i in range(8)]
    o += [("wgate", i) for i in range(4)]
    o += [("wmv", i) for i in range(8)]
    o += [("wout", i) for i in range(8)]
    o += [("wxq", i) for i in range(8)]
    o += [("wxo", i) for i in range(8)]
    for a, b in ((0, 8), (8, 16), (16, 22)):
        for j in range(a, b):
            o += [("wup", j), ("wup", 22 + j)]
        o += [("wdn", (a // 8) * 8 + i) for i in range(8)]
    for h in range(4):
        o += [("rqk", 4 * h + i) for i in range(4)]
        o += [("rv", 4 * h + i) for i in range(4)]
        o += [("rg", 4 * h + i) for i in range(4)]
        if h % 2:
            o += [("rout", (h // 2) * 8 + i) for i in range(8)]
    for p in range(4):
        o += [("sk", 2 * p), ("sk", 2 * p + 1), ("sq", 2 * p), ("sq", 2 * p + 1)]
        o += [("sv", 4 * p + i) for i in range(4)]
        o += [("sg", 4 * p + i) for i in range(4)]
        if p:
            o += [("sout", 4 * (p - 1) + i) for i in range(4)]
    o += [("sout", 12 + i) for i in range(4)]
    return o


def program(nc, A, out):
    root = ExitStack()
    with root:
        def sem(n):
            return root.enter_context(nc.semaphore(n))

        NPH = 6
        PE, AC, DV, GP = (Engine([sem(f"s_{n}{i}") for i in range(NPH)]) for n in ("pe", "act", "dve", "pool"))
        SY = Engine([sem("s_sy")])
        engines = (PE, AC, DV, GP)

        def alloc(stack, name, shape, dt=F32):
            return stack.enter_context(nc.sbuf_tensor(name, shape, dt))

        banks = [root.enter_context(nc.psum_tensor(f"ps{i}", [128, 512], F32)) for i in range(8)]
        bank_free = Banks([[] for _ in range(8)])
        bank_at = {}

        def bank(pool=(0, 1, 2, 3)):
            bank_at[pool] = bank_at.get(pool, -1) + 1
            i = pool[bank_at[pool] % len(pool)]
            assert not bank_free.held[i], i
            bank_free.held[i] = True
            return i, banks[i], bank_free[i]

        dma_sems = {}

        def load(name, dst, src, *after, eng=SY):
            s = dma_sems.get(name)
            if s is None:
                s = dma_sems[name] = [sem("d_" + name), 0]
            s[1] += 16
            sm, v = s[0], s[1]
            eng.wait(*after)
            eng.q.append(("d", (dst, src), sm))
            return (sm, v)

        RAW = [alloc(root, f"raw{i}", [128, SLAB]) for i in range(NRAW)]
        SH = [alloc(root, f"sh{i}", [128, SLAB], F32R) for i in range(NSPL)]
        SL = [alloc(root, f"sl{i}", [128, SLAB], F32R) for i in range(NSPL)]
        XH = alloc(root, "xh", [128, 8, T], F32R)
        XL = alloc(root, "xl", [128, 8, T], F32R)
        X2H = alloc(root, "x2h", [128, 8, T], F32R)
        X2L = alloc(root, "x2l", [128, 8, T], F32R)
        PRM = alloc(root, "prm", [128, NPRM])
        IDN = alloc(root, "idn", [128, 128])
        ONE = alloc(root, "one", [128, 128])
        RB = alloc(root, "rb", [128, T])
        RC = alloc(root, "rc", [128, 16])
        MSQ = alloc(root, "msq", [128, 16])
        NH = alloc(root, "nh", [128, 16])
        SQ = [alloc(root, f"sq{i}", [128, T]) for i in range(2)]
        DG = alloc(root, "dg", [128, T])

        def prm(n, i=0):
            return PRM[:, PCOL[n] + i:PCOL[n] + i + 1]

        t_prm = load("prm", PRM[:], A["prm"])
        t_cst = load("cst", IDN[:], A["cst"][0])
        t_cst = load("cst", ONE[:], A["cst"][1])
        t_nh = GP.do(lambda e: e.memset(NH[:], -0.5))

        order = weight_order()
        raw_free = [[] for _ in range(NRAW)]
        spl_free = [None] * NSPL
        raw_tok = {}
        spl_tok = {}
        st = {"dma": 0, "hi": 0, "lo": 0, "use": 0}

        def send(j):
            n, i = order[j]
            raw_tok[j] = load(f"w{j % NRAW}", RAW[j % NRAW][:], A[n][i], raw_free[j % NRAW])

        def sends():
            while st["dma"] < min(len(order), st["lo"] + NRAW):
                send(st["dma"])
                st["dma"] += 1

        def split_hi():
            j = st["hi"]
            r, s = j % NRAW, j % NSPL
            spl_tok[j] = [AC.do(lambda e: e.activation(SH[s][:], RAW[r][:], ACT.Copy), raw_tok[j], spl_free[s])]
            st["hi"] += 1

        def split_lo():
            j = st["lo"]
            r, s = j % NRAW, j % NSPL
            spl_tok[j].append(DV.do(lambda e: e.tensor_tensor(SL[s][:], RAW[r][:], SH[s][:].bitcast(F32),
                                                              ALU.subtract), spl_tok[j], raw_tok[j], spl_free[s]))
            raw_free[r] = list(spl_tok[j])
            st["lo"] += 1
            sends()

        def pump():
            top = min(len(order), st["use"] + NSPL)
            sends()
            while st["hi"] < top:
                while st["lo"] < st["hi"]:
                    split_lo()
                split_hi()

        def take(name, cols, off=0):
            j = st["use"] + off
            assert order[j][0] == name, (order[j], name)
            sends()
            while st["lo"] <= j:
                if st["hi"] == st["lo"]:
                    split_hi()
                split_lo()
            s = j % NSPL
            v = [x[s][:].rearrange("p (k c) -> p k c", c=cols) for x in (SH, SL)]
            return v[0], v[1], spl_tok[j], s

        def done(s, tok):
            spl_free[s] = tok
            st["use"] += 1
            pump()

        fills = []

        def tick():
            while fills:
                try:
                    next(fills[0])
                    return
                except StopIteration:
                    fills.pop(0)

        def drain():
            while fills:
                tick()

        small = []

        def trickle(n=1):
            for _ in range(n):
                if small:
                    small.pop(0)()

        def mm3(dst, ah, al, bh, bl, start, stop, *w, inc=False):
            PE.do(lambda e: e.matmul(dst, ah, bh, start=start, stop=False, skip_group_check=True), *w, inc=False)
            PE.do(lambda e: e.matmul(dst, ah, bl, start=False, stop=False, skip_group_check=True), inc=False)
            return PE.do(lambda e: e.matmul(dst, al, bh, start=False, stop=stop, skip_group_check=True), inc=stop or inc)

        def mm(dst, a, b, start, stop, *w, inc=None):
            return PE.do(lambda e: e.matmul(dst, a, b, start=start, stop=stop, skip_group_check=True), *w,
                         inc=stop if inc is None else inc)

        grain = {"t": 2, "s": 2}

        def pause(i, n):
            if (i + 1) * grain["t"] // n > i * grain["t"] // n:
                tick()
                trickle(grain["s"])

        def proj_fm(name, dst, X, xt, nk, bw, N=T, mt=1, ks=None):
            wh, wl, wt, s = take(name, 128 * mt)
            ks = ks or range(nk)
            for m in range(mt):
                for n, k in enumerate(ks):
                    c = slice(m * 128, m * 128 + 128)
                    t = mm3(dst[m][:, 0:N], wh[:, k, c], wl[:, k, c], X[0][:, k, 0:N], X[1][:, k, 0:N],
                            n == 0, n == nk - 1, wt, xt[k], bw)
                    pause(m * nk + n, mt * nk)
            done(s, t)
            return t

        def group(items, nk, N=T, mt=1, ks=None, pre=None, post=None):
            g = [take(it[0], 128 * mt, off) for off, it in enumerate(items)]
            out_t = [None] * len(items)
            for n, k in enumerate(ks or range(nk)):
                if pre:
                    pre(k)
                for i, (name, dst, X, xt, bw) in enumerate(items):
                    wh, wl, wt, s = g[i]
                    for m in range(mt):
                        c = slice(m * 128, m * 128 + 128)
                        out_t[i] = mm3(dst[m][:, 0:N], wh[:, k, c], wl[:, k, c], X[0][:, k, 0:N], X[1][:, k, 0:N],
                                       n == 0, n == nk - 1, wt, xt[k], bw)
                if post:
                    post(k)
                if n == 2:
                    pump()
                tick()
                trickle(grain["s"])
            for i in range(len(items)):
                done(g[i][3], out_t[i])
            return out_t

        def stream(items, evac, nk=8, ng=3, ks=None, pre=None, post=None, fin=None, mt=1):
            def banks_of():
                return [bank() for _ in range(mt)]
            bb = [banks_of() for _ in range(ng)]
            tt = group([(nm, [x[1] for x in b], X, xt, [x[2] for x in b]) for (nm, X, xt), b in zip(items, bb)],
                       nk, mt=mt, ks=ks, pre=pre, post=post)
            rest = list(items[ng:])
            held = list(zip(bb, tt))
            if fin:
                fin[0]()
                if rest and (ng + 1) * mt <= 4:
                    nm, X, xt = rest.pop(0)
                    b = banks_of()
                    held.append((b, proj_fm(nm, [x[1] for x in b], X, xt, nk, [x[2] for x in b], mt=mt)))
                fin[1]()
            for n, (b, t) in enumerate(held):
                evac(n, b, t)
            for n, (nm, X, xt) in enumerate(rest):
                b = banks_of()
                t = proj_fm(nm, [x[1] for x in b], X, xt, nk, [x[2] for x in b], mt=mt)
                evac(len(held) + n, b, t)

        def proj_tm(name, dst, X, xt, bw, nb=NB):
            out_t = []
            for g in range(4):
                wh, wl, wt, s = take(name, 512)
                for tb in range(nb):
                    for k in range(2):
                        kk = 2 * g + k
                        c = slice(tb * 128, tb * 128 + 128)
                        t = mm3(dst[tb][:], X[0][:, kk, c], X[1][:, kk, c], wh[:, k, :], wl[:, k, :],
                                kk == 0, kk == 7, wt, xt[kk], bw[tb], inc=(tb == nb - 1 and k == 1))
                    if g == 3:
                        out_t.append(t)
                    pause(tb, nb)
                done(s, t)
            return out_t

        PE.wait(t_cst)
        for e_ in (AC, DV, GP):
            e_.wait(t_prm, t_cst)
        GP.wait(t_nh)
        DV.wait(t_nh)

        sq_free = [None, None]
        sq_at = [0]

        def colsum(src, col0, dst, first, last, N, srct, bw=None):
            i = sq_at[0] % 2
            sq_at[0] += 1
            a = AC.do(lambda e: e.activation(SQ[i][:, 0:N], src, ACT.Square), srct, sq_free[i])

            def sums():
                for tb in range(N // 128):
                    t = mm(dst[:, col0 + tb:col0 + tb + 1], SQ[i][:, tb * 128:tb * 128 + 128], ONE[:, 0:1],
                           first and tb == 0, last, a, bw, inc=(tb == N // 128 - 1))
                sq_free[i] = t
                return t
            return sums

        rc_free = {}

        def rstd(src, n, t, scale, col=0):
            m, r = MSQ[:, col:col + n], RC[:, col:col + n]
            d = DV.do(lambda e: e.tensor_scalar(m, src, scale, EPS, ALU.mult, ALU.add), t, rc_free.get(col))
            g = GP.do(lambda e: e.tensor_tensor(r, m, NH[:, 0:n], ALU.pow), d)
            rc_free[col] = g
            return d, g

        dg_free = [None]

        def diag(col, nb, ct):
            return DV.do(lambda e: e.tensor_tensor(DG[:, 0:nb * 128].rearrange("p (a b) -> p a b", b=128),
                                                   bm(IDN[:], nb), bc(col, 128), ALU.mult), ct, dg_free[0])

        def rows_mm(nb, d, bw, dst):
            t = mm(dst, ONE[:], DG[:, 0:nb * 128], True, True, d, bw)
            dg_free[0] = t
            return t

        def rows(col, nb, ct, bw, dst):
            return rows_mm(nb, diag(col, nb, ct), bw, dst)

        rb_free = [[]]

        def fin_a(bi, bk, t, nb):
            d, g = rstd(bk[:, 0:nb], nb, t, 1.0 / 1024)
            bank_free[bi] = [d]
            return g, diag(RC[:, 0:nb], nb, g)

        def fin_b(d, nb, rb, pool=(6,)):
            i2, b2, w2 = bank(pool)
            t2 = rows_mm(nb, d, w2, b2[:, 0:nb * 128])
            if rb is None:
                return i2, b2, t2
            c = DV.do(lambda e: e.tensor_copy(rb[:, 0:nb * 128], b2[:, 0:nb * 128]), t2, rb_free[0])
            bank_free[i2] = [c]
            return c

        def scaled(src, g, k, XXH, XXL, tk, N=T, free=None):
            a = AC.do(lambda e: e.activation(XXH[:, k, 0:N], src, ACT.Copy, scale=g), tk, free)
            d = DV.do(lambda e: e.scalar_tensor_tensor(XXL[:, k, 0:N], src, g, XXH[:, k, 0:N].bitcast(F32),
                                                       ALU.mult, ALU.subtract), a, tk, free)
            return [a, d]

        late = []

        def flush_late():
            while late:
                late.pop(0)()

        def parts(src, k, XXH, XXL, tk, free=None, late=None):
            toks = [AC.do(lambda e: e.activation(XXH[:, k, :], src, ACT.Copy), tk, free)]

            def low():
                toks.append(DV.do(lambda e: e.tensor_tensor(XXL[:, k, :], src, XXH[:, k, :].bitcast(F32),
                                                            ALU.subtract), toks, tk, free))
            if late is None:
                low()
            else:
                late.append(low)
            return toks

        keepA = ExitStack()
        QK0 = alloc(keepA, "qk0", [128, 4, T])
        ACC = alloc(keepA, "acc", [128, 4, T])
        KM = alloc(keepA, "km", [128, 8, 256])
        KQ = KM[:].rearrange("p (a b) m -> p a (b m)", b=2)
        VM = QK0[:].rearrange("p a t -> p (a t)").rearrange("p (b c) -> p b c", b=2)
        ph = ExitStack()
        CP = alloc(ph, "cp", [128, 4, T + 32])
        QK1 = alloc(ph, "qk1", [128, 4, T])
        CM = alloc(ph, "cm", [128, 2, 128])
        CH = alloc(ph, "ch", [128, len(CSH), 64])
        UNIT = {n: alloc(ph, n, [128, w]) for n, w in (("u_bv", 1024), ("u_kbe", 1024), ("u_kd", 1024), ("u_f1", 1024),
                                                       ("u_f2", 1024), ("u_a", 512), ("u_l", 512), ("u_tt", 512))}
        GT = alloc(ph, "gt", [128, 4, T])
        PAD = alloc(ph, "pad", [128, T + 4])
        CA = [alloc(ph, f"ca{i}", [128, T]) for i in range(2)]
        VF = alloc(ph, "vf", [128, T])
        SG = VF
        MRB = CA[0][:, 0:256]
        SS = alloc(ph, "ss", [128, 2, 128])
        SMV = alloc(ph, "smv", [128, 160])
        WAB = alloc(ph, "wab", [128, 64])
        WABH = alloc(ph, "wabh", [128, 64], F32R)
        WABL = alloc(ph, "wabl", [128, 64], F32R)
        LNC = alloc(ph, "lnc", [128, 16])
        OLN = alloc(ph, "oln", [128, 16])
        EG = alloc(ph, "eg", [128, 2, 8])

        xsrc = A["xT"].rearrange("(k p) t -> p k t", p=128)
        def load_x(i):
            return load(f"x{i}", (QK0, ACC)[i // 2][:, 2 * (i % 2):2 * (i % 2) + 2, :], xsrc[:, 2 * i:2 * i + 2, :])

        t_x = [load_x(0)]
        sends()
        t_x += [load_x(i) for i in (1, 2, 3)]
        t_wab = load("wab", WAB[:], A["wab"])
        t_m = load("mem", GT[:].rearrange("p a (b t) -> p (a b) t", t=256),
                   A["memT"].rearrange("(k p) t -> p k t", p=128))
        t_cm = load("cm", CM[:], A["cst"][2:].rearrange("n p c -> p n c"))
        t_ch = load("ch", CH[:], A["csh"])
        cst = {n: CM[:, i, :] for i, n in enumerate(CST[2:])}
        csh = {n: CH[:, i, :] for i, n in enumerate(CSH)}

        zp = [GP.do(lambda e: e.memset(PAD[:, 0:4], 0.0))]
        zp.append(GP.do(lambda e: e.memset(CP[:, :, 0:32], 0.0)))
        zp.append(GP.do(lambda e: e.memset(SS[:], 0.0)))
        t_ss0 = zp[-1]

        def xk(k):
            return (QK0, ACC)[k // 4][:, k % 4, :]

        X = (XH, XL)
        xt = [None] * 8
        sx = {}
        st_b = bank((7,))

        def x_pre(k):
            xt[k] = scaled(xk(k), prm("norm_g", k), k, XH, XL, t_x[k // 2])
            sx[k] = colsum(xk(k), 0, st_b[1], k == 0, k == 7, T, t_x[k // 2], st_b[2])

        def x_post(k):
            sx["t"] = sx[k]()

        def x_fin_a():
            sx["g"], sx["d"] = fin_a(st_b[0], st_b[1], sx["t"], 4)
            x_read.extend([AC.last(), DV.last()])

        def x_fin_b():
            sx["r"] = fin_b(sx["d"], 4, RB)

        x_read = []
        pad_free = [[]]
        ca_at = [0]
        ca_free = [None, None]
        vf_free = [[]]
        unit_free = {}

        def evac_conv(tile, dst, extra, put, i, b, t):
            pi = ca_at[0] % 2
            ca_at[0] += 1
            P, C = PAD, CA[pi]
            d = DV.do(lambda e: e.tensor_tensor(P[:, 4:4 + T], b[:], RB[:], ALU.mult), t, sx["r"], pad_free[0], zp)
            bank_free[i] = [d]
            s_ = {"d": d}

            def tap(j):
                w = prm("gconv", tile * 4 + j)
                if j == 0:
                    s_["d"] = DV.do(lambda e: e.tensor_scalar(C[:], P[:, 1:1 + T], w, None, ALU.mult), s_["d"],
                                    ca_free[pi])
                else:
                    s_["d"] = DV.do(lambda e: e.scalar_tensor_tensor(C[:], P[:, 1 + j:1 + j + T], w, C[:], ALU.mult,
                                                                     ALU.add), s_["d"])
                if j == 3:
                    pad_free[0] = [s_["d"]]
                    a = AC.do(lambda e: e.activation(dst, C[:], ACT.Silu), s_["d"], extra)
                    ca_free[pi] = a
                    put(a)
            for j in range(4):
                tap(j)

        bv_t = [[None, None], [None, None]]
        o_t = [[], []]
        qk_t = [[None] * 4, [None] * 4]
        QKS = (QK0, QK1)

        def v4(x):
            return x.rearrange("p (h b c) -> p h b c", h=2, b=NB)

        u_done = []

        def gdn(p, QK, qk_t, out_t):
            UB, UKB, UKD, F1, F2, UA, UL, UTT = (UNIT[n][:] for n in
                                                 ("u_bv", "u_kbe", "u_kd", "u_f1", "u_f2", "u_a", "u_l", "u_tt"))
            UT, UX = F1[:, 0:512], F1[:, 512:1024]
            LM = [F2[:, 0:512], F2[:, 512:1024]]
            g3 = lambda x: x.rearrange("p (g c) -> p g c", c=64)
            h3 = lambda x, h: x[:, h * T:h * T + T].rearrange("p (b c) -> p b c", c=128)
            hd = lambda x, h: x[:, h * T:h * T + T]
            gch = lambda i, h: sv3(i)[:, :, 2 * p + h]
            RR = (slice(0, 64), slice(64, 128))
            chunks = [(h, tb, par) for h in range(2) for tb in range(NB) for par in range(2)]
            uf = unit_free.get
            bi, bk, bw = bank((4, 5))
            for n in range(4):
                f = colsum(QK[:, n, :], 4 * n, bk, n == 0, True, T, qk_t[n], bw)
                yield
                t = f()
            yield
            d, g = rstd(bk[:, 0:16], 16, t, 1.0)
            bank_free[bi] = [d]
            nt = [None] * 4
            for n in range(4):
                dg = diag(RC[:, 4 * n:4 * n + 4], 4, g)
                yield
                i2, b2, w2 = bank((4, 5))
                t = rows_mm(4, dg, w2, b2[:])
                if n < 2:
                    nt[n] = DV.do(lambda e, n=n, b2=b2: e.scalar_tensor_tensor(
                        QK[:, n, :], QK[:, n, :], 128.0 ** -0.5, b2[:], ALU.mult, ALU.mult), t, qk_t[n])
                else:
                    nt[n] = DV.do(lambda e, n=n, b2=b2: e.tensor_tensor(QK[:, n, :], QK[:, n, :], b2[:], ALU.mult),
                                  t, qk_t[n])
                bank_free[i2] = [nt[n]]
            kb = [None, None]
            ea_ = [None, None]
            dd = []
            for h in range(2):
                dg = diag(gch(3, h), 4, t_gc)
                yield
                i2, b2, w2 = bank((4, 5))
                t = rows_mm(4, dg, w2, b2[:])
                for par in range(2):
                    R = RR[par]
                    dst = g3(UA[R, h * 256:h * 256 + 256])
                    src = b2[R, :].rearrange("p (b q c) -> p b q c", q=2, c=64)[:, :, par, :]
                    d = DV.do(lambda e, R=R, dst=dst, src=src, h=h: e.tensor_tensor(
                        dst, src, bc(gch(3, h)[R], 64), ALU.subtract), t, uf("u_a"))
                    dd.append(d)
                ea_[h] = AC.do(lambda e, h=h, b2=b2: e.activation(hd(F1, h), b2[:], ACT.Exp), t, d, uf("u_f1"), f1_read)
                bank_free[i2] = [ea_[h]]
                dg = diag(gch(2, h), 4, t_beta)
                yield
                i2, b2, w2 = bank((4, 5))
                t = rows_mm(4, dg, w2, b2[:])
                kb[h] = DV.do(lambda e, h=h, b2=b2: e.tensor_tensor(hd(F2, h), QK[:, 2 + h, :], b2[:], ALU.mult),
                              t, nt[2 + h], uf("u_f2"))
                bank_free[i2] = [kb[h]]
            a = AC.do(lambda e: e.activation(UA, UA, ACT.Relu, scale=-1.0), dd)
            a = AC.do(lambda e: e.activation(UA, UA, ACT.Exp, scale=-1.0), a)
            mk = GP.do(lambda e: e.tensor_tensor(g3(UA), g3(UA), bm(csh["mc"], 8), ALU.mult), a, t_ch)
            lm = GP.do(lambda e: e.tensor_tensor(g3(UL), g3(UA), bm(csh["ms"], 8), ALU.mult), mk, uf("u_l"))
            yield
            i3, b3, w3 = bank((4, 5))
            for n, (h, tb, par) in enumerate(chunks):
                c = slice(tb * 128 + par * 64, tb * 128 + par * 64 + 64)
                o = (h * 4 + tb) * 64
                t = mm(b3[RR[par], o:o + 64], QK[:, 2 + h, c], hd(F2, h)[:, c], True, True, kb, w3, nt[2 + h],
                       inc=n == 15)
            lt = DV.do(lambda e, b3=b3: e.tensor_tensor(UL, UL, b3[:], ALU.mult), t, lm)
            bank_free[i3] = [lt]
            kb_read = t
            yield
            d = DV.do(lambda e: e.scalar_tensor_tensor(g3(UTT), g3(UL), -1.0, bm(csh["m1t"], 8), ALU.mult, ALU.mult),
                      lt, uf("u_tt"), t_ch)
            tt = DV.do(lambda e: e.tensor_tensor(g3(UTT), g3(UTT), bm(csh["id64"], 8), ALU.add), d)
            i3, b3, w3 = bank((4, 5))
            for n, (h, tb, par) in enumerate(chunks):
                c = slice(tb * 128 + par * 64, tb * 128 + par * 64 + 64)
                o = (h * 4 + tb) * 64
                t = mm(b3[RR[par], o:o + 64], QK[:, 2 + h, c], QK[:, h, c], True, True, w3, nt[h], inc=n == 15)
            at = DV.do(lambda e, b3=b3: e.tensor_tensor(UA, UA, b3[:], ALU.mult), t, lm)
            bank_free[i3] = [at]
            qe = []
            for h in range(2):
                qe.append(DV.do(lambda e, h=h: e.tensor_tensor(QK[:, h, :], QK[:, h, :], hd(F1, h), ALU.mult),
                                ea_[h], t))
                eg = DV.do(lambda e, h=h: e.tensor_copy(EG[:, h, :], hd(F1, h)[:, 63:T:64]), ea_[h], uf("eg"))
            lmt = [GP.do(lambda e: e.tensor_tensor(g3(LM[0]), g3(UL), bm(csh["m2t"], 8), ALU.mult), lt, kb_read),
                   None]
            yield
            i3, b3, w3 = bank((4, 5))
            for n, (h, tb, par) in enumerate(chunks):
                o = (h * 4 + tb) * 64
                R = RR[par]
                t = mm(b3[R, o:o + 64], UTT[R, o:o + 64], csh["id64"][R, :], True, True, w3, tt, inc=n == 15)
            tl = AC.do(lambda e, b3=b3: e.activation(UT, b3[:], ACT.Copy), t, qe, eg)
            bank_free[i3] = [tl]
            xfree = [qe[1], eg]
            k_tm = []

            def keys(h):
                i3, b3, w3 = bank((4, 5))
                for tb in range(NB):
                    c = slice(tb * 128, tb * 128 + 128)
                    t = PE.do(lambda e, c=c: e.transpose(b3[:, c], QK[:, 2 + h, c], IDN[:]), w3, nt[2 + h])
                b33 = b3[:].rearrange("p (b c) -> p b c", c=128)
                DV.do(lambda e: e.tensor_tensor(h3(UKB, h), b33, bc(gch(6, h), 128), ALU.mult), t, uf("u_kbe"))
                k2 = DV.do(lambda e: e.tensor_tensor(h3(UKD, h), b33, bc(gch(7, h), 128), ALU.mult), t, uf("u_kd"))
                bank_free[i3] = [k2]
                k_tm.append(k2)

            for n_, s in enumerate((2, 4, 8, 16, 32)):
                yield
                if n_ < 2:
                    keys(n_)
                M_ = LM[n_ % 2]
                i3, b3, w3 = bank((4, 5))
                for n, (h, tb, par) in enumerate(chunks):
                    o = (h * 4 + tb) * 64
                    R = RR[par]
                    t = mm(b3[R, o:o + 64], M_[R, o:o + 64], UT[R, o:o + 64], True, True, w3, tl, lmt[n_ % 2],
                           inc=n == 15)
                xx = DV.do(lambda e, b3=b3: e.scalar_tensor_tensor(g3(UX), g3(b3[:]), -1.0, bm(csh["id64"], 8),
                                                                   ALU.mult, ALU.add), t, xfree)
                bank_free[i3] = [xx]
                if s < 32:
                    nm = f"m{2 * s}t"
                    lmt[(n_ + 1) % 2] = GP.do(lambda e, n_=n_, nm=nm: e.tensor_tensor(
                        g3(LM[(n_ + 1) % 2]), g3(UL), bm(csh[nm], 8), ALU.mult), t)
                yield
                i4, b4, w4 = bank((4, 5))
                for n, (h, tb, par) in enumerate(chunks):
                    o = (h * 4 + tb) * 64
                    R = RR[par]
                    t2 = mm(b4[R, o:o + 64], UX[R, o:o + 64], UTT[R, o:o + 64], True, True, w4, xx, tt, inc=n == 15)
                if s < 32:
                    i3, b3, w3 = bank((4, 5))
                    for n, (h, tb, par) in enumerate(chunks):
                        o = (h * 4 + tb) * 64
                        R = RR[par]
                        t2 = mm(b3[R, o:o + 64], UTT[R, o:o + 64], UX[R, o:o + 64], True, True, w3, inc=n == 15)
                tt = DV.do(lambda e, b4=b4: e.tensor_copy(UTT, b4[:]), t2)
                bank_free[i4] = [tt]
                if s < 32:
                    tl = AC.do(lambda e, b3=b3: e.activation(UT, b3[:], ACT.Copy), t2)
                    bank_free[i3] = [tl]
                xfree = [t2]
            yield
            ut = []
            for h in range(2):
                i3, b3, w3 = bank((4, 5))
                for tb in range(NB):
                    for par in range(2):
                        R = RR[par]
                        o = (h * 4 + tb) * 64
                        t = mm(b3[R, tb * 128:tb * 128 + 128], UTT[R, o:o + 64], hd(UB, h)[R, tb * 128:tb * 128 + 128],
                               True, True, w3, tt, bv_t[p][h], inc=tb == 3 and par == 1)
                ut.append(AC.do(lambda e, h=h, b3=b3: e.activation(hd(F1, h), b3[:], ACT.Copy), t, xx))
                bank_free[i3] = [ut[h]]
                yield
            wt = []
            for par in range(2):
                i3, b3, w3 = bank((4, 5))
                R = RR[par]
                for h in range(2):
                    for tb in range(NB):
                        o = (h * 4 + tb) * 64
                        t = mm(b3[:, o:o + 64], hd(UKB, h)[R, tb * 128:tb * 128 + 128], UTT[R, o:o + 64], True, True,
                               w3, k_tm, tt, inc=h == 1 and tb == 3)
                dst = F2.rearrange("p (g q c) -> p g q c", q=2, c=64)[:, :, par, :]
                wt.append(AC.do(lambda e, dst=dst, b3=b3: e.activation(dst, g3(b3[:]), ACT.Copy), t))
                bank_free[i3] = [wt[par]]
                yield
            VN = QK[:, 2:4, :].rearrange("p h (b c) -> p h b c", c=128)
            U4 = v4(F1)
            i4, po, w4 = bank((6,))
            i5, po1, w5 = bank((7,))
            P2 = [po, po1]
            if p:
                z = GP.do(lambda e: e.memset(SS[:], 0.0), u_done)
            else:
                z = t_ss0
            s_t = [z, z]
            for n in range(8):
                tb, par = n // 2, n % 2
                R = RR[par]
                cc = slice(n * 64, n * 64 + 64)
                i3, b3, w3 = bank((4, 5))
                for h in range(2):
                    t = mm(b3[R, h * 128:h * 128 + 128], hd(F2, h)[:, cc], SS[:, h, :], True, True, w3, wt, s_t[h])
                vn = DV.do(lambda e, R=R, tb=tb, b3=b3: e.tensor_tensor(
                    VN[R, :, tb, :], U4[R, :, tb, :], b3[R, 0:256].rearrange("p (h c) -> p h c", h=2),
                    ALU.subtract), t, ut, kb_read)
                bank_free[i3] = [vn]
                for h in range(2):
                    mm(P2[h][:, cc], SS[:, h, :], QK[:, h, cc], True, False, s_t[h], qe[h], w4, w5)
                yield
                i3, b3, w3 = bank((4, 5))
                for h in range(2):
                    tk = mm(b3[:, h * 128:h * 128 + 128], hd(UKD, h)[R, tb * 128:tb * 128 + 128], VN[R, h, tb, :],
                            True, True, vn, w3)
                for h in range(2):
                    o = (h * 4 + tb) * 64
                    to = mm(P2[h][:, cc], VN[R, h, tb, :], UA[R, o:o + 64], False, True, at)
                for h in range(2):
                    s_t[h] = DV.do(lambda e, h=h, n=n, b3=b3: e.scalar_tensor_tensor(
                        SS[:, h, :], SS[:, h, :], EG[:, h, n:n + 1], b3[:, h * 128:h * 128 + 128], ALU.mult,
                        ALU.add), tk, to, eg)
                bank_free[i3] = [s_t[1]]
                yield
            ot = []
            for h in range(2):
                ot.append(AC.do(lambda e, h=h: e.activation(QK[:, h, :], P2[h][:], ACT.Copy), to))
            bank_free[i4] = [ot[0]]
            bank_free[i5] = [ot[1]]
            u_done.extend([PE.last(), DV.last(), AC.last()])
            for n in list(UNIT) + ["eg"]:
                unit_free[n] = [PE.last(), DV.last(), AC.last()]
            out_t.extend(ot)

        held_v = []
        f1_read = []
        vq = []

        def v_tm(p, h, a):
            i, b, w = bank((4, 5))
            for tb in range(NB):
                c = slice(h * T + tb * 128, h * T + tb * 128 + 128)
                o = slice(tb * 128, tb * 128 + 128)
                t = PE.do(lambda e, c=c, o=o: e.transpose(b[:, o], UNIT["u_f1"][:, c], IDN[:]), w, a)
            f1_read.append(t)
            dst = UNIT["u_bv"][:, h * T:h * T + T].rearrange("p (b c) -> p b c", c=128)

            def scale():
                bv_t[p][h] = DV.do(lambda e: e.tensor_tensor(dst, b[:].rearrange("p (b c) -> p b c", c=128),
                                                             bc(sv3(2)[:, :, 2 * p + h], 128), ALU.mult), t,
                                   unit_free.get("u_bv"))
                bank_free[i] = [bv_t[p][h]]
            if p:
                scale()
            else:
                held_v.append(scale)

        def put_qk(p, n):
            def put(a):
                qk_t[p][n] = a
            return put

        def qkv_item(p, n, b, t):
            i, b_, _ = b
            j, h = n // 2, n % 2
            if j < 2:
                evac_conv(j * 4 + 2 * p + h, QKS[p][:, n, :], x_read, put_qk(p, n), i, b_, t)
            else:
                evac_conv(8 + 2 * p + h, UNIT["u_f1"][:, h * T:h * T + T], unit_free.get("u_f1"),
                          lambda a: vq.append(lambda: v_tm(p, h, a)), i, b_, t)

        stream([("wqkv", X, xt)] * 6, lambda n, b, t: qkv_item(0, n, b[0], t), pre=x_pre, post=x_post,
               fin=(x_fin_a, x_fin_b))
        t_rc, t_rb = sx["g"], sx["r"]

        tabh = AC.do(lambda e: e.activation(WABH[:], WAB[:], ACT.Copy), t_wab)
        tabl = DV.do(lambda e: e.tensor_tensor(WABL[:], WAB[:], WABH[:].bitcast(F32), ALU.subtract), tabh, t_wab)
        i, b, w = bank()
        PE.wait(tabh, tabl)
        for tb in range(NB):
            for k in range(8):
                c = slice(tb * 128, tb * 128 + 128)
                t = mm3(b[:, tb * 8:tb * 8 + 8], XH[:, k, c], XL[:, k, c], WABH[:, 8 * k:8 * k + 8],
                        WABL[:, 8 * k:8 * k + 8], k == 0, k == 7, w, xt[k])
        while vq:
            vq.pop(0)()
        ab = SMV[:, 0:32].rearrange("p (b c) -> p b c", c=8)
        d = DV.do(lambda e, b=b: e.tensor_tensor(ab, b[:, 0:32].rearrange("p (b c) -> p b c", c=8), bc(RC[:, 0:4], 8),
                                                 ALU.mult), t, t_rc)
        bank_free[i] = [d]
        av = ab[:, :, 0:4]
        d = DV.do(lambda e: e.tensor_tensor(av, av, bm(PRM[:, PCOL["dtb"]:PCOL["dtb"] + 4], 4), ALU.add), d)

        def sv(i, n=16):
            return SMV[:, 32 + i * 16:32 + i * 16 + n]

        def sv3(i):
            return sv(i).rearrange("p (b h) -> p b h", h=4)

        a4 = AC.do(lambda e: e.activation(sv3(2), ab[:, :, 4:8], ACT.Sigmoid), d)
        AC.q.append(("i", lambda e: e.preload_act_table_set("natural_log_exp_and_others"), None))
        ea = AC.do(lambda e: e.activation(LNC[:, 12:16], PRM[:, PCOL["alog"]:PCOL["alog"] + 4], ACT.Exp))
        a1 = AC.do(lambda e: e.activation(sv3(0), av, ACT.Abs), d)
        a2 = AC.do(lambda e: e.activation(sv(0), sv(0), ACT.Exp, scale=-1.0), a1)
        a3 = AC.do(lambda e: e.activation(sv(0), sv(0), ACT.Ln, bias=1.0), a2)
        d1 = DV.do(lambda e: e.scalar_tensor_tensor(sv3(1), av, 0.0, sv3(0), ALU.max, ALU.add), a3, d)
        d2 = DV.do(lambda e: e.scalar_tensor_tensor(sv3(1), sv3(1), -1.0, bm(LNC[:, 12:16], 4), ALU.mult, ALU.mult),
                   d1, ea)
        i, b, w = bank()
        mm(b[:, 0:16], cst["tri"], sv(1), True, True, d2, w, t_cm, inc=False)
        t = mm(b[:, 16:32], cst["blk"], sv(1), False, True)
        d3 = DV.do(lambda e, b=b: e.tensor_copy(SMV[:, 80:112], b[:, 0:32]), t)
        bank_free[i] = [d3]
        a5 = AC.do(lambda e: e.activation(sv(5), sv(3), ACT.Exp), d3)
        d4 = DV.do(lambda e: e.tensor_tensor(sv(6), sv(5), sv(2), ALU.mult), a5, a4)
        d5 = DV.do(lambda e: e.tensor_tensor(sv(7), sv(4), sv(3), ALU.subtract), d3)
        a6 = AC.do(lambda e: e.activation(sv(7), sv(7), ACT.Exp), d5)
        sm_t = [d4, a6, a4, d3]
        DV.wait(*sm_t, t_ch)
        AC.wait(*sm_t)
        PE.wait(t_ch)
        t_beta, t_gc = a4, d3
        while held_v:
            held_v.pop(0)()

        grain["t"], grain["s"] = 4, 1
        fills.append(gdn(0, QK0, qk_t[0], o_t[0]))

        acc_t = [None] * 4

        def cfm_conv(c, tk):
            stt = {"t": tk}

            def one(j):
                w = prm("cw", c * 31 + j)
                src = CP[:, c, 2 + j:2 + j + T]
                if j == 0:
                    stt["t"] = DV.do(lambda e: e.tensor_scalar(ACC[:, c, :], src, w, prm("cb", c), ALU.mult,
                                                               ALU.add), stt["t"], x_read)
                else:
                    stt["t"] = DV.do(lambda e: e.scalar_tensor_tensor(ACC[:, c, :], src, w, ACC[:, c, :],
                                                                      ALU.mult, ALU.add), stt["t"])
                acc_t[c] = stt["t"]
            return [lambda j=j: one(j) for j in range(31)]

        for n in range(4):
            b = bank()
            qkv_item(1, n, b, proj_fm("wqkv", [b[1]], X, xt, 8, b[2]))
        for c in range(4):
            i, b, w = bank()
            t = proj_fm("wcfm", [b], X, xt, 8, w)
            d = DV.do(lambda e, b=b: e.tensor_tensor(SG[:], b[:], RB[:], ALU.mult), t, t_rb, vf_free[0])
            bank_free[i] = [d]
            a = AC.do(lambda e: e.activation(SG[:], SG[:], ACT.Sigmoid), d)
            i, b, w = bank()
            t = proj_fm("wcfm", [b], X, xt, 8, w)
            cpv = CP[:, c, 32:32 + T]
            d = DV.do(lambda e, b=b, v=cpv: e.tensor_tensor(v, b[:], RB[:], ALU.mult), t, t_rb)
            bank_free[i] = [d]
            d = DV.do(lambda e, v=cpv: e.tensor_tensor(v, v, SG[:], ALU.mult), d, a, zp)
            vf_free[0] = [d]
            small.extend(cfm_conv(c, d))

        b4, b5 = bank(), bank()
        t4 = proj_fm("wqkv", [b4[1]], X, xt, 8, b4[2])
        drain()
        qkv_item(1, 4, b4, t4)
        t5 = proj_fm("wqkv", [b5[1]], X, xt, 8, b5[2])
        qkv_item(1, 5, b5, t5)
        fills.append(gdn(1, QK1, qk_t[1], o_t[1]))
        small[8:8] = vq
        del vq[:]

        MXH = X2H[:, 0:4, :].rearrange("p k (a t) -> p (k a) t", a=2)
        MXL = X2L[:, 0:4, :].rearrange("p k (a t) -> p (k a) t", a=2)

        def mk(k):
            return GT[:, k // 2, (k % 2) * 256:(k % 2) * 256 + 256]

        mt_ = [scaled(mk(k), prm("mem_g", k), k, MXH, MXL, t_m, N=256) for k in range(8)]
        bi, bk, bw = bank((3,))
        pend = None
        for k in range(8):
            f = colsum(mk(k), 0, bk, k == 0, k == 7, 256, t_m, bw)
            if pend:
                pend()
            pend = f
        t = pend()
        d = DV.do(lambda e, bk=bk: e.tensor_scalar(LNC[:, 0:2], bk[:, 0:2], 1.0 / 1024, EPS, ALU.mult, ALU.add), t)
        mrc = GP.do(lambda e: e.tensor_tensor(LNC[:, 2:4], LNC[:, 0:2], NH[:, 0:2], ALU.pow), d)
        bank_free[bi] = [d]
        tick()
        i2, b2, w2 = bank((3,))
        t = rows(LNC[:, 2:4], 2, mrc, w2, b2[:, 0:256])
        mrb = DV.do(lambda e, b2=b2: e.tensor_copy(MRB, b2[:, 0:256]), t, ca_free)
        bank_free[i2] = [mrb]
        gt_free = [AC.last(), DV.last()]
        km_t = []
        grain["t"], grain["s"] = 2, 2
        for m in range(8):
            i, b, w = bank((0, 1, 2))
            t = proj_fm("wmk", [b], (MXH, MXL), mt_, 8, w, N=256)
            km_t.append(DV.do(lambda e, b=b, m=m: e.tensor_tensor(KM[:, m, :], b[:, 0:256], MRB, ALU.mult), t,
                              mrb))
            bank_free[i] = [km_t[-1]]

        grain["t"], grain["s"] = 4, 1
        gt_t = []
        for c in range(4):
            i, b, w = bank((0, 1, 2))
            t = proj_fm("wgate", [b], X, xt, 8, w)
            d = DV.do(lambda e, b=b, c=c: e.tensor_tensor(GT[:, c, :], b[:], RB[:], ALU.mult), t, gt_free)
            bank_free[i] = [d]
            gt_t.append(AC.do(lambda e, c=c: e.activation(GT[:, c, :], GT[:, c, :], ACT.Silu), d))

        def cfm_norm():
            bi, bk, bw = bank((3,))
            for c in range(4):
                for tb in range(NB):
                    t = mm(bk[:, tb:tb + 1], ACC[:, c, tb * 128:tb * 128 + 128], ONE[:, 0:1], c == 0 and tb == 0,
                           c == 3, acc_t[c], bw)
            d = DV.do(lambda e, bk=bk: e.tensor_scalar(LNC[:, 4:8], bk[:, 0:4], 1.0 / 512, None, ALU.mult), t)
            bank_free[bi] = [d]
            dg = diag(LNC[:, 4:8], 4, d)
            yield
            i2, b2, w2 = bank((3,))
            t = rows_mm(4, dg, w2, b2[:])
            xs = []
            for c in range(4):
                xs.append(DV.do(lambda e, c=c, b2=b2: e.tensor_tensor(ACC[:, c, :], ACC[:, c, :], b2[:],
                                                                      ALU.subtract), t, acc_t[c]))
            bank_free[i2] = [xs[-1]]
            yield
            bi, bk, bw = bank((3,))
            pend = None
            for c in range(4):
                f = colsum(ACC[:, c, :], 0, bk, c == 0, c == 3, T, xs[c], bw)
                if pend:
                    pend()
                pend = f
            t = pend()
            d = DV.do(lambda e, bk=bk: e.tensor_scalar(LNC[:, 4:8], bk[:, 0:4], 1.0 / 512, EPS, ALU.mult, ALU.add), t)
            g = GP.do(lambda e: e.tensor_tensor(LNC[:, 8:12], LNC[:, 4:8], NH[:, 0:4], ALU.pow), d)
            bank_free[bi] = [d]
            dg = diag(LNC[:, 8:12], 4, g)
            yield
            i2, b2, w2 = bank((3,))
            t = rows_mm(4, dg, w2, b2[:])
            for c in range(4):
                d = DV.do(lambda e, c=c, b2=b2: e.scalar_tensor_tensor(ACC[:, c, :], ACC[:, c, :], prm("lg", c), b2[:],
                                                                       ALU.mult, ALU.mult), t)
                a = AC.do(lambda e, c=c: e.activation(ACC[:, c, :], ACC[:, c, :], ACT.Silu, bias=prm("lb", c)), d)
                mix_t[4 + c] = parts(ACC[:, c, :], 4 + c, X2H, X2L, a)
            bank_free[i2] = [d]

        mix_t = [None] * 8
        fin_t = [None] * 4

        def gdn_out(p):
            QK = QKS[p]
            bi, bk, bw = bank((3,))
            f = [colsum(QK[:, h, :], 4 * h, bk, h == 0, True, T, o_t[p][h], bw) for h in range(2)]
            yield
            t = [x() for x in f]
            d = DV.do(lambda e: e.tensor_scalar(OLN[:, 0:8], bk[:, 0:8], 1.0 / 128, EPS, ALU.mult, ALU.add), t)
            g = GP.do(lambda e: e.tensor_tensor(OLN[:, 8:16], OLN[:, 0:8], NH[:, 0:8], ALU.pow), d)
            bank_free[bi] = [d]
            for h in range(2):
                dg = diag(OLN[:, 8 + 4 * h:12 + 4 * h], 4, g)
                yield
                hh = 2 * p + h
                i2, b2, w2 = bank((3,))
                t = rows_mm(4, dg, w2, b2[:])
                d = DV.do(lambda e, h=h, b2=b2: e.scalar_tensor_tensor(QK[:, h, :], QK[:, h, :], prm("gn"), b2[:],
                                                                       ALU.mult, ALU.mult), t, o_t[p][h])
                bank_free[i2] = [d]
                fin_t[hh] = DV.do(lambda e, h=h, hh=hh: e.tensor_tensor(GT[:, hh, :], QK[:, h, :], GT[:, hh, :],
                                                                        ALU.mult), d, gt_t[hh])
                yield

        for _ in gdn_out(0):
            tick()
        v_free = [AC.last(), DV.last(), PE.last()]
        vm_t = []
        grain["t"], grain["s"] = 2, 2
        cn = cfm_norm()
        for cg in range(2):
            bb = [bank((0, 1, 2)) for _ in range(2)]
            t = proj_tm("wmv", [x[1] for x in bb], (MXH, MXL), mt_, [x[2] for x in bb], nb=2)
            for tb in range(2):
                i, b, w = bb[tb]
                vm_t.append(AC.do(lambda e, b=b, tb=tb, cg=cg: e.activation(
                    VM[:, tb, cg * 512:cg * 512 + 512], b[:], ACT.Copy, scale=LNC[:, 2 + tb:3 + tb]), t[tb], v_free,
                    mrc))
                bank_free[i] = [vm_t[-1]]
        mem_read = [PE.last()]
        while small:
            trickle(4)
            tick()
        for _ in cn:
            tick()
            tick()
        drain()
        for _ in gdn_out(1):
            pass
        for hh in range(4):
            mix_t[hh] = parts(GT[:, hh, :], hh, X2H, X2L, fin_t[hh], mem_read)

        end_m = [e_.last() for e_ in engines]
        ph.close()

        def phase():
            for e_ in (AC, DV, GP):
                e_.wait(end_m)

        ph = ExitStack()
        phase()
        for e_ in engines:
            e_.next_phase()

        def y_evac(k, b, i, t, first, last, ystate):
            f = None
            if last and k == 0:
                ystate["bank"] = bank((7,))
            if first:
                if last:
                    bi, bk, bw = ystate["bank"]
                    f = colsum(b[:], 0, bk, k == 0, k == 7, T, t, bw)
                yt = AC.do(lambda e: e.activation(Y[:, k, :], b[:], ACT.Copy), t, y_free[0])
            else:
                yt = DV.do(lambda e: e.tensor_tensor(Y[:, k, :], Y[:, k, :], b[:], ALU.add), t, ystate["t"][k])
                if last:
                    bi, bk, bw = ystate["bank"]
                    f = colsum(Y[:, k, :], 0, bk, k == 0, k == 7, T, yt, bw)
            ystate["t"][k] = yt
            bank_free[i] = [yt]
            if last:
                if ystate.get("pend"):
                    ystate["pend"]()
                ystate["pend"] = f

        y_free = [[]]

        class Boundary:

            def __init__(self, ystate, gpost, hts, pres):
                self.ys, self.gpost, self.hts, self.pres = ystate, gpost, hts, pres
                self.xts = [[None] * 8 for _ in pres]
                self.f = {}
                bi, bk, bw = ystate["bank"]
                g, d = fin_a(bi, bk, ystate["pend"](), 4)
                self.i2, self.b2, self.t2 = fin_b(d, 4, None)
                if pres:
                    self.sb = bank((7,))
                self.ht = [None] * 8

            def pre(self, k):
                if k == 0:
                    self.first(0)
                    self.second(0)
                if k < 7:
                    self.first(k + 1)
                if k:
                    self.second(k)

            def second(self, k):
                for n, (g, XXH, XXL, free) in enumerate(self.pres):
                    self.xts[n][k].append(DV.do(lambda e, g=g, XXH=XXH, XXL=XXL: e.scalar_tensor_tensor(
                        XXL[:, k, :], H[:, k, :], prm(g[0], g[1] + k), XXH[:, k, :].bitcast(F32), ALU.mult,
                        ALU.subtract), self.xts[n][k], self.ht[k], free))

            def first(self, k):
                b2, gp = self.b2, self.gpost
                d = DV.do(lambda e: e.scalar_tensor_tensor(Y[:, k, :], Y[:, k, :], prm(gp[0], gp[1] + k), b2[:],
                                                           ALU.mult, ALU.mult), self.t2, self.ys["t"][k])
                if k == 7:
                    bank_free[self.i2] = [d]
                d = DV.do(lambda e: e.tensor_tensor(H[:, k, :], H[:, k, :], Y[:, k, :], ALU.add), d, self.hts[k])
                self.ht[k] = d
                if k == 7:
                    y_free[0] = [d]
                for n, (g, XXH, XXL, free) in enumerate(self.pres):
                    self.xts[n][k] = [AC.do(lambda e, g=g, XXH=XXH: e.activation(
                        XXH[:, k, :], H[:, k, :], ACT.Copy, scale=prm(g[0], g[1] + k)), d, free)]
                if self.pres:
                    self.f[k] = colsum(H[:, k, :], 0, self.sb[1], k == 0, k == 7, T, d, self.sb[2])

            def post(self, k):
                self.t = self.f[k]()

            def a(self):
                rb_free[0] = [DV.last(), AC.last()]
                self.g, self.d = fin_a(self.sb[0], self.sb[1], self.t, 4)

            def b(self):
                self.r = fin_b(self.d, 4, RB)

            def kw(self):
                return dict(pre=self.pre, post=self.post, fin=(self.a, self.b))

        H = alloc(ph, "h", [128, 8, T])
        Y = alloc(ph, "y", [128, 8, T])
        X2 = (X2H, X2L)

        def y_stream(name, xt_, nk, first, last, ys, ks=None):
            stream([(name, X2, xt_)] * 8, lambda m, b, t: y_evac(m, b[0][1], b[0][0], t, first, last, ys), nk=nk,
                   ks=ks)

        grain["t"], grain["s"] = 2, 2
        ys = {"t": [None] * 8}
        y_stream("wout", mix_t, 8, True, True, ys, ks=[4, 5, 6, 7, 0, 1, 2, 3])
        hts = [load(f"h{i}", H[:, 2 * i:2 * i + 2, :], xsrc[:, 2 * i:2 * i + 2, :], end_m) for i in range(4)]
        hts = [hts[k // 2] for k in range(8)]
        xt_free = [PE.last()]
        B = Boundary(ys, ("norm_g", 8), hts, [(("norm_g", 16), XH, XL, xt_free)])
        xt = B.xts[0]

        pa = ExitStack()
        QX = [alloc(pa, f"qx{i}", [128, 2, T]) for i in range(2)]
        PM = [alloc(pa, f"pm{i}", [128, NB, 256]) for i in range(2)]
        PT = alloc(pa, "pt", [128, 2, T])
        SX = alloc(pa, "sx", [128, 16])
        o_x = [None] * 8
        ax = {"q": [[], []], "pt": [], "sx": [], "pm": [[], []]}

        def attend(h, qt):
            Q = QX[h % 2]
            Pm = PM[h % 2]
            pe_ = []
            for u in range(2):
                i, b, w = bank((4, 5))
                for v in range(2):
                    c = slice((2 * u + v) * 128, (2 * u + v) * 128 + 128)
                    for d_ in range(2):
                        t = mm(b[:, v * 256:v * 256 + 256], Q[:, d_, c], KM[:, 2 * h + d_, :], d_ == 0, d_ == 1, w,
                               qt[d_], km_t[2 * h + d_])
                d = DV.do(lambda e, u=u, b=b: e.tensor_reduce(SX[:, 2 * u:2 * u + 2],
                                                              b[:].rearrange("p (v m) -> p v m", v=2), AXX,
                                                              ALU.max), t, ax["sx"])
                d = DV.do(lambda e, u=u: e.tensor_scalar(SX[:, 4 + 2 * u:6 + 2 * u], SX[:, 2 * u:2 * u + 2], -1.0 / 16,
                                                         None, ALU.mult), d)
                for v in range(2):
                    tb = 2 * u + v
                    a = AC.do(lambda e, tb=tb, v=v, b=b: e.activation(
                        Pm[:, tb, :], b[:, v * 256:v * 256 + 256], ACT.Exp, scale=1.0 / 16,
                        bias=SX[:, 4 + tb:5 + tb], accum_out=SX[:, 8 + tb:9 + tb]), d, ax["pm"][h % 2])
                    pe_.append(a)
                bank_free[i] = [a]
                yield
            ax["q"][h % 2] = [t]
            r = DV.do(lambda e: e.reciprocal(SX[:, 12:16], SX[:, 8:12]), pe_)
            n_ = DV.do(lambda e: e.tensor_tensor(Pm[:], Pm[:], bc(SX[:, 12:16], 256), ALU.mult), r)
            ax["sx"] = [n_]
            yield
            pt = []
            for mb in range(2):
                i, b, w = bank((4, 5))
                for tb in range(NB):
                    t = PE.do(lambda e, tb=tb, mb=mb, b=b: e.transpose(
                        b[:, tb * 128:tb * 128 + 128], Pm[:, tb, mb * 128:mb * 128 + 128], IDN[:]), w, n_)
                pt.append(AC.do(lambda e, mb=mb, b=b: e.activation(PT[:, mb, :], b[:], ACT.Copy), t, ax["pt"]))
                bank_free[i] = [pt[-1]]
            ax["pm"][h % 2] = [t]
            yield
            for et in range(2):
                i, b, w = bank((4, 5))
                for mb in range(2):
                    c = slice(h * 256 + et * 128, h * 256 + et * 128 + 128)
                    t = mm(b[:], VM[:, mb, c], PT[:, mb, :], mb == 0, mb == 1, w, pt[mb], vm_t)
                o_x[2 * h + et] = parts(b[:], 2 * h + et, X2H, X2L, t, xo_free)
                bank_free[i] = list(o_x[2 * h + et])
            ax["pt"] = [t]
            yield

        xo_free = [xt_free]
        qts = [[None, None] for _ in range(4)]

        def xq_evac(m, b, t):
            i, b_, _ = b[0]
            h, d_ = m // 2, m % 2
            if d_ == 0:
                while len(fills) > 1:
                    tick()
            qts[h][d_] = DV.do(lambda e: e.tensor_tensor(QX[h % 2][:, d_, :], b_[:], RB[:], ALU.mult), t, B.r,
                               ax["q"][h % 2])
            bank_free[i] = [qts[h][d_]]
            if d_:
                fills.append(attend(h, qts[h]))

        stream([("wxq", (XH, XL), xt)] * 8, xq_evac, **B.kw())
        hts = B.ht
        drain()
        ys = {"t": [None] * 8}
        y_stream("wxo", o_x, 8, True, True, ys)
        xt_free = [PE.last()]
        end_m = [e_.last() for e_ in engines]
        pa.close()
        phase()
        for e_ in engines:
            e_.next_phase()
        B = Boundary(ys, ("norm_g", 24), hts, [(("norm_g", 32), XH, XL, xt_free)])
        xt = B.xts[0]

        pf = ExitStack()
        UP = [alloc(pf, f"up{i}", [128, T + 4]) for i in range(4)]
        UC = [alloc(pf, f"uc{i}", [128, T]) for i in range(4)]
        zu = [GP.do(lambda e, u=u: e.memset(u[:, 0:4], 0.0)) for u in UP]
        up_free = [[] for _ in range(4)]
        uc_free = [[] for _ in range(4)]
        ys = {"t": [None] * 8}
        m_free = [PE.last()]
        mid = [None] * 8
        ab_ = {}

        def up_evac(a0, m, b, t):
            i, b_, _ = b[0]
            j, half = a0 + m // 2, m % 2
            n = m % 4
            ch = j + 22 * half
            U, C = UP[n], UC[n]
            d = DV.do(lambda e: e.tensor_tensor(U[:, 4:4 + T], b_[:], RB[:], ALU.mult), t, B.r, up_free[n], zu)
            bank_free[i] = [d]
            if half == 0:
                flush_late()
            d = DV.do(lambda e: e.tensor_scalar(C[:], U[:, 2:2 + T], prm("fw", ch * 3), prm("fb", ch), ALU.mult,
                                                ALU.add), d, uc_free[n])
            for q in (1, 2):
                d = DV.do(lambda e, q=q: e.scalar_tensor_tensor(C[:], U[:, 2 + q:2 + q + T], prm("fw", ch * 3 + q),
                                                                C[:], ALU.mult, ALU.add), d)
            up_free[n] = [d]
            if half == 0:
                ab_[0] = (AC.do(lambda e: e.activation(C[:], C[:], ACT.Silu), d), C, n)
                return
            ta, Ca, na = ab_[0]
            d = DV.do(lambda e: e.tensor_tensor(Ca[:], Ca[:], C[:], ALU.mult), ta, d)
            uc_free[na] = mid[j - a0] = parts(Ca[:], j - a0, X2H, X2L, d, m_free, late=late)
            uc_free[n] = [d]

        for part, (a0, b0) in enumerate(((0, 8), (8, 16), (16, 22))):
            stream([("wup", (XH, XL), xt)] * (2 * (b0 - a0)), lambda m, b, t, a0=a0: up_evac(a0, m, b, t),
                   **(B.kw() if part == 0 else {}))
            flush_late()
            y_stream("wdn", mid, b0 - a0, part == 0, part == 2, ys)
            m_free = [PE.last()]
        hts = B.ht
        xt_free = [PE.last()]
        end_m = [e_.last() for e_ in engines]
        pf.close()
        phase()
        for e_ in engines:
            e_.next_phase()
        B = Boundary(ys, ("norm_g", 40), hts, [(("rpre", 0), XH, XL, xt_free)])
        xt = B.xts[0]

        pr = ExitStack()
        CS = alloc(pr, "cs", [128, 2, T])
        DD = alloc(pr, "dd", [128, T])
        QR, KR = KQ[:, 0:2, :], KQ[:, 2:4, :]
        TM = [alloc(pr, f"tm{i}", [128, T]) for i in range(3)]
        SC = alloc(pr, "sc", [128, 1280])
        VR, GR = QK0, ACC
        BN = alloc(pr, "bn", [128, NB, 10])
        SOFF = [0, 512, 896, 1152]
        t_cs = load("cs", CS[:], A["rope"], end_m)
        tm_free = [[], [], []]
        free = {"qk": [], "v": [], "sc": [], "g": [], "dd": [], "bn": []}
        o_r = [None] * 8
        x2_free = [[PE.last()]]

        def rot(dst, ops):
            (i1, b1, t1), (i2, b2, t2) = ops
            a = DV.do(lambda e: e.tensor_tensor(TM[0][:], b1[:], RB[:], ALU.mult), t1, B.r, tm_free[0])
            bank_free[i1] = [a]
            c = DV.do(lambda e: e.tensor_tensor(TM[1][:], b2[:], RB[:], ALU.mult), t2, tm_free[1])
            bank_free[i2] = [c]
            cos, sin = CS[:, 0, :], CS[:, 1, :]
            d1 = DV.do(lambda e: e.tensor_tensor(dst[:, 0, :], TM[0][:], cos, ALU.mult), a, t_cs, free["qk"])
            d2 = DV.do(lambda e: e.tensor_tensor(TM[2][:], TM[1][:], sin, ALU.mult), c, tm_free[2])
            d3 = DV.do(lambda e: e.tensor_tensor(dst[:, 0, :], dst[:, 0, :], TM[2][:], ALU.subtract), d1, d2)
            d4 = DV.do(lambda e: e.tensor_tensor(dst[:, 1, :], TM[0][:], sin, ALU.mult), a)
            d5 = DV.do(lambda e: e.tensor_tensor(TM[2][:], TM[1][:], cos, ALU.mult), d3)
            d6 = DV.do(lambda e: e.tensor_tensor(dst[:, 1, :], dst[:, 1, :], TM[2][:], ALU.add), d4, d5)
            tm_free[0] = [d4]
            tm_free[1] = [d5]
            tm_free[2] = [d6]
            return [d3, d6]

        def retain(h, qt, kt, vt, gt, t_dd):
            sc = []
            for s in range(NB):
                n = (4 - s) * 128
                i, b, w = bank((4, 5))
                for d_ in range(2):
                    t = mm(b[:, 0:n], KR[:, d_, s * 128:s * 128 + 128], QR[:, d_, s * 128:T], d_ == 0, d_ == 1, w, qt,
                           kt)
                sc.append(DV.do(lambda e, s=s, n=n, b=b: e.tensor_tensor(SC[:, SOFF[s]:SOFF[s] + n], b[:, 0:n],
                                                                         DD[:, 0:n], ALU.mult), t, t_dd,
                                free["sc"]))
                bank_free[i] = [sc[-1]]
                yield
            free["qk"] = [t]
            free["dd"] = [sc[-1]]
            while gt[0] is None:
                yield
            gg = []
            for tb in range(NB):
                i, b, w = bank((6, 7))
                for s in range(tb + 1):
                    t = mm(b[:], SC[:, SOFF[s] + (tb - s) * 128:SOFF[s] + (tb - s) * 128 + 128], VR[:, s, :], s == 0,
                           s == tb, w, sc, vt[s])
                s6, ag, rs = BN[:, tb, 0:6], BN[:, tb, 6:8], BN[:, tb, 8:9]
                d = DV.do(lambda e, b=b, s6=s6: e.bn_stats(s6, b[:]), t, free["bn"])
                d = DV.do(lambda e, s6=s6, ag=ag: e.bn_aggr(ag, s6), d)
                d = DV.do(lambda e, tb=tb: e.tensor_scalar(BN[:, tb, 9:10], BN[:, tb, 7:8], EPS, None, ALU.add), d)
                g = GP.do(lambda e, tb=tb, rs=rs: e.tensor_tensor(rs, BN[:, tb, 9:10], NH[:, 0:1], ALU.pow), d)
                yield
                c = DV.do(lambda e, tb=tb, b=b, rs=rs: e.tensor_scalar(
                    SQB[tb % 2][:], b[:], BN[:, tb, 6:7], rs, ALU.subtract, ALU.mult), g, d, sqb_free[tb % 2])
                bank_free[i] = [c]
                c = DV.do(lambda e, tb=tb: e.tensor_tensor(GR[:, tb, :], GR[:, tb, :], SQB[tb % 2][:], ALU.mult), c,
                          gt[tb])
                sqb_free[tb % 2] = [c]
                gg.append(c)
            free["v"] = [t]
            free["sc"] = [t]
            free["bn"] = [gg[-1]]
            yield
            for et in range(4):
                i, b, w = bank((4, 5))
                for tb in range(NB):
                    t = PE.do(lambda e, tb=tb, et=et, b=b: e.transpose(
                        b[:, tb * 128:tb * 128 + 128], GR[:, tb, et * 128:et * 128 + 128], IDN[:]), w, gg[tb])
                kk = (h % 2) * 4 + et
                o_r[kk] = parts(b[:], kk, X2H, X2L, t, x2_free[0])
                bank_free[i] = list(o_r[kk])
                if et % 2:
                    yield
            free["g"] = [t]

        SQB = [alloc(pr, f"sqb{i}", [128, T]) for i in range(2)]
        sqb_free = [[], []]
        ys = {"t": [None] * 8}
        for h in range(4):
            two = []
            qkt = []

            def rqk_evac(n, b, t, two=two, qkt=qkt):
                two.append((b[0][0], b[0][1], t))
                if n % 2:
                    qkt.append(rot((QR, KR)[n // 2], two[-2:]))

            stream([("rqk", (XH, XL), xt)] * 4, rqk_evac, ng=3 if h == 0 else 1, **(B.kw() if h == 0 else {}))
            qt, kt = qkt
            t_rc = B.g
            drain()
            t_dd = load("dd", DD[:], A["rdec"][h], free["dd"], end_m)
            res = []
            for j, nm in enumerate(("rv", "rg")):
                bb = [bank() for _ in range(4)]
                t = proj_tm(nm, [x[1] for x in bb], (XH, XL), xt, [x[2] for x in bb])
                r_ = []
                for tb in range(NB):
                    i, b, w = bb[tb]
                    if j == 0:
                        a = AC.do(lambda e, tb=tb, b=b: e.activation(VR[:, tb, :], b[:], ACT.Copy,
                                                                     scale=RC[:, tb:tb + 1]), t[tb], t_rc, free["v"])
                    else:
                        a = AC.do(lambda e, tb=tb, b=b: e.activation(GR[:, tb, :], b[:], ACT.Silu,
                                                                     scale=RC[:, tb:tb + 1]), t[tb], t_rc, free["g"])
                    bank_free[i] = [a]
                    r_.append(a)
                res.append(r_)
                if j == 0:
                    gt = [None] * 4
                    fills.append(retain(h, qt, kt, r_, gt, t_dd))
                else:
                    for tb in range(NB):
                        gt[tb] = r_[tb]
            if h % 2:
                drain()
                y_stream("rout", o_r, 8, h == 1, h == 3, ys)
                x2_free[0] = [PE.last()]
        hts = B.ht
        xt_free = [PE.last()]
        end_m = [e_.last() for e_ in engines]
        pr.close()
        phase()
        for e_ in engines:
            e_.next_phase()
        B = Boundary(ys, ("rpost", 0), hts, [(("kvn", 0), XH, XL, xt_free), (("spre", 0), X2H, X2L, xt_free)])
        xk_t, xs_t = B.xts

        sbs = ExitStack()
        MH = alloc(sbs, "mh", [128, 4, T], F32R)
        ML = alloc(sbs, "ml", [128, 4, T], F32R)
        KS, QS = KQ[:, 0:2, :], KQ[:, 2:4, :]
        VS, GS = QK0, ACC
        ZZ = alloc(sbs, "zz", [128, 1280])
        SP = alloc(sbs, "sp", [128, 1280])
        BIG = alloc(sbs, "big", [128, 128])
        LOW = alloc(sbs, "low", [128, 128])
        t_big = load("big", BIG[:], A["sbc"][0], end_m)
        t_low = load("big", LOW[:], A["sbc"][1])
        free = {"k": [], "q": [], "v": [], "g": [[], [], [], []], "z": [], "sp": []}
        m_free = [[]]
        o_s = [None] * 4
        AC.q.append(("i", lambda e: e.preload_act_table_set("natural_log_exp_and_others"), None))

        sb = {"z": 0, "busy": False}

        def stick(h, kt, qt, vt, gt):
            zt = []
            for s in range(NB):
                n = (4 - s) * 128
                i, b, w = bank((4, 5))
                t = mm(b[:, 0:n], KS[:, h, s * 128:s * 128 + 128], QS[:, h, s * 128:T], True, True, w, kt, qt)
                o = SOFF[s]
                d = DV.do(lambda e, o=o, b=b: e.tensor_tensor(ZZ[:, o:o + 128], b[:, 0:128], BIG[:], ALU.min), t,
                          t_big, free["z"])
                zt.append(d)
                if n > 128:
                    a = AC.do(lambda e, o=o, n=n, b=b: e.activation(ZZ[:, o + 128:o + n], b[:, 128:n], ACT.Copy), t,
                              free["z"], d)
                    zt.append(a)
                    bank_free[i] = [d, a]
                else:
                    bank_free[i] = [d]
                if s % 2:
                    yield
            if h:
                free["k"] = [t]
            sb["z"] += 1
            a = AC.do(lambda e: e.activation(SP[:], ZZ[:], ACT.Abs), zt, free["sp"])
            a = AC.do(lambda e: e.activation(SP[:], SP[:], ACT.Exp, scale=-1.0), a)
            a = AC.do(lambda e: e.activation(SP[:], SP[:], ACT.Ln, bias=1.0), a)
            sp = DV.do(lambda e: e.scalar_tensor_tensor(SP[:], ZZ[:], 0.0, SP[:], ALU.max, ALU.add), a, zt)
            for _ in range(4):
                yield
            wt = []
            for s in range(NB):
                n = (4 - s) * 128
                i, b, w = bank((4, 5))
                for j in range(s, NB):
                    m = (4 - j) * 128
                    t = mm(b[:, n - m:n], LOW[:] if j == s else ONE[:], SP[:, SOFF[j]:SOFF[j] + m], j == s, j == 3, w,
                           sp, t_low)
                o = SOFF[s]
                d = DV.do(lambda e, o=o, n=n, b=b: e.tensor_tensor(ZZ[:, o:o + n], ZZ[:, o:o + n], b[:, 0:n],
                                                                   ALU.subtract), t, sp)
                bank_free[i] = [d]
                wt.append(AC.do(lambda e, o=o, n=n: e.activation(ZZ[:, o:o + n], ZZ[:, o:o + n], ACT.Exp), d))
                if s % 2:
                    yield
            free["sp"] = [t]
            while sb["busy"]:
                yield
            for et in range(2):
                i, b, w = bank((6, 7))
                for s in range(NB):
                    n = (4 - s) * 128
                    t = mm(b[:, T - n:T], VS[:, s, h * 256 + et * 128:h * 256 + et * 128 + 128],
                           ZZ[:, SOFF[s]:SOFF[s] + n], s == 0, s == 3, w, wt[s], vt[s])
                kk = 2 * h + et
                d = DV.do(lambda e, kk=kk, b=b: e.tensor_tensor(GS[:, kk, :], GS[:, kk, :], b[:], ALU.mult), t,
                          gt[kk])
                bank_free[i] = [d]
                o_s[kk] = parts(GS[:, kk, :], kk, MH, ML, d, m_free[0])
                free["g"][kk] = list(o_s[kk])
                yield
            free["z"] = [t]
            if h:
                free["v"] = [t]

        ys = {"t": [None] * 8}

        def sout(part):
            def evac(n, b, t):
                for m in range(2):
                    y_evac(2 * n + m, b[m][1], b[m][0], t, part == 0, part == 3, ys)
            stream([("sout", (MH, ML), o_s)] * 4, evac, nk=4, ng=2, mt=2)
            m_free[0] = [PE.last()]

        XS, XK = (X2H, X2L), (XH, XL)
        for p in range(4):
            bb = []
            stream([("sk", XK, xk_t)] * 2 + [("sq", XS, xs_t)] * 2, lambda n, b, t: bb.append((b[0][0], b[0][1], t)),
                   ng=3 if p == 0 else 1, **(B.kw() if p == 0 else {}))
            t_rc, t_rb = B.g, B.r
            while p and sb["z"] < 2 * p:
                tick()
            kt, qt, gt = [], [], [None] * 4
            for n, (i, b, t) in enumerate(bb):
                h = n % 2
                if n < 2:
                    kt.append(DV.do(lambda e, b=b, h=h: e.tensor_tensor(KS[:, h, :], b[:], RB[:], ALU.mult), t, t_rb,
                                    free["k"]))
                    bank_free[i] = kt[-1:]
                else:
                    qt.append(DV.do(lambda e, b=b, h=h: e.scalar_tensor_tensor(
                        QS[:, h, :], b[:], 128.0 ** -0.5, RB[:], ALU.mult, ALU.mult), t))
                    bank_free[i] = qt[-1:]
            bb = [bank() for _ in range(4)]
            t = proj_tm("sv", [x[1] for x in bb], XK, xk_t, [x[2] for x in bb])
            drain()
            vt = []
            for tb in range(NB):
                i, b, w = bb[tb]
                vt.append(AC.do(lambda e, tb=tb, b=b: e.activation(VS[:, tb, :], b[:], ACT.Copy,
                                                                   scale=RC[:, tb:tb + 1]), t[tb], t_rc, free["v"]))
                bank_free[i] = [vt[-1]]
            for kk in range(4):
                i, b, w = bank()
                t = proj_fm("sg", [b], XS, xs_t, 8, w)
                d = DV.do(lambda e, kk=kk, b=b: e.tensor_tensor(GS[:, kk, :], b[:], RB[:], ALU.mult), t,
                          free["g"][kk])
                bank_free[i] = [d]
                gt[kk] = AC.do(lambda e, kk=kk: e.activation(GS[:, kk, :], GS[:, kk, :], ACT.Silu), d)
            fills.append(stick(0, kt, qt, vt, gt))
            fills.append(stick(1, kt, qt, vt, gt))
            if p:
                sb["busy"] = True
                sout(p - 1)
                sb["busy"] = False
        drain()
        sout(3)
        F = Boundary(ys, ("spost", 0), B.ht, [])
        osrc = out.rearrange("(k p) t -> p k t", p=128)
        ot = []
        for k in range(8):
            F.pre(k)
            if k % 2:
                ot.append(load(f"h{k // 2}", osrc[:, k - 1:k + 1, :], H[:, k - 1:k + 1, :], F.ht[k - 1], F.ht[k]))
        SY.wait(*ot)
        sbs.close()
        ph.close()
        keepA.close()

        block = root.enter_context(nc.Block())

        @block.sync
        def _(e):
            for kind, a, b in SY.q:
                if kind == "w":
                    e.wait_ge(a, b)
                else:
                    e.dma_start(a[0], a[1]).then_inc(b, 16)

        @block.tensor
        def _(e):
            PE.emit(e)

        @block.scalar
        def _(e):
            AC.emit(e)

        @block.vector
        def _(e):
            DV.emit(e)

        @block.gpsimd
        def _(e):
            GP.emit(e)


def constants():
    i = np.arange(128)
    p, c = i[:, None], i[None, :]
    same = (p // 64) == (c // 64)
    m = {"ident": p == c, "ones": np.ones((128, 128), bool), "tri": same & (p <= c), "blk": same}
    cst = np.stack([m[n].astype(np.float32) for n in CST])
    p, c = p % 64, c[:, :64]
    m = {"id64": p == c, "mc": p <= c, "ms": p < c, "m1t": (p // 2 == c // 2) & (p < c)}
    for s in (2, 4, 8, 16, 32):
        m[f"m{s}t"] = (p // (2 * s) == c // (2 * s)) & ((c // s) % 2 == 1) & ((p // s) % 2 == 0)
    csh = np.stack([m[n].astype(np.float32) for n in CSH], 1)
    p = i[:, None]
    c = i[None, :]
    half = 128
    inv = (1.0 / (np.float32(10000.0) ** (np.arange(half, dtype=np.float32) / np.float32(half)))).astype(np.float32)
    ang = (np.arange(T, dtype=np.float32)[None, :] * inv[:, None]).astype(np.float32)
    rope = np.stack([np.cos(ang.astype(np.float64)), np.sin(ang.astype(np.float64))], 1).astype(np.float32)
    rd = []
    for h in range(4):
        lg = np.log1p(-np.exp2(-5.0 - h))
        diff = np.arange(T)[None, :] - p
        rd.append(np.where(diff >= 0, np.exp(lg * np.maximum(diff, 0)), 0.0) / 16.0)
    rdec = np.stack(rd).astype(np.float32)
    sbc = np.stack([np.where(p < c, np.float32(3e38), np.float32(-30000.0)), (p >= c).astype(np.float32)])
    return {"cst": cst, "csh": csh, "rope": np.ascontiguousarray(rope), "rdec": rdec, "sbc": sbc.astype(np.float32)}


def cols(v):
    v = np.asarray(v)
    return v.reshape(-1, 128).T


def fm(w, nk=8):
    K, N = w.shape
    return w.reshape(K // 128 // nk, nk, 128, N // 128, 128).transpose(0, 3, 2, 1, 4).reshape(-1, 128, nk * 128)


def tm(w):
    K, N = w.shape
    return w.reshape(K // 256, 2, 128, N // 512, 512).transpose(3, 0, 2, 1, 4).reshape(-1, 128, 1024)


def kernel(**inputs):
    import concourse.bacc as _bacc
    from concourse.bass_utils import run_bass_kernel_spmd as _run

    I = {k: np.asarray(v) for k, v in inputs.items()}
    w_in = I["w_in"][0]
    gw = I["gdn_conv_w"][0]
    P = np.concatenate([
        cols(I["norm_g"][0]), cols(I["mem_norm_g"][0]),
        gw.reshape(4, 12, 128).transpose(2, 1, 0).reshape(128, 48), cols(I["gdn_norm_g"][0]),
        I["cfm_dw_w"][0].reshape(31, 4, 128).transpose(2, 1, 0).reshape(128, 124),
        cols(I["cfm_dw_b"][0]), cols(I["cfm_ln_g"][0]), cols(I["cfm_ln_b"][0]),
        I["ffn_conv_w"][0].reshape(3, 44, 128).transpose(2, 1, 0).reshape(128, 132), cols(I["ffn_conv_b"][0]),
        cols(I["ret_norm_pre_2"][0]), cols(I["ret_norm_post_2"][0]), cols(I["kv_norm_2"]),
        cols(I["sb_norm_pre_2"][0]), cols(I["sb_norm_post_2"][0]),
        np.broadcast_to(I["gdn_a_log"][0][None, :], (128, 4)), np.broadcast_to(I["gdn_dt_bias"][0][None, :], (128, 4)),
    ], axis=1)
    dn = I["ffn_w_down"][0]
    dn2 = fm(dn[2048:], 6)
    wdn = np.concatenate([fm(dn[:2048]), np.pad(dn2, ((0, 0), (0, 0), (0, 256)))])
    rin = I["ret_w_in_2"][0]
    rqk = np.concatenate([rin[:, j * 1024 + h * 256:j * 1024 + h * 256 + 256] for h in range(4) for j in range(2)],
                         axis=1)
    kv = I["w_kv_2"]
    sin_ = I["sb_w_in_2"][0]
    so = I["sb_w_out_2"][0]
    sout = so.reshape(4, 4, 128, 4, 256).transpose(0, 3, 2, 1, 4).reshape(16, 128, 1024)
    arrays = {
        "xT": I["x"][0].T, "memT": I["mem"][0].T, "prm": P,
        "wab": w_in[:, 2048:2056].reshape(8, 128, 8).transpose(1, 0, 2).reshape(128, 64),
        "wcfm": fm(w_in[:, 2056:3080]), "wqkv": fm(w_in[:, 0:1536]), "wgate": fm(w_in[:, 1536:2048]),
        "wmk": fm(I["xa_w_kv"][0][:, :1024]), "wmv": tm(I["xa_w_kv"][0][:, 1024:]),
        "wout": fm(I["w_out"][0]), "wxq": fm(I["xa_w_q"][0]), "wxo": fm(I["xa_w_o"][0]),
        "wup": fm(I["ffn_w_up"][0]), "wdn": wdn, "rqk": fm(rqk), "rv": tm(rin[:, 2048:4096]),
        "rg": tm(rin[:, 4096:]), "rout": fm(I["ret_w_out_2"][0]), "sk": fm(kv[:, :1024]), "sv": tm(kv[:, 1024:]),
        "sq": fm(sin_[:, :1024]), "sg": fm(sin_[:, 1024:]), "sout": sout,
    }
    arrays.update(constants())
    nc = _bacc.Bacc("TRN2", target_bir_lowering=False, num_devices=1)
    arrs, A = {}, {}
    for n, a in arrays.items():
        a = np.ascontiguousarray(a)
        arrs["in_" + n] = a
        A[n] = nc.dram_tensor("in_" + n, a.shape, mybir.dt.from_np(a.dtype), kind="ExternalInput").ap()
    out = nc.dram_tensor("out_0", (1024, T), F32, kind="ExternalOutput").ap()
    program(nc, A, out)
    r = _run(nc, [arrs], core_ids=[0])
    return np.ascontiguousarray(r.results[0]["out_0"].T)[None]
```

```python
from contextlib import ExitStack

import numpy as np

import concourse.bass as bass
from concourse import mybir

F32 = mybir.dt.float32
F32R = mybir.dt.float32r
ALU = mybir.AluOpType
ACT = mybir.ActivationFunctionType
AXX = mybir.AxisListType.X

T = 512
NB = 4
EPS = 1e-6
NRAW = 3
NSPL = 4
SLAB = 1024

PCOL = {}
_at = 0
for _n, _w in (("norm_g", 48), ("mem_g", 8), ("gconv", 48), ("gn", 1), ("cw", 124), ("cb", 4), ("lg", 4), ("lb", 4),
               ("fw", 132), ("fb", 44), ("rpre", 8), ("rpost", 8), ("kvn", 8), ("spre", 8), ("spost", 8),
               ("alog", 4), ("dtb", 4)):
    PCOL[_n] = _at
    _at += _w
NPRM = _at

CST = ["ident", "ones", "tri", "blk"]
CSH = ["id64", "mc", "ms", "m1t", "m2t", "m4t", "m8t", "m16t", "m32t"]


class Engine:

    def __init__(self, sems):
        self.sems = sems
        self.phase = 0
        self.n = 0
        self.q = []
        self.seen = {}

    def wait(self, *toks):
        for t in toks:
            if t is None:
                continue
            if isinstance(t, list):
                self.wait(*t)
                continue
            s, v = t
            if self.seen.get(s.name, 0) < v:
                self.seen[s.name] = v
                self.q.append(("w", s, v))

    def do(self, fn, *toks, inc=True):
        self.wait(*toks)
        if not inc:
            self.q.append(("i", fn, None))
            return None
        self.n += 1
        s = self.sems[self.phase]
        self.q.append(("i", fn, s))
        return (s, self.n)

    def last(self):
        return (self.sems[self.phase], self.n) if self.n else None

    def next_phase(self):
        self.phase += 1
        self.n = 0

    def emit(self, e):
        for kind, a, b in self.q:
            if kind == "w":
                e.wait_ge(a, b)
            else:
                ins = a(e)
                if b is not None:
                    ins.then_inc(b, 1)


class Banks(list):

    def __init__(self, x):
        super().__init__(x)
        self.held = [False] * len(x)

    def __setitem__(self, i, toks):
        self.held[i] = False
        super().__setitem__(i, toks)


def bc(ap, n):
    return ap.unsqueeze(2).broadcast_to([ap.shape[0], ap.shape[1], n])


def bm(ap, n):
    return ap.unsqueeze(1).broadcast_to([ap.shape[0], n, ap.shape[1]])


def weight_order():
    o = []
    for p in range(2):
        for j in range(3):
            for h in range(2):
                if (p, h) == (1, 0) and j != 1:
                    for c in ((0, 1), (), (2, 3))[j]:
                        o += [("wcfm", 4 + c), ("wcfm", c)]
                o.append(("wqkv", j * 4 + 2 * p + h))
    o += [("wmk", i) for i in range(8)]
    o += [("wgate", i) for i in range(4)]
    o += [("wmv", i) for i in range(8)]
    o += [("wout", i) for i in range(8)]
    o += [("wxq", i) for i in range(8)]
    o += [("wxo", i) for i in range(8)]
    for a, b in ((0, 8), (8, 16), (16, 22)):
        for j in range(a, b):
            o += [("wup", j), ("wup", 22 + j)]
        o += [("wdn", (a // 8) * 8 + i) for i in range(8)]
    for h in range(4):
        o += [("rqk", 4 * h + i) for i in range(4)]
        o += [("rv", 4 * h + i) for i in range(4)]
        o += [("rg", 4 * h + i) for i in range(4)]
        if h % 2:
            o += [("rout", (h // 2) * 8 + i) for i in range(8)]
    for p in range(4):
        o += [("sk", 2 * p), ("sk", 2 * p + 1), ("sq", 2 * p), ("sq", 2 * p + 1)]
        if p:
            o += [("sout", 4 * (p - 1) + i) for i in range(4)]
        o += [("sv", 4 * p + i) for i in range(4)]
        o += [("sg", 4 * p + i) for i in range(4)]
    o += [("sout", 12 + i) for i in range(4)]
    return o


def program(nc, A, out):
    root = ExitStack()
    with root:
        def sem(n):
            return root.enter_context(nc.semaphore(n))

        NPH = 6
        PE, AC, DV, GP = (Engine([sem(f"s_{n}{i}") for i in range(NPH)]) for n in ("pe", "act", "dve", "pool"))
        SY = Engine([sem("s_sy")])
        engines = (PE, AC, DV, GP)

        def alloc(stack, name, shape, dt=F32):
            return stack.enter_context(nc.sbuf_tensor(name, shape, dt))

        banks = [root.enter_context(nc.psum_tensor(f"ps{i}", [128, 512], F32)) for i in range(8)]
        bank_free = Banks([[] for _ in range(8)])
        bank_at = {}

        def bank(pool=(0, 1, 2, 3)):
            bank_at[pool] = bank_at.get(pool, -1) + 1
            i = pool[bank_at[pool] % len(pool)]
            assert not bank_free.held[i], i
            bank_free.held[i] = True
            return i, banks[i], bank_free[i]

        dma_sems = {}

        def load(name, dst, src, *after, eng=SY):
            s = dma_sems.get(name)
            if s is None:
                s = dma_sems[name] = [sem("d_" + name), 0]
            s[1] += 16
            sm, v = s[0], s[1]
            eng.wait(*after)
            eng.q.append(("d", (dst, src), sm))
            return (sm, v)

        RAW = [alloc(root, f"raw{i}", [128, SLAB]) for i in range(NRAW)]
        SH = [alloc(root, f"sh{i}", [128, SLAB], F32R) for i in range(NSPL)]
        SL = [alloc(root, f"sl{i}", [128, SLAB], F32R) for i in range(NSPL)]
        XH = alloc(root, "xh", [128, 8, T], F32R)
        XL = alloc(root, "xl", [128, 8, T], F32R)
        X2H = alloc(root, "x2h", [128, 8, T], F32R)
        X2L = alloc(root, "x2l", [128, 8, T], F32R)
        PRM = alloc(root, "prm", [128, NPRM])
        IDN = alloc(root, "idn", [128, 128])
        ONE = alloc(root, "one", [128, 128])
        RB = alloc(root, "rb", [128, T])
        RC = alloc(root, "rc", [128, 16])
        MSQ = alloc(root, "msq", [128, 16])
        NH = alloc(root, "nh", [128, 16])
        SQ = [alloc(root, f"sq{i}", [128, T]) for i in range(2)]
        DG = alloc(root, "dg", [128, T])

        def prm(n, i=0):
            return PRM[:, PCOL[n] + i:PCOL[n] + i + 1]

        t_prm = load("prm", PRM[:], A["prm"])
        t_cst = load("cst", IDN[:], A["cst"][0])
        t_cst = load("cst", ONE[:], A["cst"][1])
        t_nh = GP.do(lambda e: e.memset(NH[:], -0.5))

        order = weight_order()
        raw_free = [[] for _ in range(NRAW)]
        spl_free = [None] * NSPL
        raw_tok = {}
        spl_tok = {}
        st = {"dma": 0, "hi": 0, "lo": 0, "use": 0}

        def send(j):
            n, i = order[j]
            raw_tok[j] = load(f"w{j % NRAW}", RAW[j % NRAW][:], A[n][i], raw_free[j % NRAW])

        def sends():
            while st["dma"] < min(len(order), st["lo"] + NRAW):
                send(st["dma"])
                st["dma"] += 1

        def split_hi():
            j = st["hi"]
            r, s = j % NRAW, j % NSPL
            spl_tok[j] = [AC.do(lambda e: e.activation(SH[s][:], RAW[r][:], ACT.Copy), raw_tok[j], spl_free[s])]
            st["hi"] += 1

        def split_lo():
            j = st["lo"]
            r, s = j % NRAW, j % NSPL
            spl_tok[j].append(DV.do(lambda e: e.tensor_tensor(SL[s][:], RAW[r][:], SH[s][:].bitcast(F32),
                                                              ALU.subtract), spl_tok[j], raw_tok[j], spl_free[s]))
            raw_free[r] = list(spl_tok[j])
            st["lo"] += 1
            sends()

        def pump():
            top = min(len(order), st["use"] + NSPL)
            sends()
            while st["hi"] < top:
                while st["lo"] < st["hi"]:
                    split_lo()
                split_hi()

        def take(name, cols, off=0):
            j = st["use"] + off
            assert order[j][0] == name, (order[j], name)
            sends()
            while st["lo"] <= j:
                if st["hi"] == st["lo"]:
                    split_hi()
                split_lo()
            s = j % NSPL
            v = [x[s][:].rearrange("p (k c) -> p k c", c=cols) for x in (SH, SL)]
            return v[0], v[1], spl_tok[j], s

        def done(s, tok):
            spl_free[s] = tok
            st["use"] += 1
            pump()

        fills = []

        def tick():
            while fills:
                try:
                    next(fills[0])
                    return
                except StopIteration:
                    fills.pop(0)

        def drain():
            while fills:
                tick()

        side = []

        def side_tick():
            while side:
                try:
                    next(side[0])
                    return
                except StopIteration:
                    side.pop(0)

        small = []
        small_gp = []
        mb_ = {}

        def trickle(n=1):
            for _ in range(n):
                if small:
                    small.pop(0)()
            if small_gp and "r" in mb_:
                small_gp.pop(0)()

        def mm3(dst, ah, al, bh, bl, start, stop, *w, inc=False):
            PE.do(lambda e: e.matmul(dst, ah, bh, start=start, stop=False, skip_group_check=True), *w, inc=False)
            PE.do(lambda e: e.matmul(dst, ah, bl, start=False, stop=False, skip_group_check=True), inc=False)
            return PE.do(lambda e: e.matmul(dst, al, bh, start=False, stop=stop, skip_group_check=True), inc=stop or inc)

        def mm(dst, a, b, start, stop, *w, inc=None):
            return PE.do(lambda e: e.matmul(dst, a, b, start=start, stop=stop, skip_group_check=True), *w,
                         inc=stop if inc is None else inc)

        grain = {"t": 2, "s": 2}

        def pause(i, n):
            if (i + 1) * grain["t"] // n > i * grain["t"] // n:
                tick()
                trickle(grain["s"])
                side_tick()

        def proj_fm(name, dst, X, xt, nk, bw, N=T, mt=1, ks=None, after=None):
            wh, wl, wt, s = take(name, 128 * mt)
            ks = ks or range(nk)
            for m in range(mt):
                for n, k in enumerate(ks):
                    c = slice(m * 128, m * 128 + 128)
                    t = mm3(dst[m][:, 0:N], wh[:, k, c], wl[:, k, c], X[0][:, k, 0:N], X[1][:, k, 0:N],
                            n == 0, n == nk - 1, wt, xt[k], bw)
                    pause(m * nk + n, mt * nk)
            if after:
                after(t)
            done(s, t)
            return t

        def group(items, nk, N=T, mt=1, ks=None, pre=None, post=None, ticks=1):
            g = [take(it[0], 128 * mt, off) for off, it in enumerate(items)]
            out_t = [None] * len(items)
            for n, k in enumerate(ks or range(nk)):
                if pre:
                    pre(k)
                for i, (name, dst, X, xt, bw) in enumerate(items):
                    wh, wl, wt, s = g[i]
                    for m in range(mt):
                        c = slice(m * 128, m * 128 + 128)
                        mm(dst[m][:, 0:N], wh[:, k, c], X[0][:, k, 0:N], n == 0, False, wt, xt[k][0], bw)
                        mm(dst[m][:, 0:N], wl[:, k, c], X[0][:, k, 0:N], False, False)
                for i, (name, dst, X, xt, bw) in enumerate(items):
                    wh = g[i][0]
                    for m in range(mt):
                        c = slice(m * 128, m * 128 + 128)
                        out_t[i] = mm(dst[m][:, 0:N], wh[:, k, c], X[1][:, k, 0:N], False, n == nk - 1, xt[k])
                if post:
                    post(k)
                if n == 2:
                    pump()
                for _ in range(ticks):
                    tick()
                side_tick()
                trickle(grain["s"])
            for i in range(len(items)):
                done(g[i][3], out_t[i])
            return out_t

        def stream(items, evac, nk=8, ng=3, ks=None, pre=None, post=None, fin=None, mt=1):
            def banks_of():
                return [bank() for _ in range(mt)]
            if ng == 1 and not pre:
                ng = 0
            bb = [banks_of() for _ in range(ng)]
            tt = group([(nm, [x[1] for x in b], X, xt, [x[2] for x in b]) for (nm, X, xt), b in zip(items, bb)],
                       nk, mt=mt, ks=ks, pre=pre, post=post) if ng else []
            rest = list(items[ng:])
            held = list(zip(bb, tt))
            if fin:
                fin[0]()
                if rest and (ng + 1) * mt <= 4:
                    nm, X, xt = rest.pop(0)
                    b = banks_of()
                    held.append((b, proj_fm(nm, [x[1] for x in b], X, xt, nk, [x[2] for x in b], mt=mt)))
                fin[1]()
            for n, (b, t) in enumerate(held):
                evac(n, b, t)
            for n, (nm, X, xt) in enumerate(rest):
                b = banks_of()
                t = proj_fm(nm, [x[1] for x in b], X, xt, nk, [x[2] for x in b], mt=mt)
                evac(len(held) + n, b, t)

        def proj_tm(name, dst, X, xt, bw, evac, nb=NB):
            for g in range(4):
                wh, wl, wt, s = take(name, 512)
                for tb in range(nb):
                    for k in range(2):
                        kk = 2 * g + k
                        c = slice(tb * 128, tb * 128 + 128)
                        t = mm3(dst[tb][:], X[0][:, kk, c], X[1][:, kk, c], wh[:, k, :], wl[:, k, :],
                                kk == 0, kk == 7, wt, xt[kk], bw[tb], inc=(tb == nb - 1 and k == 1))
                    if g == 3:
                        evac(tb, t)
                    pause(tb, nb)
                done(s, t)

        PE.wait(t_cst)
        AC.q.append(("i", lambda e: e.preload_act_table_set("natural_log_exp_and_others"), None))
        for e_ in (AC, DV, GP):
            e_.wait(t_prm, t_cst)
        GP.wait(t_nh)
        DV.wait(t_nh)

        sq_free = [None, None]
        sq_at = [0]

        def colsum(src, col0, dst, first, last, N, srct, bw=None):
            i = sq_at[0] % 2
            sq_at[0] += 1
            a = AC.do(lambda e: e.activation(SQ[i][:, 0:N], src, ACT.Square), srct, sq_free[i])

            def sums():
                for tb in range(N // 128):
                    t = mm(dst[:, col0 + tb:col0 + tb + 1], SQ[i][:, tb * 128:tb * 128 + 128], ONE[:, 0:1],
                           first and tb == 0, last, a, bw, inc=(tb == N // 128 - 1))
                sq_free[i] = t
                return t
            return sums

        dg_free = [None]
        SA = DG
        sa_free = dg_free
        sa = {}

        def sqsum(src, k, dst, srct, bw):
            i = sq_at[0] % 2
            if k:
                sq_at[0] += 1
            o = SQ[i] if k else SA
            a = AC.do(lambda e: e.activation(o[:], src, ACT.Square), srct, sq_free[i] if k else sa_free[0])
            if k == 0:
                sa["t"] = a
            elif k < 7:
                sa["t"] = sq_free[i] = GP.do(lambda e: e.tensor_tensor(SA[:], SA[:], o[:], ALU.add), a, sa["t"])
            else:
                def sums():
                    for n, (q, w) in enumerate(((SA, sa["t"]), (o, a))):
                        for tb in range(NB):
                            t = mm(dst[:, tb:tb + 1], q[:, tb * 128:tb * 128 + 128], ONE[:, 0:1], n == 0 and tb == 0,
                                   n == 1, w, bw, inc=(tb == NB - 1))
                        if n == 0:
                            sa_free[0] = t
                    sq_free[i] = t
                    return t
                return sums

        rc_free = {}

        def rstd(src, n, t, scale, col=0):
            m, r = MSQ[:, col:col + n], RC[:, col:col + n]
            d = DV.do(lambda e: e.tensor_scalar(m, src, scale, EPS, ALU.mult, ALU.add), t, rc_free.get(col))
            g = GP.do(lambda e: e.tensor_tensor(r, m, NH[:, 0:n], ALU.pow), d)
            rc_free[col] = g
            return d, g

        def diag(col, nb, ct):
            return DV.do(lambda e: e.tensor_tensor(DG[:, 0:nb * 128].rearrange("p (a b) -> p a b", b=128),
                                                   bm(IDN[:], nb), bc(col, 128), ALU.mult), ct, dg_free[0])

        def rows_mm(nb, d, bw, dst):
            t = mm(dst, ONE[:], DG[:, 0:nb * 128], True, True, d, bw)
            dg_free[0] = t
            return t

        def rows(col, nb, ct, bw, dst):
            return rows_mm(nb, diag(col, nb, ct), bw, dst)

        rb_free = [[]]

        def fin_a(bi, bk, t, nb):
            d, g = rstd(bk[:, 0:nb], nb, t, 1.0 / 1024)
            bank_free[bi] = [d]
            return g, diag(RC[:, 0:nb], nb, g)

        def fin_b(d, nb, rb, pool=(6,)):
            i2, b2, w2 = bank(pool)
            t2 = rows_mm(nb, d, w2, b2[:, 0:nb * 128])
            if rb is None:
                return i2, b2, t2
            c = DV.do(lambda e: e.tensor_copy(rb[:, 0:nb * 128], b2[:, 0:nb * 128]), t2, rb_free[0])
            bank_free[i2] = [c]
            return c

        def scaled(src, g, k, XXH, XXL, tk, N=T, free=None):
            a = AC.do(lambda e: e.activation(XXH[:, k, 0:N], src, ACT.Copy, scale=g), tk, free)
            d = DV.do(lambda e: e.scalar_tensor_tensor(XXL[:, k, 0:N], src, g, XXH[:, k, 0:N].bitcast(F32),
                                                       ALU.mult, ALU.subtract), a, tk, free)
            return [a, d]

        def scaled_copy(n, dst, b, c, *w):
            if n % 2:
                return DV.do(lambda e: e.tensor_scalar(dst, b[:], c, None, ALU.mult), *w)
            return AC.do(lambda e: e.activation(dst, b[:], ACT.Copy, scale=c), *w)

        late = []

        def flush_late():
            while late:
                late.pop(0)()

        def parts(src, k, XXH, XXL, tk, free=None, late=None):
            toks = [AC.do(lambda e: e.activation(XXH[:, k, :], src, ACT.Copy), tk, free)]

            def low():
                toks.append(DV.do(lambda e: e.tensor_tensor(XXL[:, k, :], src, XXH[:, k, :].bitcast(F32),
                                                            ALU.subtract), toks, tk, free))
            if late is None:
                low()
            else:
                late.append(low)
            return toks

        keepA = ExitStack()
        QK0 = alloc(keepA, "qk0", [128, 4, T])
        ACC = alloc(keepA, "acc", [128, 4, T])
        KM = alloc(keepA, "km", [128, 8, 256])
        KQ = KM[:].rearrange("p (a b) m -> p a (b m)", b=2)
        VM = QK0[:].rearrange("p a t -> p (a t)").rearrange("p (b c) -> p b c", b=2)
        ph = ExitStack()
        CP = alloc(ph, "cp", [128, 4, T + 32])
        QK1 = alloc(ph, "qk1", [128, 4, T])
        CM = alloc(ph, "cm", [128, 2, 128])
        CH = alloc(ph, "ch", [128, len(CSH), 64])
        UNIT = {n: alloc(ph, n, [128, w]) for n, w in (("u_bv", 1024), ("u_kbe", 1024), ("u_kd", 1024), ("u_f1", 1024),
                                                       ("u_f2", 1024), ("u_a", 512), ("u_l", 512), ("u_tt", 512))}
        GT = alloc(ph, "gt", [128, 4, T])
        PAD = alloc(ph, "pad", [128, T + 4])
        CA = [alloc(ph, f"ca{i}", [128, T]) for i in range(2)]
        VF = alloc(ph, "vf", [128, T])
        SG = VF
        MRB = CM[:].rearrange("p a b -> p (a b)")
        SS = alloc(ph, "ss", [128, 2, 128])
        SMV = alloc(ph, "smv", [128, 160])
        WAB = alloc(ph, "wab", [128, 64])
        WABH = alloc(ph, "wabh", [128, 64], F32R)
        WABL = alloc(ph, "wabl", [128, 64], F32R)
        LNC = alloc(ph, "lnc", [128, 16])
        OLN = alloc(ph, "oln", [128, 16])
        EG = alloc(ph, "eg", [128, 2, 8])

        xsrc = A["xT"].rearrange("(k p) t -> p k t", p=128)
        def load_x(i):
            return load(f"x{i}", (QK0, ACC)[i // 2][:, 2 * (i % 2):2 * (i % 2) + 2, :], xsrc[:, 2 * i:2 * i + 2, :])

        t_x = [load_x(0)]
        sends()
        t_x += [load_x(i) for i in (1, 2, 3)]
        t_wab = load("wab", WAB[:], A["wab"])
        t_m = load("mem", GT[:].rearrange("p a (b t) -> p (a b) t", t=256),
                   A["memT"].rearrange("(k p) t -> p k t", p=128))
        t_cm = load("cm", CM[:], A["cst"][2:].rearrange("n p c -> p n c"))
        t_ch = load("ch", CH[:], A["csh"])
        cst = {n: CM[:, i, :] for i, n in enumerate(CST[2:])}
        csh = {n: CH[:, i, :] for i, n in enumerate(CSH)}

        zp = [GP.do(lambda e: e.memset(PAD[:, 0:4], 0.0))]
        zp.append(GP.do(lambda e: e.memset(CP[:, :, 0:32], 0.0)))
        zp.append(GP.do(lambda e: e.memset(SS[:], 0.0)))
        t_ss0 = zp[-1]

        def xk(k):
            return (QK0, ACC)[k // 4][:, k % 4, :]

        X = (XH, XL)
        xt = [None] * 8
        sx = {}
        st_b = bank((7,))

        def x_pre(k):
            xt[k] = scaled(xk(k), prm("norm_g", k), k, XH, XL, t_x[k // 2])
            sx[k] = colsum(xk(k), 0, st_b[1], k == 0, k == 7, T, t_x[k // 2], st_b[2])

        def x_post(k):
            if k == 5:
                split_wab()
            sx["t"] = sx[k]()

        def x_fin_a():
            sx["g"], sx["d"] = fin_a(st_b[0], st_b[1], sx["t"], 4)
            x_read.extend([AC.last(), DV.last()])

        def x_fin_b():
            sx["r"] = fin_b(sx["d"], 4, RB)

        x_read = []
        pad_free = [[]]
        ca_at = [0]
        ca_free = [None, None]
        vf_free = [[]]
        unit_free = {}

        def evac_conv(tile, dst, extra, put, i, b, t):
            pi = ca_at[0] % 2
            ca_at[0] += 1
            P, C = PAD, CA[pi]
            d = DV.do(lambda e: e.tensor_tensor(P[:, 4:4 + T], b[:], RB[:], ALU.mult), t, sx["r"], pad_free[0], zp)
            bank_free[i] = [d]
            s_ = {"d": d}

            def tap(j):
                w = prm("gconv", tile * 4 + j)
                if j == 0:
                    s_["d"] = DV.do(lambda e: e.tensor_scalar(C[:], P[:, 1:1 + T], w, None, ALU.mult), s_["d"],
                                    ca_free[pi])
                else:
                    s_["d"] = DV.do(lambda e: e.scalar_tensor_tensor(C[:], P[:, 1 + j:1 + j + T], w, C[:], ALU.mult,
                                                                     ALU.add), s_["d"])
                if j == 3:
                    pad_free[0] = [s_["d"]]
                    a = AC.do(lambda e: e.activation(dst, C[:], ACT.Silu), s_["d"], extra)
                    ca_free[pi] = a
                    put(a)
            for j in range(4):
                tap(j)

        bv_t = [[None, None], [None, None]]
        o_t = [[], []]
        qk_t = [[None] * 4, [None] * 4]
        QKS = (QK0, QK1)

        def v4(x):
            return x.rearrange("p (h b c) -> p h b c", h=2, b=NB)

        u_done = []

        def gdn(p, QK, qk_t, out_t):
            UB, UKB, UKD, F1, F2, UA, UL, UTT = (UNIT[n][:] for n in
                                                 ("u_bv", "u_kbe", "u_kd", "u_f1", "u_f2", "u_a", "u_l", "u_tt"))
            UT, UX = F1[:, 0:512], F1[:, 512:1024]
            LM = [F2[:, 0:512], F2[:, 512:1024]]
            g3 = lambda x: x.rearrange("p (g c) -> p g c", c=64)
            h3 = lambda x, h: x[:, h * T:h * T + T].rearrange("p (b c) -> p b c", c=128)
            hd = lambda x, h: x[:, h * T:h * T + T]
            gch = lambda i, h: sv3(i)[:, :, 2 * p + h]
            RR = (slice(0, 64), slice(64, 128))
            chunks = [(h, tb, par) for h in range(2) for tb in range(NB) for par in range(2)]
            uf = unit_free.get
            KB0, KB1, KD0, KD1 = UKB[:, 0:512], UKB[:, 512:1024], UKD[:, 0:512], UKD[:, 512:1024]

            def dia(dst, col, ct, free):
                return DV.do(lambda e: e.tensor_tensor(dst.rearrange("p (a b) -> p a b", b=128), bm(IDN[:], 4),
                                                       bc(col, 128), ALU.mult), ct, free)

            bi, bk, bw = bank((4, 5))
            for n in range(4):
                f = colsum(QK[:, n, :], 4 * n, bk, n == 0, True, T, qk_t[n], bw)
                yield
                t = f()
            d, g = rstd(bk[:, 0:16], 16, t, 1.0)
            bank_free[bi] = [d]
            DGC, DBE = (UL, UTT), (F2[:, 512:1024], UA)
            if p == 0:
                cumsums()
            bd = [dia(DBE[h], gch(2, h), lg["beta"], uf(("u_f2", "u_a")[h])) for h in range(2)]
            gd = [dia(DGC[h], gch(3, h), lg["gc"], uf(("u_l", "u_tt")[h])) for h in range(2)]
            nd = [dia((KD0, KD1, KB0, KB1)[n], RC[:, 4 * n:4 * n + 4], g, uf(("u_kd", "u_kbe")[n // 2]))
                  for n in (2, 3, 0, 1)]
            kb = [None, None]
            nt = [None] * 4
            for m, n in enumerate((2, 3, 0, 1)):
                yield
                i2, b2, w2 = bank((4, 5))
                t = mm(b2[:], ONE[:], (KD0, KD1, KB0, KB1)[n], True, True, nd[m], w2)
                if n < 2:
                    nt[n] = DV.do(lambda e, n=n, b2=b2: e.scalar_tensor_tensor(
                        QK[:, n, :], QK[:, n, :], 128.0 ** -0.5, b2[:], ALU.mult, ALU.mult), t, qk_t[n])
                else:
                    nt[n] = DV.do(lambda e, n=n, b2=b2: e.tensor_tensor(QK[:, n, :], QK[:, n, :], b2[:], ALU.mult),
                                  t, qk_t[n])
                bank_free[i2] = [nt[n]]
                if n >= 2:
                    h = n - 2
                    yield
                    i2, b2, w2 = bank((4, 5))
                    t = mm(b2[:], ONE[:], DBE[h], True, True, bd[h], w2)
                    kb[h] = DV.do(lambda e, h=h, b2=b2: e.tensor_tensor(hd(F2, h), QK[:, 2 + h, :], b2[:], ALU.mult),
                                  t, nt[2 + h], uf("u_f2"))
                    bank_free[i2] = [kb[h]]
            while len(f1_read) < 2 * p + 2:
                if vq:
                    vq.pop(0)()
                yield
            ea_ = [None, None]
            dd = []
            for h in range(2):
                yield
                i2, b2, w2 = bank((4, 5))
                t = mm(b2[:], ONE[:], DGC[h], True, True, gd[h], w2)
                for par in range(2):
                    R = RR[par]
                    dst = g3(UA[R, h * 256:h * 256 + 256])
                    src = b2[R, :].rearrange("p (b q c) -> p b q c", q=2, c=64)[:, :, par, :]
                    d = DV.do(lambda e, R=R, dst=dst, src=src, h=h: e.tensor_tensor(
                        dst, src, bc(gch(3, h)[R], 64), ALU.subtract), t, uf("u_a"))
                    dd.append(d)
                ea_[h] = AC.do(lambda e, h=h, b2=b2: e.activation(hd(F1, h), b2[:], ACT.Exp), t, d, uf("u_f1"),
                               f1_read)
                bank_free[i2] = [ea_[h]]
            a = AC.do(lambda e: e.activation(UA, UA, ACT.Relu, scale=-1.0), dd)
            a = AC.do(lambda e: e.activation(UA, UA, ACT.Exp, scale=-1.0), a)
            mk = GP.do(lambda e: e.tensor_tensor(g3(UA), g3(UA), bm(csh["mc"], 8), ALU.mult), a, t_ch)
            lm = GP.do(lambda e: e.tensor_tensor(g3(UL), g3(UA), bm(csh["ms"], 8), ALU.mult), mk, uf("u_l"))
            yield
            i3, b3, w3 = bank((4, 5))
            for n, (h, tb, par) in enumerate(chunks):
                c = slice(tb * 128 + par * 64, tb * 128 + par * 64 + 64)
                o = (h * 4 + tb) * 64
                t = mm(b3[RR[par], o:o + 64], QK[:, 2 + h, c], hd(F2, h)[:, c], True, True, kb, w3, nt[2 + h],
                       inc=n == 15)
            lt = DV.do(lambda e, b3=b3: e.tensor_tensor(UL, UL, b3[:], ALU.mult), t, lm)
            bank_free[i3] = [lt]
            kb_read = t
            yield
            d = DV.do(lambda e: e.scalar_tensor_tensor(g3(UTT), g3(UL), -1.0, bm(csh["m1t"], 8), ALU.mult, ALU.mult),
                      lt, uf("u_tt"), t_ch)
            tt = DV.do(lambda e: e.tensor_tensor(g3(UTT), g3(UTT), bm(csh["id64"], 8), ALU.add), d)
            i3, b3, w3 = bank((4, 5))
            for n, (h, tb, par) in enumerate(chunks):
                c = slice(tb * 128 + par * 64, tb * 128 + par * 64 + 64)
                o = (h * 4 + tb) * 64
                t = mm(b3[RR[par], o:o + 64], QK[:, 2 + h, c], QK[:, h, c], True, True, w3, nt[h], inc=n == 15)
            at = DV.do(lambda e, b3=b3: e.tensor_tensor(UA, UA, b3[:], ALU.mult), t, lm)
            bank_free[i3] = [at]
            qe = []
            for h in range(2):
                qe.append(DV.do(lambda e, h=h: e.tensor_tensor(QK[:, h, :], QK[:, h, :], hd(F1, h), ALU.mult),
                                ea_[h], t))
                eg = DV.do(lambda e, h=h: e.tensor_copy(EG[:, h, :], hd(F1, h)[:, 63:T:64]), ea_[h], uf("eg"))
            lmt = [GP.do(lambda e: e.tensor_tensor(g3(LM[0]), g3(UL), bm(csh["m2t"], 8), ALU.mult), lt, kb_read),
                   None]
            yield
            i3, b3, w3 = bank((4, 5))
            for n, (h, tb, par) in enumerate(chunks):
                o = (h * 4 + tb) * 64
                R = RR[par]
                t = mm(b3[R, o:o + 64], UTT[R, o:o + 64], csh["id64"][R, :], True, True, w3, tt, inc=n == 15)
            tl = AC.do(lambda e, b3=b3: e.activation(UT, b3[:], ACT.Copy), t, qe, eg)
            bank_free[i3] = [tl]
            xfree = [qe[1], eg]
            k_tm = []

            def keys(h):
                i3, b3, w3 = bank((4, 5))
                for tb in range(NB):
                    c = slice(tb * 128, tb * 128 + 128)
                    t = PE.do(lambda e, c=c: e.transpose(b3[:, c], QK[:, 2 + h, c], IDN[:]), w3, nt[2 + h])
                b33 = b3[:].rearrange("p (b c) -> p b c", c=128)
                DV.do(lambda e: e.tensor_tensor(h3(UKB, h), b33, bc(gch(6, h), 128), ALU.mult), t, uf("u_kbe"))
                k2 = DV.do(lambda e: e.tensor_tensor(h3(UKD, h), b33, bc(gch(7, h), 128), ALU.mult), t, uf("u_kd"))
                bank_free[i3] = [k2]
                k_tm.append(k2)

            for n_, s in enumerate((2, 4, 8, 16, 32)):
                yield
                if n_ < 2:
                    keys(n_)
                M_ = LM[n_ % 2]
                i3, b3, w3 = bank((4, 5))
                for n, (h, tb, par) in enumerate(chunks):
                    o = (h * 4 + tb) * 64
                    R = RR[par]
                    t = mm(b3[R, o:o + 64], M_[R, o:o + 64], UT[R, o:o + 64], True, True, w3, tl, lmt[n_ % 2],
                           inc=n == 15)
                xx = DV.do(lambda e, b3=b3: e.scalar_tensor_tensor(g3(UX), g3(b3[:]), -1.0, bm(csh["id64"], 8),
                                                                   ALU.mult, ALU.add), t, xfree)
                bank_free[i3] = [xx]
                if s < 32:
                    nm = f"m{2 * s}t"
                    lmt[(n_ + 1) % 2] = GP.do(lambda e, n_=n_, nm=nm: e.tensor_tensor(
                        g3(LM[(n_ + 1) % 2]), g3(UL), bm(csh[nm], 8), ALU.mult), t)
                yield
                i4, b4, w4 = bank((4, 5))
                for n, (h, tb, par) in enumerate(chunks):
                    o = (h * 4 + tb) * 64
                    R = RR[par]
                    t2 = mm(b4[R, o:o + 64], UX[R, o:o + 64], UTT[R, o:o + 64], True, True, w4, xx, tt, inc=n == 15)
                if s < 32:
                    i3, b3, w3 = bank((4, 5))
                    for n, (h, tb, par) in enumerate(chunks):
                        o = (h * 4 + tb) * 64
                        R = RR[par]
                        t2 = mm(b3[R, o:o + 64], UTT[R, o:o + 64], UX[R, o:o + 64], True, True, w3, inc=n == 15)
                tt = DV.do(lambda e, b4=b4: e.tensor_copy(UTT, b4[:]), t2)
                bank_free[i4] = [tt]
                if s < 32:
                    tl = AC.do(lambda e, b3=b3: e.activation(UT, b3[:], ACT.Copy), t2)
                    bank_free[i3] = [tl]
                xfree = [t2]
            yield
            ut = []
            for h in range(2):
                i3, b3, w3 = bank((4, 5))
                for tb in range(NB):
                    for par in range(2):
                        R = RR[par]
                        o = (h * 4 + tb) * 64
                        t = mm(b3[R, tb * 128:tb * 128 + 128], UTT[R, o:o + 64], hd(UB, h)[R, tb * 128:tb * 128 + 128],
                               True, True, w3, tt, bv_t[p][h], inc=tb == 3 and par == 1)
                ut.append(AC.do(lambda e, h=h, b3=b3: e.activation(hd(F1, h), b3[:], ACT.Copy), t, xx))
                bank_free[i3] = [ut[h]]
                yield
            wt = []
            for par in range(2):
                i3, b3, w3 = bank((4, 5))
                R = RR[par]
                for h in range(2):
                    for tb in range(NB):
                        o = (h * 4 + tb) * 64
                        t = mm(b3[:, o:o + 64], hd(UKB, h)[R, tb * 128:tb * 128 + 128], UTT[R, o:o + 64], True, True,
                               w3, k_tm, tt, inc=h == 1 and tb == 3)
                dst = F2.rearrange("p (g q c) -> p g q c", q=2, c=64)[:, :, par, :]
                wt.append(AC.do(lambda e, dst=dst, b3=b3: e.activation(dst, g3(b3[:]), ACT.Copy), t))
                bank_free[i3] = [wt[par]]
                yield
            VN = QK[:, 2:4, :].rearrange("p h (b c) -> p h b c", c=128)
            U4 = v4(F1)
            i4, po, w4 = bank((6,))
            i5, po1, w5 = bank((7,))
            P2 = [po, po1]
            if p:
                z = GP.do(lambda e: e.memset(SS[:], 0.0), u_done)
            else:
                z = t_ss0
            s_t = [z, z]
            for n in range(8):
                tb, par = n // 2, n % 2
                R = RR[par]
                cc = slice(n * 64, n * 64 + 64)
                i3, b3, w3 = bank((4, 5))
                for h in range(2):
                    t = mm(b3[R, h * 128:h * 128 + 128], hd(F2, h)[:, cc], SS[:, h, :], True, True, w3, wt, s_t[h])
                vn = DV.do(lambda e, R=R, tb=tb, b3=b3: e.tensor_tensor(
                    VN[R, :, tb, :], U4[R, :, tb, :], b3[R, 0:256].rearrange("p (h c) -> p h c", h=2),
                    ALU.subtract), t, ut, kb_read)
                bank_free[i3] = [vn]
                for h in range(2):
                    mm(P2[h][:, cc], SS[:, h, :], QK[:, h, cc], True, False, s_t[h], qe[h], w4, w5)
                yield
                i3, b3, w3 = bank((4, 5))
                for h in range(2):
                    tk = mm(b3[:, h * 128:h * 128 + 128], hd(UKD, h)[R, tb * 128:tb * 128 + 128], VN[R, h, tb, :],
                            True, True, vn, w3)
                for h in range(2):
                    o = (h * 4 + tb) * 64
                    to = mm(P2[h][:, cc], VN[R, h, tb, :], UA[R, o:o + 64], False, True, at)
                for h in range(2):
                    s_t[h] = DV.do(lambda e, h=h, n=n, b3=b3: e.scalar_tensor_tensor(
                        SS[:, h, :], SS[:, h, :], EG[:, h, n:n + 1], b3[:, h * 128:h * 128 + 128], ALU.mult,
                        ALU.add), tk, to, eg)
                bank_free[i3] = [s_t[1]]
                yield
            ot = []
            for h in range(2):
                ot.append(AC.do(lambda e, h=h: e.activation(QK[:, h, :], P2[h][:], ACT.Copy), to))
            bank_free[i4] = [ot[0]]
            bank_free[i5] = [ot[1]]
            u_done.extend([PE.last(), DV.last(), AC.last()])
            for n in list(UNIT) + ["eg"]:
                unit_free[n] = [PE.last(), DV.last(), AC.last()]
            out_t.extend(ot)

        f1_read = []
        vq = []

        def v_tm(p, h, a):
            i, b, w = bank((3,) if p else (4, 5))
            for tb in range(NB):
                c = slice(h * T + tb * 128, h * T + tb * 128 + 128)
                o = slice(tb * 128, tb * 128 + 128)
                t = PE.do(lambda e, c=c, o=o: e.transpose(b[:, o], UNIT["u_f1"][:, c], IDN[:]), w, a)
            f1_read.append(t)
            dst = UNIT["u_bv"][:, h * T:h * T + T].rearrange("p (b c) -> p b c", c=128)

            def scale():
                bv_t[p][h] = DV.do(lambda e: e.tensor_tensor(dst, b[:].rearrange("p (b c) -> p b c", c=128),
                                                             bc(sv3(2)[:, :, 2 * p + h], 128), ALU.mult), t,
                                   unit_free.get("u_bv"))
                bank_free[i] = [bv_t[p][h]]
            scale()

        def put_qk(p, n):
            def put(a):
                qk_t[p][n] = a
            return put

        def qkv_item(p, n, b, t):
            i, b_, _ = b
            j, h = n // 2, n % 2
            if j < 2:
                evac_conv(j * 4 + 2 * p + h, QKS[p][:, n, :], x_read, put_qk(p, n), i, b_, t)
            else:
                evac_conv(8 + 2 * p + h, UNIT["u_f1"][:, h * T:h * T + T], unit_free.get("u_f1"),
                          lambda a: vq.append(lambda: v_tm(p, h, a)), i, b_, t)

        ABT = VF[0:8, :]
        ab = SMV[:, 0:32].rearrange("p (b c) -> p b c", c=8)

        def sv(i, n=16):
            return SMV[:, 32 + i * 16:32 + i * 16 + n]

        def sv3(i):
            return sv(i).rearrange("p (b h) -> p b h", h=4)

        lg = {}

        def split_wab():
            a = AC.do(lambda e: e.activation(WABH[:], WAB[:], ACT.Copy), t_wab)
            d = DV.do(lambda e: e.tensor_tensor(WABL[:], WAB[:], WABH[:].bitcast(F32), ALU.subtract), a, t_wab)
            lg["w"] = [a, d]

        def logits():
            i, b, w = bank()
            for k in range(8):
                c = slice(8 * k, 8 * k + 8)
                t = mm3(b[0:8, :], WABH[:, c], WABL[:, c], XH[:, k, :], XL[:, k, :], k == 0, k == 7, w, xt[k],
                        lg["w"])
            lg["t"] = DV.do(lambda e: e.tensor_tensor(ABT, b[0:8, :], RB[0:8, :], ALU.mult), t, sx["r"])
            bank_free[i] = [lg["t"]]

        def decay():
            i, b, w = bank()
            for tb in range(NB):
                t = PE.do(lambda e, tb=tb: e.transpose(b[:, tb * 8:tb * 8 + 8], ABT[:, tb * 128:tb * 128 + 128],
                                                       IDN[0:8, 0:8]), lg["t"], w)
            vf_free[0] = [t]
            d = DV.do(lambda e: e.tensor_copy(SMV[:, 0:32], b[:, 0:32]), t)
            bank_free[i] = [d]
            av = ab[:, :, 0:4]
            d = DV.do(lambda e: e.tensor_tensor(av, av, bm(PRM[:, PCOL["dtb"]:PCOL["dtb"] + 4], 4), ALU.add), d)
            a4 = AC.do(lambda e: e.activation(sv3(2), ab[:, :, 4:8], ACT.Sigmoid), d)
            AC.q.append(("i", lambda e: e.preload_act_table_set("natural_log_exp_and_others"), None))
            ea = AC.do(lambda e: e.activation(LNC[:, 12:16], PRM[:, PCOL["alog"]:PCOL["alog"] + 4], ACT.Exp))
            a1 = AC.do(lambda e: e.activation(sv3(0), av, ACT.Abs), d)
            a2 = AC.do(lambda e: e.activation(sv(0), sv(0), ACT.Exp, scale=-1.0), a1)
            a3 = AC.do(lambda e: e.activation(sv(0), sv(0), ACT.Ln, bias=1.0), a2)
            d1 = DV.do(lambda e: e.scalar_tensor_tensor(sv3(1), av, 0.0, sv3(0), ALU.max, ALU.add), a3, d)
            lg["g"] = DV.do(lambda e: e.scalar_tensor_tensor(sv3(1), sv3(1), -1.0, bm(LNC[:, 12:16], 4), ALU.mult,
                                                             ALU.mult), d1, ea)
            lg["beta"] = a4

        def cumsums():
            i, b, w = bank((6,))
            mm(b[:, 0:16], cst["tri"], sv(1), True, True, lg["g"], w, t_cm, inc=False)
            t = mm(b[:, 16:32], cst["blk"], sv(1), False, True)
            d3 = DV.do(lambda e: e.tensor_copy(SMV[:, 80:112], b[:, 0:32]), t)
            bank_free[i] = [d3]
            a5 = AC.do(lambda e: e.activation(sv(5), sv(3), ACT.Exp), d3)
            d4 = DV.do(lambda e: e.tensor_tensor(sv(6), sv(5), sv(2), ALU.mult), a5, lg["beta"])
            d5 = DV.do(lambda e: e.tensor_tensor(sv(7), sv(4), sv(3), ALU.subtract), d3)
            a6 = AC.do(lambda e: e.activation(sv(7), sv(7), ACT.Exp), d5)
            sm_t = [d4, a6, lg["beta"], d3]
            DV.wait(*sm_t, t_ch)
            AC.wait(*sm_t)
            lg["gc"] = d3

        def item0(n, b, t):
            if n == 4:
                PE.wait(t_ch)
                grain["t"], grain["s"] = 4, 1
                fills.append(gdn(0, QK0, qk_t[0], o_t[0]))
                tick()
            qkv_item(0, n, b[0], t)
            if n == 2:
                logits()
            elif n == 3:
                decay()

        stream([("wqkv", X, xt)] * 6, item0, pre=x_pre, post=x_post, fin=(x_fin_a, x_fin_b))
        t_rc, t_rb = sx["g"], sx["r"]

        MXH = X2H[:, 4:8, :].rearrange("p k (a t) -> p (k a) t", a=2)
        MXL = X2L[:, 4:8, :].rearrange("p k (a t) -> p (k a) t", a=2)
        mt_ = [None] * 8
        gt_free = []
        mb_["b"] = bank((7,))

        def mk(k):
            return GT[:, k // 2, (k % 2) * 256:(k % 2) * 256 + 256]

        def mem_tile(k):
            mt_[k] = scaled(mk(k), prm("mem_g", k), k, MXH, MXL, t_m, N=256)
            mb_[k] = AC.do(lambda e: e.activation(KM[:, k, :], mk(k), ACT.Square), t_m)

        def mem_rms():
            _, bk, bw = mb_["b"]
            for k in range(8):
                for tb in range(2):
                    t = mm(bk[:, tb:tb + 1], KM[:, k, tb * 128:tb * 128 + 128], ONE[:, 0:1], k == 0 and tb == 0,
                           k == 7, mb_[k], bw)
            d = DV.do(lambda e: e.tensor_scalar(LNC[:, 0:2], bk[:, 0:2], 1.0 / 1024, EPS, ALU.mult, ALU.add), t)
            mb_["g"] = GP.do(lambda e: e.tensor_tensor(LNC[:, 2:4], LNC[:, 0:2], NH[:, 0:2], ALU.pow), d)
            bank_free[7] = [d]
            gt_free.extend([AC.last(), DV.last()])

        def mem_rows():
            mb_["d"] = DV.do(lambda e: e.tensor_tensor(KM[:, 0, :].rearrange("p (a b) -> p a b", b=128),
                                                       bm(IDN[:], 2), bc(LNC[:, 2:4], 128), ALU.mult), mb_["g"])

        def mem_rows2():
            i2, b2, w2 = bank((7,))
            t = mm(b2[:, 0:256], ONE[:], KM[:, 0, :], True, True, mb_["d"], w2)
            mb_["r"] = DV.do(lambda e: e.tensor_copy(MRB, b2[:, 0:256]), t, lg["gc"])
            bank_free[i2] = [mb_["r"]]

        small.extend([lambda k=k: mem_tile(k) for k in range(8)] + [mem_rms, mem_rows, mem_rows2])

        acc_t = [None] * 4
        ON_GP = (1, 2)
        tmp_free = [None, None]
        tmps = [KQ[:, 2, :], KQ[:, 3, :]]

        def cfm_conv_gp(c, tk):
            stt = {}

            def one(j):
                w = prm("cw", c * 31 + j)
                src = CP[:, c, 2 + j:2 + j + T]
                if j == 0:
                    stt["t"] = AC.do(lambda e: e.activation(ACC[:, c, :], src, ACT.Identity, scale=w, bias=prm("cb", c)),
                                     tk, x_read)
                else:
                    tmp = tmps[j % 2]
                    a = AC.do(lambda e: e.activation(tmp, src, ACT.Copy, scale=w), tk, mb_["r"], tmp_free[j % 2])
                    stt["t"] = tmp_free[j % 2] = GP.do(lambda e: e.tensor_tensor(ACC[:, c, :], ACC[:, c, :], tmp,
                                                                                 ALU.add), a, stt["t"])
                acc_t[c] = stt["t"]
            return [lambda j=j: one(j) for j in range(31)]

        def cfm_conv(c, tk):
            stt = {"t": tk}

            def one(j):
                w = prm("cw", c * 31 + j)
                src = CP[:, c, 2 + j:2 + j + T]
                if j == 0:
                    stt["t"] = DV.do(lambda e: e.tensor_scalar(ACC[:, c, :], src, w, prm("cb", c), ALU.mult,
                                                               ALU.add), stt["t"], x_read)
                else:
                    stt["t"] = DV.do(lambda e: e.scalar_tensor_tensor(ACC[:, c, :], src, w, ACC[:, c, :],
                                                                      ALU.mult, ALU.add), stt["t"])
                acc_t[c] = stt["t"]
            return [lambda j=j: one(j) for j in range(31)]

        def glu(c):
            i, b, w = bank()
            t = proj_fm("wcfm", [b], X, xt, 8, w)
            d = DV.do(lambda e, b=b: e.tensor_tensor(SG[:], b[:], RB[:], ALU.mult), t, t_rb, vf_free[0])
            bank_free[i] = [d]
            a = AC.do(lambda e: e.activation(SG[:], SG[:], ACT.Sigmoid), d)
            i, b, w = bank()
            t = proj_fm("wcfm", [b], X, xt, 8, w)
            cpv = CP[:, c, 32:32 + T]
            d = DV.do(lambda e, b=b, v=cpv: e.tensor_tensor(v, b[:], RB[:], ALU.mult), t, t_rb)
            bank_free[i] = [d]
            d = DV.do(lambda e, v=cpv: e.tensor_tensor(v, v, SG[:], ALU.mult), d, a, zp)
            vf_free[0] = [d]
            if c in ON_GP:
                small_gp.extend(cfm_conv_gp(c, d))
            else:
                small.extend(cfm_conv(c, d))

        glu(0)
        glu(1)

        for n in range(4):
            b = bank()
            qkv_item(1, n, b, proj_fm("wqkv", [b[1]], X, xt, 8, b[2]))

        glu(2)
        glu(3)
        b4, b5 = bank(), bank()
        t4 = proj_fm("wqkv", [b4[1]], X, xt, 8, b4[2])
        drain()
        fills.append(gdn(1, QK1, qk_t[1], o_t[1]))
        tick()
        qkv_item(1, 4, b4, t4)
        t5 = proj_fm("wqkv", [b5[1]], X, xt, 8, b5[2])
        qkv_item(1, 5, b5, t5)

        DV.wait(*[t for t in tmp_free if t])
        tmps[:] = [CA[0][:], CA[1][:]]
        for i in range(2):
            tmp_free[i] = [ca_free[i]]

        km_t = []
        grain["t"], grain["s"] = 2, 2
        for m in range(8):
            i, b, w = bank((0, 1, 2))
            t = proj_fm("wmk", [b], (MXH, MXL), mt_, 8, w, N=256)
            km_t.append(DV.do(lambda e, b=b, m=m: e.tensor_tensor(KM[:, m, :], b[:, 0:256], MRB, ALU.mult), t,
                              mb_["r"]))
            bank_free[i] = [km_t[-1]]

        grain["t"], grain["s"] = 4, 1
        gt_t = []
        for c in range(4):
            i, b, w = bank((0, 1, 2))
            t = proj_fm("wgate", [b], X, xt, 8, w)
            d = DV.do(lambda e, b=b, c=c: e.tensor_tensor(GT[:, c, :], b[:], RB[:], ALU.mult), t, gt_free)
            bank_free[i] = [d]
            gt_t.append(AC.do(lambda e, c=c: e.activation(GT[:, c, :], GT[:, c, :], ACT.Silu), d))

        mem_read = []

        def cfm_norm():
            while small or small_gp:
                trickle(2)
                yield
            bi, bk, bw = bank((3,))
            for c in range(4):
                for tb in range(NB):
                    t = mm(bk[:, tb:tb + 1], ACC[:, c, tb * 128:tb * 128 + 128], ONE[:, 0:1], c == 0 and tb == 0,
                           c == 3, acc_t[c], bw)
            d = DV.do(lambda e, bk=bk: e.tensor_scalar(LNC[:, 4:8], bk[:, 0:4], 1.0 / 512, None, ALU.mult), t)
            bank_free[bi] = [d]
            dg = diag(LNC[:, 4:8], 4, d)
            yield
            i2, b2, w2 = bank((3,))
            t = rows_mm(4, dg, w2, b2[:])
            xs = []
            for c in range(4):
                xs.append(DV.do(lambda e, c=c, b2=b2: e.tensor_tensor(ACC[:, c, :], ACC[:, c, :], b2[:],
                                                                      ALU.subtract), t, acc_t[c]))
            bank_free[i2] = [xs[-1]]
            yield
            bi, bk, bw = bank((3,))
            pend = None
            for c in range(4):
                f = colsum(ACC[:, c, :], 0, bk, c == 0, c == 3, T, xs[c], bw)
                if pend:
                    pend()
                pend = f
            t = pend()
            d = DV.do(lambda e, bk=bk: e.tensor_scalar(LNC[:, 4:8], bk[:, 0:4], 1.0 / 512, EPS, ALU.mult, ALU.add), t)
            g = GP.do(lambda e: e.tensor_tensor(LNC[:, 8:12], LNC[:, 4:8], NH[:, 0:4], ALU.pow), d)
            bank_free[bi] = [d]
            dg = diag(LNC[:, 8:12], 4, g)
            yield
            i2, b2, w2 = bank((3,))
            t = rows_mm(4, dg, w2, b2[:])
            while not mem_read:
                yield
            for c in range(4):
                yield
                d = DV.do(lambda e, c=c, b2=b2: e.scalar_tensor_tensor(ACC[:, c, :], ACC[:, c, :], prm("lg", c), b2[:],
                                                                       ALU.mult, ALU.mult), t)
                a = AC.do(lambda e, c=c: e.activation(ACC[:, c, :], ACC[:, c, :], ACT.Silu, bias=prm("lb", c)), d)
                mix_t[4 + c] = parts(ACC[:, c, :], 4 + c, X2H, X2L, a, mem_read)
            bank_free[i2] = [d]

        mix_t = [None] * 8
        fin_t = [None] * 4

        def gdn_out(p):
            QK = QKS[p]
            while len(o_t[p]) < 2:
                yield
            bi, bk, bw = bank((3,))
            f = [colsum(QK[:, h, :], 4 * h, bk, h == 0, True, T, o_t[p][h], bw) for h in range(2)]
            yield
            t = [x() for x in f]
            d = DV.do(lambda e: e.tensor_scalar(OLN[:, 0:8], bk[:, 0:8], 1.0 / 128, EPS, ALU.mult, ALU.add), t)
            g = GP.do(lambda e: e.tensor_tensor(OLN[:, 8:16], OLN[:, 0:8], NH[:, 0:8], ALU.pow), d)
            bank_free[bi] = [d]
            for h in range(2):
                dg = diag(OLN[:, 8 + 4 * h:12 + 4 * h], 4, g)
                yield
                hh = 2 * p + h
                i2, b2, w2 = bank((3,))
                t = rows_mm(4, dg, w2, b2[:])
                d = DV.do(lambda e, h=h, b2=b2: e.scalar_tensor_tensor(QK[:, h, :], QK[:, h, :], prm("gn"), b2[:],
                                                                       ALU.mult, ALU.mult), t, o_t[p][h])
                bank_free[i2] = [d]
                fin_t[hh] = DV.do(lambda e, h=h, hh=hh: e.tensor_tensor(GT[:, hh, :], QK[:, h, :], GT[:, hh, :],
                                                                        ALU.mult), d, gt_t[hh])
                yield

        def head_parts(k):
            mix_t[k] = parts(GT[:, k, :], k, X2H, X2L, fin_t[k])

        side.append(gdn_out(0))
        vm_t = []
        v_free = []
        grain["t"], grain["s"] = 2, 2
        for cg in range(2):
            bb = [bank((0, 1, 2)) for _ in range(2)]

            def vm_evac(tb, t, bb=bb, cg=cg):
                if cg == 0 and tb == 0:
                    while side:
                        side_tick()
                    v_free.extend([AC.last(), DV.last(), PE.last()])
                    side.append(cfm_norm())
                i, b, w = bb[tb]
                vm_t.append(AC.do(lambda e: e.activation(VM[:, tb, cg * 512:cg * 512 + 512], b[:], ACT.Copy,
                                                         scale=LNC[:, 2 + tb:3 + tb]), t, v_free, mb_["g"]))
                bank_free[i] = [vm_t[-1]]

            proj_tm("wmv", [x[1] for x in bb], (MXH, MXL), mt_, [x[2] for x in bb], vm_evac, nb=2)
            if cg == 0:
                for k in range(2):
                    head_parts(k)
        mem_read.append(PE.last())
        def wout_pre(k):
            while (fin_t if k < 4 else mix_t)[k] is None:
                tick()
                side_tick()
            if k < 4 and mix_t[k] is None:
                head_parts(k)

        side.append(gdn_out(1))
        grain["t"], grain["s"] = 2, 2
        wout_b = [bank((0, 1, 2)) for _ in range(3)]
        wout_t = group([("wout", [b[1]], (X2H, X2L), mix_t, [b[2]]) for b in wout_b], 8, ks=[0, 1, 4, 5, 6, 7, 2, 3],
                       pre=wout_pre, ticks=2)
        assert not fills and not small

        end_m = [e_.last() for e_ in engines]
        ph.close()

        def phase():
            for e_ in (AC, DV, GP):
                e_.wait(end_m)

        ph = ExitStack()
        phase()
        for e_ in engines:
            e_.next_phase()

        def y_evac(k, b, i, t, first, last, ystate):
            f = None
            if last and k == 0:
                ystate["bank"] = bank((7,))
            if first:
                if last:
                    bi, bk, bw = ystate["bank"]
                    f = sqsum(b[:], k, bk, t, bw)
                yt = AC.do(lambda e: e.activation(Y[:, k, :], b[:], ACT.Copy), t, y_free[0])
            else:
                yt = DV.do(lambda e: e.tensor_tensor(Y[:, k, :], Y[:, k, :], b[:], ALU.add), t, ystate["t"][k])
                if last:
                    bi, bk, bw = ystate["bank"]
                    f = sqsum(Y[:, k, :], k, bk, yt, bw)
            ystate["t"][k] = yt
            bank_free[i] = [yt]
            if last:
                ystate["pend"] = f

        y_free = [[]]

        class Boundary:

            def __init__(self, ystate, gpost, hts, pres):
                self.ys, self.gpost, self.hts, self.pres = ystate, gpost, hts, pres
                self.xts = [[None] * 8 for _ in pres]
                bi, bk, bw = ystate["bank"]
                g, d = fin_a(bi, bk, ystate["pend"](), 4)
                self.i2, self.b2, self.t2 = fin_b(d, 4, None)
                if pres:
                    self.sb = bank((7,))
                self.ht = [None] * 8

            def pre(self, k):
                if k == 0:
                    self.first(0)
                    self.second(0)
                if k < 7:
                    self.first(k + 1)
                if k:
                    self.second(k)

            def second(self, k):
                for n, (g, XXH, XXL, free) in enumerate(self.pres):
                    self.xts[n][k].append(DV.do(lambda e, g=g, XXH=XXH, XXL=XXL: e.scalar_tensor_tensor(
                        XXL[:, k, :], H[:, k, :], prm(g[0], g[1] + k), XXH[:, k, :].bitcast(F32), ALU.mult,
                        ALU.subtract), self.xts[n][k], self.ht[k], free))

            def first(self, k):
                b2, gp = self.b2, self.gpost
                d = DV.do(lambda e: e.scalar_tensor_tensor(Y[:, k, :], Y[:, k, :], prm(gp[0], gp[1] + k), b2[:],
                                                           ALU.mult, ALU.mult), self.t2, self.ys["t"][k])
                if k == 7:
                    bank_free[self.i2] = [d]
                E = GP if not self.pres and k in (1, 3, 5) else DV
                d = E.do(lambda e: e.tensor_tensor(H[:, k, :], H[:, k, :], Y[:, k, :], ALU.add), d, self.hts[k])
                self.ht[k] = d
                if k == 7:
                    y_free[0] = [d]
                for n, (g, XXH, XXL, free) in enumerate(self.pres):
                    self.xts[n][k] = [AC.do(lambda e, g=g, XXH=XXH: e.activation(
                        XXH[:, k, :], H[:, k, :], ACT.Copy, scale=prm(g[0], g[1] + k)), d, free)]
                if self.pres:
                    self.f = sqsum(H[:, k, :], k, self.sb[1], d, self.sb[2])

            def post(self, k):
                if k == 7:
                    self.t = self.f()

            def a(self):
                rb_free[0] = [DV.last(), AC.last()]
                self.g, self.d = fin_a(self.sb[0], self.sb[1], self.t, 4)

            def b(self):
                self.r = fin_b(self.d, 4, RB)

            def kw(self):
                return dict(pre=self.pre, post=self.post, fin=(self.a, self.b))

        H = alloc(ph, "h", [128, 8, T])
        Y = alloc(ph, "y", [128, 8, T])
        X2 = (X2H, X2L)

        def y_stream(name, xt_, nk, first, last, ys, ks=None, pre=None):
            stream([(name, X2, xt_)] * 8, lambda m, b, t: y_evac(m, b[0][1], b[0][0], t, first, last, ys), nk=nk,
                   ks=ks, pre=pre)

        grain["t"], grain["s"] = 2, 2
        ys = {"t": [None] * 8}
        for m in range(8):
            if m < 3:
                b, t = wout_b[m], wout_t[m]
            else:
                b = bank((m % 4,))
                t = proj_fm("wout", [b[1]], X2, mix_t, 8, b[2])
            y_evac(m, b[1], b[0], t, True, True, ys)
        hts = [load(f"h{i}", H[:, 2 * i:2 * i + 2, :], xsrc[:, 2 * i:2 * i + 2, :], end_m) for i in range(4)]
        hts = [hts[k // 2] for k in range(8)]
        xt_free = [PE.last()]
        B = Boundary(ys, ("norm_g", 8), hts, [(("norm_g", 16), XH, XL, xt_free)])
        xt = B.xts[0]

        pa = ExitStack()
        QX = [alloc(pa, f"qx{i}", [128, 2, T]) for i in range(2)]
        PM = [alloc(pa, f"pm{i}", [128, NB, 256]) for i in range(2)]
        PT = alloc(pa, "pt", [128, 2, T])
        SX = alloc(pa, "sx", [128, 16])
        o_x = [None] * 8
        ax = {"q": [[], []], "pt": [], "sx": [], "pm": [[], []]}

        def attend(h, qt):
            Q = QX[h % 2]
            Pm = PM[h % 2]
            pe_ = []
            for u in range(2):
                i, b, w = bank((4, 5))
                for v in range(2):
                    c = slice((2 * u + v) * 128, (2 * u + v) * 128 + 128)
                    for d_ in range(2):
                        t = mm(b[:, v * 256:v * 256 + 256], Q[:, d_, c], KM[:, 2 * h + d_, :], d_ == 0, d_ == 1, w,
                               qt[d_], km_t[2 * h + d_])
                d = DV.do(lambda e, u=u, b=b: e.tensor_reduce(SX[:, 2 * u:2 * u + 2],
                                                              b[:].rearrange("p (v m) -> p v m", v=2), AXX,
                                                              ALU.max), t, ax["sx"])
                d = DV.do(lambda e, u=u: e.tensor_scalar(SX[:, 4 + 2 * u:6 + 2 * u], SX[:, 2 * u:2 * u + 2], -1.0 / 16,
                                                         None, ALU.mult), d)
                for v in range(2):
                    tb = 2 * u + v
                    a = AC.do(lambda e, tb=tb, v=v, b=b: e.activation(
                        Pm[:, tb, :], b[:, v * 256:v * 256 + 256], ACT.Exp, scale=1.0 / 16,
                        bias=SX[:, 4 + tb:5 + tb], accum_out=SX[:, 8 + tb:9 + tb]), d, ax["pm"][h % 2])
                    pe_.append(a)
                bank_free[i] = [a]
                yield
            ax["q"][h % 2] = [t]
            r = DV.do(lambda e: e.reciprocal(SX[:, 12:16], SX[:, 8:12]), pe_)
            n_ = DV.do(lambda e: e.tensor_tensor(Pm[:], Pm[:], bc(SX[:, 12:16], 256), ALU.mult), r)
            ax["sx"] = [n_]
            for _ in range(3):
                yield
            pt = []
            for mb in range(2):
                i, b, w = bank((4, 5))
                for tb in range(NB):
                    t = PE.do(lambda e, tb=tb, mb=mb, b=b: e.transpose(
                        b[:, tb * 128:tb * 128 + 128], Pm[:, tb, mb * 128:mb * 128 + 128], IDN[:]), w, n_)
                pt.append(AC.do(lambda e, mb=mb, b=b: e.activation(PT[:, mb, :], b[:], ACT.Copy), t, ax["pt"]))
                bank_free[i] = [pt[-1]]
            ax["pm"][h % 2] = [t]
            yield
            for et in range(2):
                i, b, w = bank((4, 5))
                for mb in range(2):
                    c = slice(h * 256 + et * 128, h * 256 + et * 128 + 128)
                    t = mm(b[:], VM[:, mb, c], PT[:, mb, :], mb == 0, mb == 1, w, pt[mb], vm_t)
                o_x[2 * h + et] = parts(b[:], 2 * h + et, X2H, X2L, t, xo_free)
                bank_free[i] = list(o_x[2 * h + et])
            ax["pt"] = [t]
            yield

        xo_free = [xt_free]
        qts = [[None, None] for _ in range(4)]

        def xq_evac(m, b, t):
            i, b_, _ = b[0]
            h, d_ = m // 2, m % 2
            if d_ == 0:
                while len(fills) > 1:
                    tick()
            qts[h][d_] = DV.do(lambda e: e.tensor_tensor(QX[h % 2][:, d_, :], b_[:], RB[:], ALU.mult), t, B.r,
                               ax["q"][h % 2])
            bank_free[i] = [qts[h][d_]]
            if d_:
                fills.append(attend(h, qts[h]))

        grain["t"] = 4
        stream([("wxq", (XH, XL), xt)] * 8, xq_evac, **B.kw())
        grain["t"] = 2
        hts = B.ht
        ys = {"t": [None] * 8}
        while len(fills) > 1:
            tick()
        y_stream("wxo", o_x, 8, True, True, ys, pre=lambda k: drain() if k == 6 else None)
        xt_free = [PE.last()]
        end_m = [e_.last() for e_ in engines]
        pa.close()
        phase()
        for e_ in engines:
            e_.next_phase()
        B = Boundary(ys, ("norm_g", 24), hts, [(("norm_g", 32), XH, XL, xt_free)])
        xt = B.xts[0]

        pf = ExitStack()
        UP = [alloc(pf, f"up{i}", [128, T + 4]) for i in range(4)]
        UC = [alloc(pf, f"uc{i}", [128, T]) for i in range(4)]
        zu = [GP.do(lambda e, u=u: e.memset(u[:, 0:4], 0.0)) for u in UP]
        up_free = [[] for _ in range(4)]
        uc_free = [[] for _ in range(4)]
        ys = {"t": [None] * 8}
        m_free = [PE.last()]
        mid = [None] * 8
        ab_ = {}

        def up_evac(a0, m, b, t):
            i, b_, _ = b[0]
            j, half = a0 + m // 2, m % 2
            n = m % 4
            ch = j + 22 * half
            U, C = UP[n], UC[n]
            d = DV.do(lambda e: e.tensor_tensor(U[:, 4:4 + T], b_[:], RB[:], ALU.mult), t, B.r, up_free[n], zu)
            bank_free[i] = [d]
            if half == 0:
                flush_late()
            d = DV.do(lambda e: e.tensor_scalar(C[:], U[:, 2:2 + T], prm("fw", ch * 3), prm("fb", ch), ALU.mult,
                                                ALU.add), d, uc_free[n])
            for q in (1, 2):
                d = DV.do(lambda e, q=q: e.scalar_tensor_tensor(C[:], U[:, 2 + q:2 + q + T], prm("fw", ch * 3 + q),
                                                                C[:], ALU.mult, ALU.add), d)
            up_free[n] = [d]
            if half == 0:
                ab_[0] = (AC.do(lambda e: e.activation(C[:], C[:], ACT.Silu), d), C, n)
                return
            ta, Ca, na = ab_[0]
            d = DV.do(lambda e: e.tensor_tensor(Ca[:], Ca[:], C[:], ALU.mult), ta, d)
            uc_free[na] = mid[j - a0] = parts(Ca[:], j - a0, X2H, X2L, d, m_free, late=late)
            uc_free[n] = [d]

        for part, (a0, b0) in enumerate(((0, 8), (8, 16), (16, 22))):
            stream([("wup", (XH, XL), xt)] * (2 * (b0 - a0)), lambda m, b, t, a0=a0: up_evac(a0, m, b, t),
                   **(B.kw() if part == 0 else {}))
            flush_late()
            y_stream("wdn", mid, b0 - a0, part == 0, part == 2, ys)
            m_free = [PE.last()]
        hts = B.ht
        xt_free = [PE.last()]
        end_m = [e_.last() for e_ in engines]
        pf.close()
        phase()
        for e_ in engines:
            e_.next_phase()
        B = Boundary(ys, ("norm_g", 40), hts, [(("rpre", 0), XH, XL, xt_free)])
        xt = B.xts[0]

        pr = ExitStack()
        CS = alloc(pr, "cs", [128, 2, T])
        DD = alloc(pr, "dd", [128, T])
        QR, KR = KQ[:, 0:2, :], KQ[:, 2:4, :]
        TM = [alloc(pr, f"tm{i}", [128, T]) for i in range(3)]
        SC = alloc(pr, "sc", [128, 1280])
        VR, GR = QK0, ACC
        BN = alloc(pr, "bn", [128, NB, 10])
        SOFF = [0, 512, 896, 1152]
        t_cs = load("cs", CS[:], A["rope"], end_m)
        tm_free = [[], [], []]
        free = {"qk": [], "v": [], "sc": [], "g": [], "dd": [], "bn": []}
        o_r = [None] * 8
        x2_free = [[PE.last()]]

        def rot(dst, ops):
            a, c = ops
            cos, sin = CS[:, 0, :], CS[:, 1, :]
            d1 = DV.do(lambda e: e.tensor_tensor(dst[:, 0, :], TM[0][:], cos, ALU.mult), a, t_cs, free["qk"])
            d2 = DV.do(lambda e: e.tensor_tensor(TM[2][:], TM[1][:], sin, ALU.mult), c, tm_free[2])
            d3 = DV.do(lambda e: e.tensor_tensor(dst[:, 0, :], dst[:, 0, :], TM[2][:], ALU.subtract), d1, d2)
            d4 = DV.do(lambda e: e.tensor_tensor(dst[:, 1, :], TM[0][:], sin, ALU.mult), a)
            d5 = DV.do(lambda e: e.tensor_tensor(TM[2][:], TM[1][:], cos, ALU.mult), d3)
            d6 = DV.do(lambda e: e.tensor_tensor(dst[:, 1, :], dst[:, 1, :], TM[2][:], ALU.add), d4, d5)
            tm_free[0] = [d4]
            tm_free[1] = [d5]
            tm_free[2] = [d6]
            return [d3, d6]

        def retain(h, qt, kt, vt, gt, t_dd):
            sc = []
            for s in range(NB):
                n = (4 - s) * 128
                i, b, w = bank((4, 5))
                for d_ in range(2):
                    t = mm(b[:, 0:n], KR[:, d_, s * 128:s * 128 + 128], QR[:, d_, s * 128:T], d_ == 0, d_ == 1, w, qt,
                           kt)
                sc.append(DV.do(lambda e, s=s, n=n, b=b: e.tensor_tensor(SC[:, SOFF[s]:SOFF[s] + n], b[:, 0:n],
                                                                         DD[:, 0:n], ALU.mult), t, t_dd,
                                free["sc"]))
                bank_free[i] = [sc[-1]]
                yield
            free["qk"] = [t]
            free["dd"] = [sc[-1]]
            while gt[0] is None:
                yield
            gg = []
            for tb in range(NB):
                i, b, w = bank((6, 7))
                for s in range(tb + 1):
                    t = mm(b[:], SC[:, SOFF[s] + (tb - s) * 128:SOFF[s] + (tb - s) * 128 + 128], VR[:, s, :], s == 0,
                           s == tb, w, sc, vt[s])
                s6, ag, rs = BN[:, tb, 0:6], BN[:, tb, 6:8], BN[:, tb, 8:9]
                d = DV.do(lambda e, b=b, s6=s6: e.bn_stats(s6, b[:]), t, free["bn"])
                d = DV.do(lambda e, s6=s6, ag=ag: e.bn_aggr(ag, s6), d)
                d = DV.do(lambda e, tb=tb: e.tensor_scalar(BN[:, tb, 9:10], BN[:, tb, 7:8], EPS, None, ALU.add), d)
                g = GP.do(lambda e, tb=tb, rs=rs: e.tensor_tensor(rs, BN[:, tb, 9:10], NH[:, 0:1], ALU.pow), d)
                yield
                c = DV.do(lambda e, tb=tb, b=b, rs=rs: e.tensor_scalar(
                    SQB[tb % 2][:], b[:], BN[:, tb, 6:7], rs, ALU.subtract, ALU.mult), g, d, sqb_free[tb % 2])
                bank_free[i] = [c]
                c = DV.do(lambda e, tb=tb: e.tensor_tensor(GR[:, tb, :], GR[:, tb, :], SQB[tb % 2][:], ALU.mult), c,
                          gt[tb])
                sqb_free[tb % 2] = [c]
                gg.append(c)
            free["v"] = [t]
            free["sc"] = [t]
            free["bn"] = [gg[-1]]
            yield
            yield
            for et in range(4):
                i, b, w = bank((4, 5))
                for tb in range(NB):
                    t = PE.do(lambda e, tb=tb, et=et, b=b: e.transpose(
                        b[:, tb * 128:tb * 128 + 128], GR[:, tb, et * 128:et * 128 + 128], IDN[:]), w, gg[tb])
                kk = (h % 2) * 4 + et
                o_r[kk] = parts(b[:], kk, X2H, X2L, t, x2_free[0])
                bank_free[i] = list(o_r[kk])
                if et % 2:
                    yield
            free["g"] = [t]

        SQB = [alloc(pr, f"sqb{i}", [128, T]) for i in range(2)]
        sqb_free = [[], []]
        ys = {"t": [None] * 8}
        for h in range(4):
            two = []
            qkt = []

            def rqk_evac(n, b, t, two=two, qkt=qkt):
                m_ = n % 2
                a = DV.do(lambda e: e.tensor_tensor(TM[m_][:], b[0][1][:], RB[:], ALU.mult), t, B.r, tm_free[m_])
                bank_free[b[0][0]] = [a]
                two.append(a)
                if n % 2:
                    qkt.append(rot((QR, KR)[n // 2], two[-2:]))

            stream([("rqk", (XH, XL), xt)] * 4, rqk_evac, ng=3 if h == 0 else 1, **(B.kw() if h == 0 else {}))
            qt, kt = qkt
            t_rc = B.g
            drain()
            t_dd = load("dd", DD[:], A["rdec"][h], free["dd"], end_m)
            res = []
            for j, nm in enumerate(("rv", "rg")):
                bb = [bank() for _ in range(4)]
                r_ = []

                def evac(tb, t, j=j, bb=bb, r_=r_):
                    i, b, w = bb[tb]
                    if j == 0:
                        a = scaled_copy(tb, VR[:, tb, :], b, RC[:, tb:tb + 1], t, t_rc, free["v"])
                    else:
                        a = AC.do(lambda e: e.activation(GR[:, tb, :], b[:], ACT.Silu, scale=RC[:, tb:tb + 1]), t,
                                  t_rc, free["g"])
                    bank_free[i] = [a]
                    r_.append(a)

                proj_tm(nm, [x[1] for x in bb], (XH, XL), xt, [x[2] for x in bb], evac)
                res.append(r_)
                if j == 0:
                    gt = [None] * 4
                    fills.append(retain(h, qt, kt, r_, gt, t_dd))
                else:
                    for tb in range(NB):
                        gt[tb] = r_[tb]
            if h % 2:
                y_stream("rout", o_r, 8, h == 1, h == 3, ys, pre=lambda k: drain() if k == 4 else None)
                x2_free[0] = [PE.last()]
        hts = B.ht
        xt_free = [PE.last()]
        end_m = [e_.last() for e_ in engines]
        pr.close()
        phase()
        for e_ in engines:
            e_.next_phase()
        B = Boundary(ys, ("rpost", 0), hts, [(("kvn", 0), XH, XL, xt_free), (("spre", 0), X2H, X2L, xt_free)])
        xk_t, xs_t = B.xts

        sbs = ExitStack()
        MH = alloc(sbs, "mh", [128, 4, T], F32R)
        ML = alloc(sbs, "ml", [128, 4, T], F32R)
        KS, QS = KQ[:, 0:2, :], KQ[:, 2:4, :]
        VS, GS = QK0, ACC
        ZZS = [alloc(sbs, f"zz{i}", [128, 1280]) for i in range(2)]
        SP = alloc(sbs, "sp", [128, 1280])
        BIG = alloc(sbs, "big", [128, 128])
        LOW = alloc(sbs, "low", [128, 128])
        t_big = load("big", BIG[:], A["sbc"][0], end_m)
        t_low = load("big", LOW[:], A["sbc"][1])
        free = {"k": [], "q": [], "v": [], "g": [[], [], [], []], "z": [[], []], "sp": []}
        m_free = [[]]
        o_s = [None] * 4
        AC.q.append(("i", lambda e: e.preload_act_table_set("natural_log_exp_and_others"), None))

        sb = {"busy": False, "z": 0}

        def stick(h, kt, qt, vt, gt):
            ZZ = ZZS[h]
            zt = []
            for s in range(NB):
                n = (4 - s) * 128
                i, b, w = bank((4, 5))
                t = mm(b[:, 0:n], KS[:, h, s * 128:s * 128 + 128], QS[:, h, s * 128:T], True, True, w, kt, qt)
                o = SOFF[s]
                d = DV.do(lambda e, o=o, b=b: e.tensor_tensor(ZZ[:, o:o + 128], b[:, 0:128], BIG[:], ALU.min), t,
                          t_big, free["z"][h])
                zt.append(d)
                if n > 128:
                    a = AC.do(lambda e, o=o, n=n, b=b: e.activation(ZZ[:, o + 128:o + n], b[:, 128:n], ACT.Copy), t,
                              free["z"][h], d)
                    zt.append(a)
                    bank_free[i] = [d, a]
                else:
                    bank_free[i] = [d]
                if s % 2:
                    yield
            if h:
                free["k"] = [t]
            sb["z"] += 1
            a = AC.do(lambda e: e.activation(SP[:], ZZ[:], ACT.Abs), zt, free["sp"])
            a = AC.do(lambda e: e.activation(SP[:], SP[:], ACT.Exp, scale=-1.0), a)
            a = AC.do(lambda e: e.activation(SP[:], SP[:], ACT.Ln, bias=1.0), a)
            sp = DV.do(lambda e: e.scalar_tensor_tensor(SP[:], ZZ[:], 0.0, SP[:], ALU.max, ALU.add), a, zt)
            for _ in range(4):
                yield
            wt = []
            for s in range(NB):
                n = (4 - s) * 128
                i, b, w = bank((4, 5))
                for j in range(s, NB):
                    m = (4 - j) * 128
                    t = mm(b[:, n - m:n], LOW[:] if j == s else ONE[:], SP[:, SOFF[j]:SOFF[j] + m], j == s, j == 3, w,
                           sp, t_low)
                o = SOFF[s]
                d = DV.do(lambda e, o=o, n=n, b=b: e.tensor_tensor(ZZ[:, o:o + n], ZZ[:, o:o + n], b[:, 0:n],
                                                                   ALU.subtract), t, sp)
                bank_free[i] = [d]
                wt.append(AC.do(lambda e, o=o, n=n: e.activation(ZZ[:, o:o + n], ZZ[:, o:o + n], ACT.Exp), d))
                if s % 2:
                    yield
            free["sp"] = [t]
            for et in range(2):
                while sb["busy"] or gt[2 * h + et] is None:
                    yield
                i, b, w = bank((6, 7))
                for s in range(NB):
                    n = (4 - s) * 128
                    t = mm(b[:, T - n:T], VS[:, s, h * 256 + et * 128:h * 256 + et * 128 + 128],
                           ZZ[:, SOFF[s]:SOFF[s] + n], s == 0, s == 3, w, wt[s], vt[s])
                kk = 2 * h + et
                d = DV.do(lambda e, kk=kk, b=b: e.tensor_tensor(GS[:, kk, :], GS[:, kk, :], b[:], ALU.mult), t,
                          gt[kk])
                bank_free[i] = [d]
                o_s[kk] = parts(GS[:, kk, :], kk, MH, ML, d, m_free[0])
                free["g"][kk] = list(o_s[kk])
                yield
            free["z"][h] = [t]
            if h:
                free["v"] = [t]

        ys = {"t": [None] * 8}

        def sout(part):
            def evac(n, b, t):
                for m in range(2):
                    y_evac(2 * n + m, b[m][1], b[m][0], t, part == 0, part == 3, ys)
            stream([("sout", (MH, ML), o_s)] * 4, evac, nk=4, ng=2 if part == 3 else 1, mt=2,
                   pre=(lambda k: drain() if k == 2 else None) if part == 3 else None)
            m_free[0] = [PE.last()]

        XS, XK = (X2H, X2L), (XH, XL)
        for p in range(4):
            kt, qt, gt = [], [], [None] * 4

            def kq_evac(n, b, t, p=p, kt=kt, qt=qt):
                while sb["z"] < 2 * p:
                    tick()
                i, b_, _ = b[0]
                h = n % 2
                if n < 2:
                    kt.append(DV.do(lambda e: e.tensor_tensor(KS[:, h, :], b_[:], RB[:], ALU.mult), t, B.r,
                                    free["k"]))
                    bank_free[i] = kt[-1:]
                else:
                    qt.append(DV.do(lambda e: e.scalar_tensor_tensor(QS[:, h, :], b_[:], 128.0 ** -0.5, RB[:],
                                                                     ALU.mult, ALU.mult), t, free["k"]))
                    bank_free[i] = qt[-1:]

            stream([("sk", XK, xk_t)] * 2 + [("sq", XS, xs_t)] * 2, kq_evac, ng=3 if p == 0 else 1,
                   **(B.kw() if p == 0 else {}))
            t_rc = B.g
            drain()
            vt = []
            fills.append(stick(0, kt, qt, vt, gt))
            fills.append(stick(1, kt, qt, vt, gt))
            if p:
                sb["busy"] = True
                sout(p - 1)
                sb["busy"] = False
            bb = [bank() for _ in range(4)]

            def v_evac(tb, t):
                vt.append(scaled_copy(1, VS[:, tb, :], bb[tb][1], RC[:, tb:tb + 1], t, t_rc, free["v"]))
                bank_free[bb[tb][0]] = [vt[-1]]

            proj_tm("sv", [x[1] for x in bb], XK, xk_t, [x[2] for x in bb], v_evac)
            for kk in range(4):
                i, b, w = bank()

                def g_evac(t):
                    d = DV.do(lambda e, kk=kk, b=b: e.tensor_tensor(GS[:, kk, :], b[:], RB[:], ALU.mult), t,
                              free["g"][kk])
                    bank_free[i] = [d]
                    gt[kk] = AC.do(lambda e, kk=kk: e.activation(GS[:, kk, :], GS[:, kk, :], ACT.Silu), d)

                proj_fm("sg", [b], XS, xs_t, 8, w, after=g_evac)
        while len(fills) > 1 or o_s[1] is None:
            tick()
        sout(3)
        F = Boundary(ys, ("spost", 0), B.ht, [])
        osrc = out.rearrange("(k p) t -> p k t", p=128)
        ot = []
        for k in range(8):
            F.pre(k)
            if k % 2:
                ot.append(load(f"h{k // 2}", osrc[:, k - 1:k + 1, :], H[:, k - 1:k + 1, :], F.ht[k - 1], F.ht[k]))
        SY.wait(*ot)
        sbs.close()
        ph.close()
        keepA.close()

        block = root.enter_context(nc.Block())

        @block.sync
        def _(e):
            for kind, a, b in SY.q:
                if kind == "w":
                    e.wait_ge(a, b)
                else:
                    e.dma_start(a[0], a[1]).then_inc(b, 16)

        @block.tensor
        def _(e):
            PE.emit(e)

        @block.scalar
        def _(e):
            AC.emit(e)

        @block.vector
        def _(e):
            DV.emit(e)

        @block.gpsimd
        def _(e):
            GP.emit(e)


def constants():
    i = np.arange(128)
    p, c = i[:, None], i[None, :]
    same = (p // 64) == (c // 64)
    m = {"ident": p == c, "ones": np.ones((128, 128), bool), "tri": same & (p <= c), "blk": same}
    cst = np.stack([m[n].astype(np.float32) for n in CST])
    p, c = p % 64, c[:, :64]
    m = {"id64": p == c, "mc": p <= c, "ms": p < c, "m1t": (p // 2 == c // 2) & (p < c)}
    for s in (2, 4, 8, 16, 32):
        m[f"m{s}t"] = (p // (2 * s) == c // (2 * s)) & ((c // s) % 2 == 1) & ((p // s) % 2 == 0)
    csh = np.stack([m[n].astype(np.float32) for n in CSH], 1)
    p = i[:, None]
    c = i[None, :]
    half = 128
    inv = (1.0 / (np.float32(10000.0) ** (np.arange(half, dtype=np.float32) / np.float32(half)))).astype(np.float32)
    ang = (np.arange(T, dtype=np.float32)[None, :] * inv[:, None]).astype(np.float32)
    rope = np.stack([np.cos(ang.astype(np.float64)), np.sin(ang.astype(np.float64))], 1).astype(np.float32)
    rd = []
    for h in range(4):
        lg = np.log1p(-np.exp2(-5.0 - h))
        diff = np.arange(T)[None, :] - p
        rd.append(np.where(diff >= 0, np.exp(lg * np.maximum(diff, 0)), 0.0) / 16.0)
    rdec = np.stack(rd).astype(np.float32)
    sbc = np.stack([np.where(p < c, np.float32(3e38), np.float32(-30000.0)), (p >= c).astype(np.float32)])
    return {"cst": cst, "csh": csh, "rope": np.ascontiguousarray(rope), "rdec": rdec, "sbc": sbc.astype(np.float32)}


def cols(v):
    v = np.asarray(v)
    return v.reshape(-1, 128).T


def fm(w, nk=8):
    K, N = w.shape
    return w.reshape(K // 128 // nk, nk, 128, N // 128, 128).transpose(0, 3, 2, 1, 4).reshape(-1, 128, nk * 128)


def tm(w):
    K, N = w.shape
    return w.reshape(K // 256, 2, 128, N // 512, 512).transpose(3, 0, 2, 1, 4).reshape(-1, 128, 1024)


def kernel(**inputs):
    import concourse.bacc as _bacc
    from concourse.bass_utils import run_bass_kernel_spmd as _run

    I = {k: np.asarray(v) for k, v in inputs.items()}
    w_in = I["w_in"][0]
    gw = I["gdn_conv_w"][0]
    P = np.concatenate([
        cols(I["norm_g"][0]), cols(I["mem_norm_g"][0]),
        gw.reshape(4, 12, 128).transpose(2, 1, 0).reshape(128, 48), cols(I["gdn_norm_g"][0]),
        I["cfm_dw_w"][0].reshape(31, 4, 128).transpose(2, 1, 0).reshape(128, 124),
        cols(I["cfm_dw_b"][0]), cols(I["cfm_ln_g"][0]), cols(I["cfm_ln_b"][0]),
        I["ffn_conv_w"][0].reshape(3, 44, 128).transpose(2, 1, 0).reshape(128, 132), cols(I["ffn_conv_b"][0]),
        cols(I["ret_norm_pre_2"][0]), cols(I["ret_norm_post_2"][0]), cols(I["kv_norm_2"]),
        cols(I["sb_norm_pre_2"][0]), cols(I["sb_norm_post_2"][0]),
        np.broadcast_to(I["gdn_a_log"][0][None, :], (128, 4)), np.broadcast_to(I["gdn_dt_bias"][0][None, :], (128, 4)),
    ], axis=1)
    dn = I["ffn_w_down"][0]
    dn2 = fm(dn[2048:], 6)
    wdn = np.concatenate([fm(dn[:2048]), np.pad(dn2, ((0, 0), (0, 0), (0, 256)))])
    rin = I["ret_w_in_2"][0]
    rqk = np.concatenate([rin[:, j * 1024 + h * 256:j * 1024 + h * 256 + 256] for h in range(4) for j in range(2)],
                         axis=1)
    kv = I["w_kv_2"]
    sin_ = I["sb_w_in_2"][0]
    so = I["sb_w_out_2"][0]
    sout = so.reshape(4, 4, 128, 4, 256).transpose(0, 3, 2, 1, 4).reshape(16, 128, 1024)
    arrays = {
        "xT": I["x"][0].T, "memT": I["mem"][0].T, "prm": P,
        "wab": w_in[:, 2048:2056].reshape(8, 128, 8).transpose(1, 0, 2).reshape(128, 64),
        "wcfm": fm(w_in[:, 2056:3080]), "wqkv": fm(w_in[:, 0:1536]), "wgate": fm(w_in[:, 1536:2048]),
        "wmk": fm(I["xa_w_kv"][0][:, :1024]), "wmv": tm(I["xa_w_kv"][0][:, 1024:]),
        "wout": fm(I["w_out"][0]), "wxq": fm(I["xa_w_q"][0]), "wxo": fm(I["xa_w_o"][0]),
        "wup": fm(I["ffn_w_up"][0]), "wdn": wdn, "rqk": fm(rqk), "rv": tm(rin[:, 2048:4096]),
        "rg": tm(rin[:, 4096:]), "rout": fm(I["ret_w_out_2"][0]), "sk": fm(kv[:, :1024]), "sv": tm(kv[:, 1024:]),
        "sq": fm(sin_[:, :1024]), "sg": fm(sin_[:, 1024:]), "sout": sout,
    }
    arrays.update(constants())
    nc = _bacc.Bacc("TRN2", target_bir_lowering=False, num_devices=1)
    arrs, A = {}, {}
    for n, a in arrays.items():
        a = np.ascontiguousarray(a)
        arrs["in_" + n] = a
        A[n] = nc.dram_tensor("in_" + n, a.shape, mybir.dt.from_np(a.dtype), kind="ExternalInput").ap()
    out = nc.dram_tensor("out_0", (1024, T), F32, kind="ExternalOutput").ap()
    program(nc, A, out)
    r = _run(nc, [arrs], core_ids=[0])
    return np.ascontiguousarray(r.results[0]["out_0"].T)[None]
```
